# Optimizing a Trainium2 kernel written in Bass

```python
import math
import jax, jax.numpy as jnp
from jax import lax
import numpy as np

D_MODEL = 1024
BATCH = 1
SEQ = 256
DEPTH = 2

N_A = DEPTH // 2
N_B = DEPTH - N_A
CONV_W = 3
HEAD_DIM = 64
N_HEADS = D_MODEL // HEAD_DIM
N_KV_HEADS = 4
GROUP = N_HEADS // N_KV_HEADS
WINDOW = 128
BLOCK = 128
ROT_DIM = HEAD_DIM // 4
ROPE_THETA = 500000.0
D_FF = ((8 * D_MODEL // 3 + 255) // 256) * 256
EPS = 1e-6
NEG = -1e30


def rmsnorm(x, g):
    xf = x.astype(jnp.float32)
    r = lax.rsqrt(jnp.mean(xf * xf, axis=-1, keepdims=True) + EPS)
    return (xf * r).astype(x.dtype) * g

def rope_tables(seq_len, dtype):
    inv_freq = ROPE_THETA ** (-jnp.arange(0, ROT_DIM, 2, dtype=jnp.float32) / ROT_DIM)
    ang = jnp.arange(seq_len, dtype=jnp.float32)[:, None] * inv_freq[None, :]
    return jnp.cos(ang)[:, None, :].astype(dtype), jnp.sin(ang)[:, None, :].astype(dtype)

def partial_rotary(t, cos, sin):
    half = ROT_DIM // 2
    t1, t2, rest = t[..., :half], t[..., half:ROT_DIM], t[..., ROT_DIM:]
    return jnp.concatenate([t1 * cos - t2 * sin, t2 * cos + t1 * sin, rest], axis=-1)

def causal_depthwise_conv3(u, w):
    s = u.shape[1]
    up = jnp.pad(u, ((0, 0), (CONV_W - 1, 0), (0, 0)))
    return up[:, 0:s] * w[0] + up[:, 1:s + 1] * w[1] + up[:, 2:s + 2] * w[2]

def short_conv_mixer(h, w_in, conv_w, w_out):
    bcx = h @ w_in
    b_gate, c_gate, u = jnp.split(bcx, 3, axis=-1)
    y = b_gate * causal_depthwise_conv3(c_gate * u, conv_w)
    return y @ w_out

def swiglu(h, w_gate_up, w_down):
    g, u = jnp.split(h @ w_gate_up, 2, axis=-1)
    return (jax.nn.silu(g) * u) @ w_down

def sliding_window_sink_attention(q, k, v, sinks):
    bsz, s = q.shape[0], q.shape[1]
    nb = s // BLOCK
    qb = q.reshape(bsz, nb, BLOCK, N_KV_HEADS, GROUP, HEAD_DIM)

    def with_prev(t):
        tb = t.reshape(bsz, nb, BLOCK, N_KV_HEADS, HEAD_DIM)
        prev = jnp.concatenate([jnp.zeros_like(tb[:, :1]), tb[:, :-1]], axis=1)
        return jnp.concatenate([prev, tb], axis=2)

    kk, vv = with_prev(k), with_prev(v)
    scale = 1.0 / math.sqrt(HEAD_DIM)
    scores = jnp.einsum('bnqhgd,bnkhd->bnhgqk', qb, kk).astype(jnp.float32) * scale

    qi = jnp.arange(BLOCK)[:, None]
    kj = jnp.arange(2 * BLOCK)[None, :]
    diff = BLOCK + qi - kj
    band = (diff >= 0) & (diff < WINDOW)
    not_pad = (jnp.arange(nb)[:, None, None] > 0) | (kj[None] >= BLOCK)
    valid = band[None] & not_pad
    scores = jnp.where(valid[None, :, None, None], scores, NEG)

    sink = jnp.broadcast_to(
        sinks.astype(jnp.float32).reshape(N_KV_HEADS, GROUP)[None, None, :, :, None, None],
        scores.shape[:-1] + (1,))
    probs = jax.nn.softmax(jnp.concatenate([scores, sink], axis=-1), axis=-1)[..., :-1]
    out = jnp.einsum('bnhgqk,bnkhd->bnqhgd', probs.astype(v.dtype), vv)
    return out.reshape(bsz, s, N_HEADS * HEAD_DIM)

def first_inputs(seed: int = 0) -> dict:
    key = jax.random.key(seed)
    ks = jax.random.split(key, 24)
    f32 = jnp.float32
    D, F = D_MODEL, D_FF
    QD = N_HEADS * HEAD_DIM
    KVD = N_KV_HEADS * HEAD_DIM

    def nrm(k, shape, fan_in):
        return jax.random.normal(k, shape, f32) * (fan_in ** -0.5)

    def gain(k, shape):
        return 1.0 + 0.05 * jax.random.normal(k, shape, f32)

    return {
        "x": jax.random.normal(ks[0], (BATCH, SEQ, D), f32),
        "a_pre_norm": gain(ks[1], (N_A, D)),
        "a_w_in": nrm(ks[2], (N_A, D, 3 * D), D),
        "a_conv_w": nrm(ks[3], (N_A, CONV_W, D), CONV_W),
        "a_w_out": nrm(ks[4], (N_A, D, D), D),
        "a_post_norm": gain(ks[5], (N_A, D)),
        "ffn_pre_norm": gain(ks[6], (DEPTH, D)),
        "ffn_w_gate_up": nrm(ks[7], (DEPTH, D, 2 * F), D),
        "ffn_w_down": nrm(ks[8], (DEPTH, F, D), F),
        "ffn_post_norm": gain(ks[9], (DEPTH, D)),
        "kv_norm": gain(ks[10], (D,)),
        "w_kv": nrm(ks[11], (D, 2 * KVD), D),
        "b_pre_norm": gain(ks[12], (N_B, D)),
        "b_w_q": nrm(ks[13], (N_B, D, QD), D),
        "b_sinks": 0.5 * jax.random.normal(ks[14], (N_B, N_HEADS), f32),
        "b_w_o": nrm(ks[15], (N_B, QD, D), QD),
        "b_post_norm": gain(ks[16], (N_B, D)),
    }

def first_block(x, a_pre_norm, a_w_in, a_conv_w, a_w_out, a_post_norm,
              ffn_pre_norm, ffn_w_gate_up, ffn_w_down, ffn_post_norm,
              kv_norm, w_kv,
              b_pre_norm, b_w_q, b_sinks, b_w_o, b_post_norm):
    bsz, s, _ = x.shape
    cos, sin = rope_tables(s, x.dtype)
    h = x
    for l in range(DEPTH):
        if l < N_A:
            mix = short_conv_mixer(rmsnorm(h, a_pre_norm[l]), a_w_in[l], a_conv_w[l], a_w_out[l])
            h = h + rmsnorm(mix, a_post_norm[l])
        else:
            j = l - N_A
            if j == 0:
                kv = rmsnorm(h, kv_norm) @ w_kv
                k_sh, v_sh = jnp.split(kv, 2, axis=-1)
                k_sh = partial_rotary(k_sh.reshape(bsz, s, N_KV_HEADS, HEAD_DIM), cos, sin)
                v_sh = v_sh.reshape(bsz, s, N_KV_HEADS, HEAD_DIM)
            q = (rmsnorm(h, b_pre_norm[j]) @ b_w_q[j]).reshape(bsz, s, N_HEADS, HEAD_DIM)
            q = partial_rotary(q, cos, sin)
            attn = sliding_window_sink_attention(q, k_sh, v_sh, b_sinks[j]) @ b_w_o[j]
            h = h + rmsnorm(attn, b_post_norm[j])
        ff = swiglu(rmsnorm(h, ffn_pre_norm[l]), ffn_w_gate_up[l], ffn_w_down[l])
        h = h + rmsnorm(ff, ffn_post_norm[l])
    return h


DEPTH_2 = 1

MLA_HEADS = 8
Q_LORA_RANK = 256
KV_LORA_RANK = 128
QK_NOPE_DIM = 64
QK_ROPE_DIM = 32
V_HEAD_DIM = 64
MLA_SCALE = (QK_NOPE_DIM + QK_ROPE_DIM) ** -0.5
Q_BLOCK = 128

RET_HEADS = 8
RET_HEAD_DIM = 64
RET_CHUNK = 128

D_MIX = MLA_HEADS * V_HEAD_DIM + RET_HEADS * RET_HEAD_DIM
D_FF_2 = 2816
ROPE_THETA_2 = 10000.0

IN_SIZES = (Q_LORA_RANK, KV_LORA_RANK, QK_ROPE_DIM,
            RET_HEADS * RET_HEAD_DIM, RET_HEADS * RET_HEAD_DIM,
            RET_HEADS * RET_HEAD_DIM, RET_HEADS * RET_HEAD_DIM)
D_IN = sum(IN_SIZES)
SPLIT_POINTS = tuple(int(s) for s in np.cumsum(IN_SIZES)[:-1])


def rms_norm(x, g):
    xf = x.astype(jnp.float32)
    y = xf * lax.rsqrt(jnp.mean(xf * xf, axis=-1, keepdims=True) + EPS)
    return (y * g.astype(jnp.float32)).astype(x.dtype)

def swiglu_2(x, w_gate, w_up, w_down):
    return (jax.nn.silu(x @ w_gate) * (x @ w_up)) @ w_down

def rope(x, pos_f):
    half = x.shape[-1] // 2
    inv = ROPE_THETA_2 ** (-jnp.arange(half, dtype=jnp.float32) / half)
    ang = pos_f[..., None] * inv
    cos = jnp.cos(ang)[:, :, None, :]
    sin = jnp.sin(ang)[:, :, None, :]
    x1 = x[..., :half].astype(jnp.float32)
    x2 = x[..., half:].astype(jnp.float32)
    return jnp.concatenate([x1 * cos - x2 * sin, x1 * sin + x2 * cos], axis=-1).astype(x.dtype)

def mla_group(c_q, c_kv, k_pe_raw, pos_f, q_norm, w_uq, kv_norm, w_ukv):
    B, S, _ = c_q.shape
    H = MLA_HEADS
    q = (rms_norm(c_q, q_norm) @ w_uq).reshape(B, S, H, QK_NOPE_DIM + QK_ROPE_DIM)
    q_nope = q[..., :QK_NOPE_DIM]
    q_pe = rope(q[..., QK_NOPE_DIM:], pos_f)
    kv = (rms_norm(c_kv, kv_norm) @ w_ukv).reshape(B, S, H, QK_NOPE_DIM + V_HEAD_DIM)
    k_nope = kv[..., :QK_NOPE_DIM]
    v = kv[..., QK_NOPE_DIM:]
    k_pe = rope(k_pe_raw[:, :, None, :], pos_f)[:, :, 0]
    nb = S // Q_BLOCK

    def block(args):
        qn, qp = args
        s = (jnp.einsum('bqhd,bkhd->bhqk', qn, k_nope).astype(jnp.float32)
             + jnp.einsum('bqhr,bkr->bhqk', qp, k_pe).astype(jnp.float32))
        p = jax.nn.softmax(s * MLA_SCALE, axis=-1)
        return jnp.einsum('bhqk,bkhd->bqhd', p.astype(v.dtype), v)

    qn_b = q_nope.reshape(B, nb, Q_BLOCK, H, QK_NOPE_DIM).swapaxes(0, 1)
    qp_b = q_pe.reshape(B, nb, Q_BLOCK, H, QK_ROPE_DIM).swapaxes(0, 1)
    out = lax.map(block, (qn_b, qp_b))
    return out.swapaxes(0, 1).reshape(B, S, H * V_HEAD_DIM)

def retention_scan(q, k, v, log_gamma, inclusive):
    B, S, H, d = q.shape
    C = RET_CHUNK
    nc = S // C
    idx = jnp.arange(C, dtype=jnp.float32)
    rel = idx[:, None] - idx[None, :]
    mask = (rel >= 0) if inclusive else (rel > 0)
    d_inner = jnp.where(mask[None], jnp.exp(log_gamma[:, None, None] * jnp.maximum(rel, 0.0)[None]), 0.0)
    q_dec = jnp.exp(log_gamma[None, :] * (idx[:, None] + 1.0))
    k_dec = jnp.exp(log_gamma[None, :] * (C - 1.0 - idx)[:, None])
    c_dec = jnp.exp(log_gamma * C)

    def to_chunks(t):
        return t.reshape(B, nc, C, H, d).swapaxes(0, 1)

    def step(state, inp):
        qc, kc, vc = inp
        s = jnp.einsum('bihd,bjhd->bhij', qc, kc) * d_inner
        inner = jnp.einsum('bhij,bjhe->bihe', s, vc)
        cross = jnp.einsum('bihd,bhde->bihe', qc * q_dec[None, :, :, None], state)
        state = (state * c_dec[None, :, None, None]
                 + jnp.einsum('bjhd,bjhe->bhde', kc * k_dec[None, :, :, None], vc))
        return state, inner + cross

    state0 = jnp.zeros((B, H, d, d), jnp.float32)
    _, out = lax.scan(step, state0, (to_chunks(q), to_chunks(k), to_chunks(v)))
    return out.swapaxes(0, 1).reshape(B, S, H, d)

def retention_group(r_q, r_k, r_v, r_g, pos_f, decay_fwd, decay_bwd):
    B, S, _ = r_q.shape
    shp = (B, S, RET_HEADS, RET_HEAD_DIM)
    q = rope(r_q.reshape(shp), pos_f).astype(jnp.float32)
    k = rope(r_k.reshape(shp), pos_f).astype(jnp.float32) * (RET_HEAD_DIM ** -0.5)
    v = r_v.reshape(shp).astype(jnp.float32)
    lg_f = jax.nn.log_sigmoid(decay_fwd.astype(jnp.float32))
    lg_b = jax.nn.log_sigmoid(decay_bwd.astype(jnp.float32))
    fwd = retention_scan(q, k, v, lg_f, True)
    bwd = jnp.flip(retention_scan(jnp.flip(q, 1), jnp.flip(k, 1), jnp.flip(v, 1), lg_b, False), 1)
    o = fwd + bwd
    mu = jnp.mean(o, axis=-1, keepdims=True)
    var = jnp.mean(jnp.square(o - mu), axis=-1, keepdims=True)
    o = ((o - mu) * lax.rsqrt(var + EPS)).reshape(B, S, RET_HEADS * RET_HEAD_DIM)
    return (jax.nn.silu(r_g.astype(jnp.float32)) * o).astype(r_q.dtype)

def second_inputs(seed: int = 0) -> dict:
    key = jax.random.key(seed)
    ks = jax.random.split(key, 24)
    f32 = jnp.float32

    def w(k, shape, fan_in):
        return jax.random.normal(k, shape, f32) * (fan_in ** -0.5)

    def gain(k, shape):
        return 1.0 + 0.02 * jax.random.normal(k, shape, f32)

    L = DEPTH_2
    offset = jax.random.randint(ks[1], (BATCH, 1), 0, 4096, dtype=jnp.int32)
    positions = offset + jnp.arange(SEQ, dtype=jnp.int32)[None, :]
    decay_init = jnp.asarray(np.log(2.0 ** (5.0 + np.arange(RET_HEADS)) - 1.0), f32)
    return {
        "x": jax.random.normal(ks[0], (BATCH, SEQ, D_MODEL), f32),
        "positions": positions,
        "ffn1_norm": gain(ks[2], (L, D_MODEL)),
        "ffn1_w_gate": w(ks[3], (L, D_MODEL, D_FF_2), D_MODEL),
        "ffn1_w_up": w(ks[4], (L, D_MODEL, D_FF_2), D_MODEL),
        "ffn1_w_down": w(ks[5], (L, D_FF_2, D_MODEL), D_FF_2),
        "mix_norm": gain(ks[6], (L, D_MODEL)),
        "w_in": w(ks[7], (L, D_MODEL, D_IN), D_MODEL),
        "q_norm": gain(ks[8], (L, Q_LORA_RANK)),
        "w_uq": w(ks[9], (L, Q_LORA_RANK, MLA_HEADS * (QK_NOPE_DIM + QK_ROPE_DIM)), Q_LORA_RANK),
        "kv_norm": gain(ks[10], (L, KV_LORA_RANK)),
        "w_ukv": w(ks[11], (L, KV_LORA_RANK, MLA_HEADS * (QK_NOPE_DIM + V_HEAD_DIM)), KV_LORA_RANK),
        "ret_decay_fwd": decay_init[None, :] + 0.05 * jax.random.normal(ks[12], (L, RET_HEADS), f32),
        "ret_decay_bwd": decay_init[None, :] + 0.05 * jax.random.normal(ks[13], (L, RET_HEADS), f32),
        "w_o": w(ks[14], (L, D_MIX, D_MODEL), D_MIX),
        "ffn2_norm": gain(ks[15], (L, D_MODEL)),
        "ffn2_w_gate": w(ks[16], (L, D_MODEL, D_FF_2), D_MODEL),
        "ffn2_w_up": w(ks[17], (L, D_MODEL, D_FF_2), D_MODEL),
        "ffn2_w_down": w(ks[18], (L, D_FF_2, D_MODEL), D_FF_2),
        "final_norm": gain(ks[19], (D_MODEL,)),
    }

def second_block(x, positions, ffn1_norm, ffn1_w_gate, ffn1_w_up, ffn1_w_down, mix_norm, w_in,
              q_norm, w_uq, kv_norm, w_ukv, ret_decay_fwd, ret_decay_bwd, w_o,
              ffn2_norm, ffn2_w_gate, ffn2_w_up, ffn2_w_down, final_norm):
    pos_f = positions.astype(jnp.float32)
    h = x
    for l in range(DEPTH_2):
        h = h + 0.5 * swiglu_2(rms_norm(h, ffn1_norm[l]), ffn1_w_gate[l], ffn1_w_up[l], ffn1_w_down[l])
        n = rms_norm(h, mix_norm[l])
        proj = n @ w_in[l]
        c_q, c_kv, k_pe, r_q, r_k, r_v, r_g = jnp.split(proj, SPLIT_POINTS, axis=-1)
        a = mla_group(c_q, c_kv, k_pe, pos_f, q_norm[l], w_uq[l], kv_norm[l], w_ukv[l])
        r = retention_group(r_q, r_k, r_v, r_g, pos_f, ret_decay_fwd[l], ret_decay_bwd[l])
        h = h + jnp.concatenate([a, r], axis=-1) @ w_o[l]
        h = h + 0.5 * swiglu_2(rms_norm(h, ffn2_norm[l]), ffn2_w_gate[l], ffn2_w_up[l], ffn2_w_down[l])
    return rms_norm(h, final_norm)


def setup_inputs(seed=0):
    out = dict(first_inputs(seed))
    for name, value in second_inputs(seed + 1).items():
        if name != "x":
            out[name + "_2"] = value
    return out


def reference(
    x, a_pre_norm, a_w_in, a_conv_w, a_w_out, a_post_norm, ffn_pre_norm, ffn_w_gate_up,
    ffn_w_down, ffn_post_norm, kv_norm, w_kv, b_pre_norm, b_w_q, b_sinks, b_w_o, b_post_norm,
    positions_2, ffn1_norm_2, ffn1_w_gate_2, ffn1_w_up_2, ffn1_w_down_2, mix_norm_2, w_in_2,
    q_norm_2, w_uq_2, kv_norm_2, w_ukv_2, ret_decay_fwd_2, ret_decay_bwd_2, w_o_2, ffn2_norm_2,
    ffn2_w_gate_2, ffn2_w_up_2, ffn2_w_down_2, final_norm_2,
):
    x = first_block(
        x, a_pre_norm, a_w_in, a_conv_w, a_w_out, a_post_norm, ffn_pre_norm, ffn_w_gate_up,
        ffn_w_down, ffn_post_norm, kv_norm, w_kv, b_pre_norm, b_w_q, b_sinks, b_w_o,
        b_post_norm,
    )
    return second_block(
        x, positions_2, ffn1_norm_2, ffn1_w_gate_2, ffn1_w_up_2, ffn1_w_down_2, mix_norm_2,
        w_in_2, q_norm_2, w_uq_2, kv_norm_2, w_ukv_2, ret_decay_fwd_2, ret_decay_bwd_2, w_o_2,
        ffn2_norm_2, ffn2_w_gate_2, ffn2_w_up_2, ffn2_w_down_2, final_norm_2,
    )


_drawn_inputs = setup_inputs


def setup_inputs(seed=0):
    import zlib

    import numpy as np

    out = dict(_drawn_inputs(seed))
    spreads = {}
    factors = {'b_sinks': 4.022,
     'ffn1_norm_2': 8.0,
     'mix_norm_2': 7.213,
     'q_norm_2': 8.0,
     'kv_norm_2': 8.0,
     'ffn2_norm_2': 23.341}
    for name, (base, spread) in spreads.items():
        noise = np.random.default_rng([zlib.crc32(name.encode()), seed]).standard_normal(out[name].shape)
        drawn = base * np.exp(spread * noise) if base else spread * noise
        out[name] = __import__('jax').numpy.asarray(drawn.astype(out[name].dtype))
    for name, factor in factors.items():
        out[name] = (out[name] * factor).astype(out[name].dtype)
    return out
```

```python
import math
from contextlib import ExitStack

import numpy as np

import concourse.bass as bass
from concourse import mybir

F32 = mybir.dt.float32
F32R = mybir.dt.float32r
BF16 = mybir.dt.bfloat16
I32 = mybir.dt.int32
ALU = mybir.AluOpType
ACT = mybir.ActivationFunctionType
AX = mybir.AxisListType

P = 128
D = 1024
KT = D // P
SEQ = 256
EPS = 1e-6
NEG = -1e30

HEADS, KV_HEADS, HD = 16, 4, 64
PAIRS = HEADS // 2
ROT_HALF = 8
MLA_HEADS, NOPE, PE_DIM, QK = 8, 64, 32, 96
Q_RANK, KV_RANK = 256, 128
LATENT = Q_RANK + KV_RANK + PE_DIM
RET_HEADS, RHALF = 8, 32
MLA_SCALE = QK ** -0.5

CHUNK = 1024
RING = 12
RAW = 4


class Phase:

    def __init__(self, mixer, index, first_chunk, first_block):
        self.mixer, self.index = mixer, index
        self.nb, self.cols, self.kd = (8, 384, 1) if mixer else (11, 512, 2)
        self.cg = KT * self.cols // CHUNK
        self.first_chunk, self.first_block = first_chunk, first_block
        self.chunks = self.nb * (self.cg + self.kd)

    def g_chunk(self, b):
        return self.first_chunk + b * self.cg + max(b - 1, 0) * self.kd

    def d_chunk(self, b):
        return self.first_chunk + min(b + 2, self.nb) * self.cg + b * self.kd


MIX = Phase(True, 0, 0, 0)
FFN1 = Phase(False, 1, MIX.chunks, MIX.nb)
B_FIRST = FFN1.first_chunk + FFN1.chunks
B_WO = B_FIRST + 12
FFN2 = Phase(False, 3, B_WO + 8, FFN1.first_block + FFN1.nb)
FFN3 = Phase(False, 4, FFN2.first_chunk + FFN2.chunks, FFN2.first_block + FFN2.nb)
C_FIRST = FFN3.first_chunk + FFN3.chunks
C_U = C_FIRST + 4
C_X = [C_FIRST] + [C_U + 3 + 4 * i for i in range(4)]
C_WO = C_X[4] + 4
FFN4 = Phase(False, 6, C_WO + 8, FFN3.first_block + FFN3.nb)
N_CHUNKS = FFN4.first_chunk + FFN4.chunks
B_INDEX, C_INDEX, LAST = 2, 5, 7
POST_NORMS = 4

GAIN = {0: 0, 1: 8, 2: 16, "q": 24, 3: 32, 4: 40, 5: 48, 6: 56}
GAIN_LAT = 64
CONV = 67
FEATS = CONV + 24
C_ID, C_ROPE, C_MASK, C_INV, C_REL = 0, 128, 160, 416, 448
CONSTS = C_REL + 4 * P
T_SINK, T_DECAY, TAB = 0, 16, 32


def head_at(i, p):
    return (2 * (i // 4) + p) * 4 + i % 4



def walk_block_step(ph, s, shift, step):
    step("G", 0, s, shift)
    if s == 0:
        step("prep", 1, ph.index)
    if s >= 1:
        step("D", 0, s - 1, shift)
    step("T", 0, s, shift)
    if s >= 1:
        step("G", 1, s - 1, shift)
        if s >= 2:
            step("D", 1, s - 2, shift)
        step("T", 1, s - 1, shift)


def walk_phase(eng, ph, step, trips):
    per = RING // (ph.cg + ph.kd)
    start = 3 if trips else ph.nb
    for s in range(start):
        walk_block_step(ph, s, 0, step)
    if trips:
        with eng.Fori(0, trips) as turn:
            for s in range(start, start + per):
                walk_block_step(ph, s, turn, step)
        for s in range(start + per * trips, ph.nb):
            walk_block_step(ph, s, 0, step)
    last = ph.nb - 1
    step("D", 0, last, 0)
    step("tail", 0, ph.index)
    step("G", 1, last, 0)
    step("D", 1, last - 1, 0)
    step("T", 1, last, 0)
    step("prep", 0, ph.index + 1)
    step("D", 1, last, 0)
    step("tail", 1, ph.index)


def walk_attention(step):
    def project(j, t):
        for c in range(4):
            step("proj", j, t, c)

    def heads(t, beside):
        step("S", t, 0)
        step("E", t, 0)
        step("S", t, 1)
        for u in range(8):
            if u < 7:
                step("E", t, u + 1)
            step("PT", t, u)
            beside(u)
            if u < 6:
                step("S", t, u + 2)
            step("PV", t, u)
            if u % 4 == 3:
                step("AO", t, u // 4)

    project(0, 0)
    step("prep", 1, B_INDEX)
    project(1, 0)
    project(2, 0)
    step("rope", 0)
    project(0, 1)
    step("QKT", 0)
    heads(0, lambda u: step("proj", 1 + u // 4, 1, u % 4))
    step("rope", 1)
    step("AT", 0)
    step("QKT", 1)
    heads(1, lambda u: step("O", 0, u))
    step("tail", 0, B_INDEX)
    step("AT", 1)
    for kt in range(5):
        step("O", 1, kt)
    step("prep", 0, B_INDEX + 1)
    for kt in range(5, 8):
        step("O", 1, kt)
    step("tail", 1, B_INDEX)


def walk_latent(step):
    def project(i, t):
        for c in range(4):
            step("X", i, t, c)

    project(0, 0)
    step("prep", 1, C_INDEX)
    project(1, 0)
    project(0, 1)
    step("LAT", 0)
    step("U", 0)
    project(2, 0)
    step("MT", 0)
    step("LAT", 1)
    step("U", 1)
    project(1, 1)
    step("MT", 1)
    beside = [(2, 1), (3, 0), (3, 1), (4, 0)]
    step("MS", 0)
    step("ME", 0)
    step("MS", 1)
    for v in range(8):
        if v < 7:
            step("ME", v + 1)
        step("MPT", v)
        i, t = beside[v // 2]
        step("X", i, t, 2 * (v % 2))
        if v < 6:
            step("MS", v + 2)
        step("MPV", v)
        step("X", i, t, 2 * (v % 2) + 1)
        if v % 4 == 3:
            step("MN", v // 4)
        if v >= 4:
            step("RROPE", (v - 4) // 2, v % 2)
    for t in range(2):
        step("RT", t)
    step("decay", 0)
    step("RS", 0)
    for hd in range(8):
        if hd < 7:
            step("decay", hd + 1)
            step("RS", hd + 1)
        step("RM", hd)
        if hd < 4:
            step("X", 4, 1, hd)
        step("RPV", hd)
    for t in range(2):
        step("gate", t)
    for t in range(2):
        step("MAT", t)
    step("GN", 0)
    for kt in range(4):
        step("Oc", 0, kt)
    step("RAT", 0)
    step("GN", 1)
    for kt in range(4, 8):
        step("Oc", 0, kt)
    step("tail", 0, C_INDEX)
    for kt in range(4):
        step("Oc", 1, kt)
    step("RAT", 1)
    step("prep", 0, C_INDEX + 1)
    for kt in range(4, 8):
        step("Oc", 1, kt)
    step("tail", 1, C_INDEX)


def walk(eng, step):
    step("start",)
    step("prep", 0, 0)
    step("fill", 0, RING)
    walk_phase(eng, MIX, lambda *a: step(*a, ph=MIX), 0)
    walk_phase(eng, FFN1, lambda *a: step(*a, ph=FFN1), 4)
    walk_attention(lambda *a: step(*a, ph=None))
    walk_phase(eng, FFN2, lambda *a: step(*a, ph=FFN2), 4)
    walk_phase(eng, FFN3, lambda *a: step(*a, ph=FFN3), 4)
    walk_latent(lambda *a: step(*a, ph=None))
    walk_phase(eng, FFN4, lambda *a: step(*a, ph=FFN4), 3)
    step("prep", 1, LAST)


def two_pi_parts():
    parts, rest = [], 2 * math.pi
    for _ in range(5):
        unit = 2.0 ** (math.floor(math.log2(rest)) - 6)
        parts.append(math.floor(rest / unit) * unit)
        rest -= parts[-1]
    return parts


def build(nc, x_in, stream, feats_in, consts_in, table_in, pos_in, posts_in, out):
    with ExitStack() as ctx:
        def sem(name):
            return ctx.enter_context(nc.semaphore(name))

        def rows2(name):
            return [sem(f"{name}{t}") for t in range(2)]

        at = [(nc.sbuf_base + 63) // 64 * 64]

        def place(name, shape, dt, offset=None):
            size = int(np.prod(shape[1:])) * (2 if dt == BF16 else 4)
            if offset is None:
                offset = at[0]
                at[0] += (size + 63) // 64 * 64
            assert offset + size <= nc.sbuf_usable_end, (name, offset + size)
            return nc.alloc_sbuf_tensor_at(name, shape, dt, offset=offset)

        raw = place("raw", [P, RAW * CHUNK], F32)
        w_high = place("w_high", [P, RING * CHUNK], F32R)
        w_low = place("w_low", [P, RING * CHUNK], F32R)
        xTh = [place(f"xTh{t}", [P, KT, P], F32R) for t in range(2)]
        xTl = [place(f"xTl{t}", [P, KT, P], F32R) for t in range(2)]
        h = [place(f"h{t}", [P, D], F32) for t in range(2)]
        post = place("post", [P, D], F32)
        junk = [place(f"junk{t}", [P, D], BF16) for t in range(2)]
        consts = place("consts", [P, CONSTS], F32)
        feats = place("feats", [P, FEATS], F32)
        table = place("table", [P, TAB], F32)
        stat = place("stat", [P, 64], F32)
        pos_i = place("pos_i", [P, 2], I32)
        trig = place("trig", [P, 8, 64], F32)
        decay_t = place("decay_t", [P, 8, 16], F32)
        mx = [place(f"mx{t}", [P, 16], F32) for t in range(2)]
        negm = [place(f"negm{t}", [P, 16], F32) for t in range(2)]
        lsum = [place(f"lsum{t}", [P, 16], F32) for t in range(2)]
        esink = [place(f"esink{t}", [P, 16], F32) for t in range(2)]
        lrec = [place(f"lrec{t}", [P, 16], F32) for t in range(2)]
        gn = [place(f"gn{t}", [P, 4, 8], F32) for t in range(2)]
        nsink = place("nsink", [P, 16], F32)
        actT_at = at[0]
        aTh = [place(f"aTh{t}", [P, 2, P], F32R) for t in range(2)]
        aTl = [place(f"aTl{t}", [P, 2, P], F32R) for t in range(2)]
        latTh = place("latTh", [P, 3, P], F32R, actT_at)
        latTl = place("latTl", [P, 3, P], F32R, actT_at + 3 * P * 4)
        union = at[0]

        hg = [place(f"hg{t}", [P, D], F32) for t in range(2)]
        gate = [place(f"gate{t}", [P, 256], F32) for t in range(2)]
        act = [place(f"act{t}", [P, 256], F32) for t in range(2)]
        cv = [place(f"cv{i}", [P, SEQ + 2], F32) for i in range(3)]
        yT = [place(f"yT{t}", [P, P], F32) for t in range(2)]

        at[0] = union
        qT = [place(f"qT{t}", [P, PAIRS, P], F32) for t in range(2)]
        qkv = [place(f"qkv{t}", [P, 1536], F32) for t in range(2)]
        kT = place("kT", [P, 2, SEQ], F32)
        x2h = [place(f"x2h{t}", [P, KT, P], F32R) for t in range(2)]
        x2l = [place(f"x2l{t}", [P, KT, P], F32R) for t in range(2)]
        sm = [place(f"sm{i}", [P, 2, SEQ], F32) for i in range(2)]
        pr = [place(f"pr{i}", [P, 2, SEQ], F32) for i in range(2)]
        prT_at = at[0]
        prT = [place(f"prT{i}", [P, 4 * P], F32) for i in range(2)]
        rtmp = [place(f"rtmp{i}", [P, 20, ROT_HALF], F32, prT_at + i * 20 * ROT_HALF * 4) for i in range(4)]

        at[0] = union
        mqT = place("mqT", [QK, MLA_HEADS, SEQ], F32)
        rqT = place("rqT", [P, 4, SEQ], F32, union)
        rkT = place("rkT", [P, 4, SEQ], F32, union + 4 * SEQ * 4)
        mkT = place("mkT", [QK, MLA_HEADS, SEQ], F32)
        lat_at = at[0]
        lat = [place(f"lat{t}", [P, LATENT], F32) for t in range(2)]
        ttmp = [place(f"ttmp{i}", [P, 8, RHALF], F32, lat_at + i * 1024 if i < 3 else None) for i in range(4)]
        mq_at = at[0]
        mq = place("mq", [P, MLA_HEADS, QK], F32)
        mk = place("mk", [P, MLA_HEADS, QK], F32)
        mo = [place(f"mo{t}", [P, 512], F32, mq_at + t * MLA_HEADS * QK * 4) for t in range(2)]
        mv = [place(f"mv{t}", [P, 512], F32) for t in range(2)]
        rqk = [place(f"rqk{t}", [P, 1024], F32) for t in range(2)]
        rv = [place(f"rv{t}", [P, 512], F32) for t in range(2)]
        p_at = at[0]
        mp = [place(f"mp{i}", [P, 2, SEQ], F32) for i in range(2)]
        sd = [place(f"sd{i}", [P, 2, SEQ], F32, p_at + i * 2 * SEQ * 4) for i in range(2)]
        latf = place("latf", [P, 3, P], F32, p_at)
        mpT = [place(f"mpT{i}", [P, 4 * P], F32) for i in range(2)]
        dm = [place(f"dm{i}", [P, 3 * P], F32, lat_at + i * 3 * P * 4) for i in range(2)]
        dtmp = place("dtmp", [P, P], F32)

        ident = consts[:, C_ID:C_ID + P]
        rope1 = consts[:, C_ROPE:C_ROPE + 32].rearrange("p (t c f) -> p t c f", t=2, c=2)
        mask = consts[:, C_MASK:C_MASK + SEQ]
        inv_freq = consts[:, C_INV:C_INV + 32]
        rel = consts[:, C_REL:C_REL + 4 * P]
        ss = [stat[:, t:t + 1] for t in range(2)]
        ms = [stat[:, 2 + t:3 + t] for t in range(2)]
        rr = [stat[:, 4 + t:5 + t] for t in range(2)]
        pss = [stat[:, 6 + t:7 + t] for t in range(2)]
        pms = [stat[:, 8 + t:9 + t] for t in range(2)]
        prr = [stat[:, 10 + t:11 + t] for t in range(2)]
        lss = [stat[:, 12 + 2 * t:14 + 2 * t] for t in range(2)]
        lms = [stat[:, 16 + 2 * t:18 + 2 * t] for t in range(2)]
        lrr = [stat[:, 20 + 2 * t:22 + 2 * t] for t in range(2)]
        half_neg = stat[:, 24:32]
        one_neg = stat[:, 32:48]
        pos_f = stat[:, 48:50]
        ang, kang, tang, cang, cosT, sinT = (trig[:, i, :] for i in range(6))
        cos2 = cosT.rearrange("p (t f) -> p t f", t=2)
        sin2 = sinT.rearrange("p (t f) -> p t f", t=2)
        lg_r2, lg_ax, lg_e, lg_s, lg_z, lg_p, lg = (decay_t[:, i, :] for i in range(7))

        pD = [ctx.enter_context(nc.psum_tensor(f"pD{t}", [P, D], F32)) for t in range(2)]
        pG = [ctx.enter_context(nc.psum_tensor(f"pG{t}", [P, 512], F32)) for t in range(2)]
        pT = [ctx.enter_context(nc.psum_tensor(f"pT{t}", [P, 512], F32)) for t in range(2)]

        w_loaded = [sem(f"w_loaded{i}") for i in range(RAW)]
        w_high_done = sem("w_high_done")
        w_split = sem("w_split")
        w_freed = sem("w_freed")
        x_loaded = rows2("x_loaded")
        feats_loaded, consts_loaded = sem("feats_loaded"), sem("consts_loaded")
        table_loaded, pos_loaded = sem("table_loaded"), sem("pos_loaded")
        post_loaded = sem("post_loaded")
        out_ready, out_stored = rows2("out_ready"), sem("out_stored")
        h_ready, ss_ready, r_ready = (rows2(n) for n in ("h_ready", "ss_ready", "r_ready"))
        pss_ready, pr_ready = (rows2(n) for n in ("pss_ready", "pr_ready"))
        hT_psum, hg_ready, xh_ready, xT_ready = (rows2(n) for n in ("hT_psum", "hg_ready", "xh_ready", "xT_ready"))
        g_done0, d_done0 = sem("g_done0"), sem("d_done0")
        gate_ready, act_ready, actT_psum = (rows2(n) for n in ("gate_ready", "act_ready", "actT_psum"))
        cuT_ready, conv_done, ah_ready, aT_ready = (rows2(n) for n in ("cuT_ready", "conv_done", "ah_ready", "aT_ready"))
        halo_zero = sem("halo_zero")
        q_done0 = sem("q_done0")
        qkv_ready, rope_done, qkT_psum = rows2("qkv_ready"), sem("rope_done"), rows2("qkT_psum")
        kqT_act, kqT_dve = rows2("kqT_act"), rows2("kqT_dve")
        s_done, sm_ready, p_ready = sem("s_done"), sem("sm_ready"), sem("p_ready")
        pT_psum, pT_ready, pv_done = sem("pT_psum"), sem("pT_ready"), sem("pv_done")
        es_arg, es_ready, ao_ready = (rows2(n) for n in ("es_arg", "es_ready", "ao_ready"))
        aoT_psum, aoh_ready, aoT_ready = (rows2(n) for n in ("aoT_psum", "aoh_ready", "aoT_ready"))
        nsink_ready = sem("nsink_ready")
        x_done0, u_done0 = sem("x_done0"), sem("u_done0")
        x_out, lat_ss, lr_ready = (rows2(n) for n in ("x_out", "lat_ss", "lr_ready"))
        latT_psum, latf_ready, lath_ready, latT_ready = (rows2(n) for n in ("latT_psum", "latf_ready", "lath_ready", "latT_ready"))
        u_out, mqk_ready, mT_psum = (rows2(n) for n in ("u_out", "mqk_ready", "mT_psum"))
        mqT_ready, mkT_ready = rows2("mqT_ready"), rows2("mkT_ready")
        ms_psum, mmax_ready, mp_ready = sem("ms_psum"), sem("mmax_ready"), sem("mp_ready")
        mpT_psum, mpT_ready, mpv_done = sem("mpT_psum"), sem("mpT_ready"), sem("mpv_done")
        mo_ready = rows2("mo_ready")
        rrope_done = rows2("rrope_done")
        rT_psum, rqT_ready, rkT_ready = rows2("rT_psum"), rows2("rqT_ready"), rows2("rkT_ready")
        dm_arg, dm_ready = sem("dm_arg"), sem("dm_ready")
        rs_psum, sd_ready, rpv_done = sem("rs_psum"), sem("sd_ready"), sem("rpv_done")
        rgate = rows2("rgate")
        gn_var, gn_r, ro_ready = (rows2(n) for n in ("gn_var", "gn_r", "ro_ready"))
        catT_psum, cath_ready, catT_ready = (rows2(n) for n in ("catT_psum", "cath_ready", "catT_ready"))
        trig_ready, sincos_ready = sem("trig_ready"), sem("sincos_ready")
        pool_chain, ve_chain = sem("pool_chain"), sem("ve_chain")
        ax_ready, e_ready, lg_ready = sem("ax_ready"), sem("e_ready"), sem("lg_ready")
        pows_ready = sem("pows_ready")

        def slot(c):
            return (c + 1) % RING * CHUNK

        def xT_base(p):
            return 2 * p + (2 if p > B_INDEX else 0)

        def freed_by(ph, b, out_part):
            return ph.d_chunk(b) + ph.kd if out_part else ph.g_chunk(b) + ph.cg

        def branch_done(eng, t, k):
            if t == 0:
                eng.wait_ge(d_done0, k + 1)
            else:
                eng.wait_ge(w_freed, [FFN1.first_chunk, B_FIRST, FFN2.first_chunk, FFN3.first_chunk,
                                      C_FIRST, FFN4.first_chunk, N_CHUNKS][k])

        def proj_done(eng, j, t):
            if t == 0:
                eng.wait_ge(q_done0, j + 1)
            else:
                eng.wait_ge(w_freed, B_FIRST + 4 * (j + 1))

        def x_product(eng, i, t):
            if t == 0:
                eng.wait_ge(x_done0, i + 1)
            else:
                eng.wait_ge(w_freed, C_X[i] + 4)

        block = ctx.enter_context(nc.Block())

        @block.sync
        def _(sp):
            for t in range(2):
                sp.dma_start(h[t][:], x_in[P * t:P * (t + 1), :]).then_inc(x_loaded[t], 16)
            sp.dma_start(consts[:], consts_in).then_inc(consts_loaded, 16)
            sp.dma_start(feats[:], feats_in).then_inc(feats_loaded, 16)
            for c in range(RAW):
                sp.dma_start(raw[:, c * CHUNK:(c + 1) * CHUNK], stream[c]).then_inc(w_loaded[c], 16)
            turns = N_CHUNKS // RAW
            with sp.Fori(1, turns) as turn:
                for i in range(RAW):
                    sp.wait_ge(w_split, turn * RAW + (i - RAW + 1))
                    sp.dma_start(raw[:, i * CHUNK:(i + 1) * CHUNK],
                                 stream[bass.ds(turn * RAW + i, 1)].rearrange("o p n -> p (o n)")
                                 ).then_inc(w_loaded[i], 16)
            for c in range(turns * RAW, N_CHUNKS):
                sp.wait_ge(w_split, c - RAW + 1)
                i = c % RAW
                sp.dma_start(raw[:, i * CHUNK:(i + 1) * CHUNK], stream[c]).then_inc(w_loaded[i], 16)
            for t in range(2):
                sp.wait_ge(out_ready[t], 1)
                sp.dma_start(out[P * t:P * (t + 1), :], hg[t][:]).then_inc(out_stored, 16)
            sp.wait_ge(out_stored, 32)

        @block.gpsimd
        def _(pool):
            links = [0]

            def link(ins):
                links[0] += 1
                ins.then_inc(pool_chain, 1)
                pool.wait_ge(pool_chain, links[0])

            def start(ph):
                pool.memset(half_neg, -0.5).then_inc(pows_ready, 1)
                pool.memset(one_neg, -1.0).then_inc(pows_ready, 1)
                pool.dma_start(table[:], table_in).then_inc(table_loaded, 16)
                pool.dma_start(pos_i[:], pos_in).then_inc(pos_loaded, 16)
                pool.dma_start(post[:], posts_in[0].partition_broadcast(P)).then_inc(post_loaded, 16)
                for i in range(3):
                    pool.memset(cv[i][:, 0:2], 0.0).then_inc(halo_zero, 1)
                pool.wait_ge(pows_ready, 2)

            def tables():
                pool.wait_ge(pos_loaded, 16)
                pool.wait_ge(consts_loaded, 16)
                link(pool.tensor_copy(pos_f, pos_i[:]))
                for t in range(2):
                    link(pool.tensor_scalar(ang[:, 32 * t:32 * t + 32], inv_freq, pos_f[:, t:t + 1], None, ALU.mult))
                magic = 1.5 * 2.0 ** 23
                for unit in (4096.0, 1.0):
                    link(pool.tensor_scalar(kang, ang, 1.0 / (unit * 2 * math.pi), magic, ALU.mult, ALU.add))
                    link(pool.tensor_scalar(kang, kang, magic, None, ALU.subtract))
                    for part in two_pi_parts():
                        link(pool.tensor_scalar(tang, kang, -part * unit, None, ALU.mult))
                        link(pool.tensor_tensor(ang, ang, tang, ALU.add))
                link(pool.tensor_scalar(cang, ang, math.pi / 2, None, ALU.add))
                link(pool.tensor_scalar(tang, cang, math.pi, -2 * math.pi, ALU.is_gt, ALU.mult))
                link(pool.tensor_tensor(cang, cang, tang, ALU.add))
                link(pool.tensor_scalar(cang, cang, 3.1415925, -3.1415925, ALU.min, ALU.max))
                pool.tensor_scalar(ang, ang, 3.1415925, -3.1415925, ALU.min, ALU.max).then_inc(trig_ready, 1)
                pool.wait_ge(table_loaded, 16)
                dec = table[:, T_DECAY:T_DECAY + 16]
                link(pool.tensor_scalar(lg_r2, dec, -1.0, 0.0, ALU.mult, ALU.max))
                link(pool.tensor_scalar(lg_ax, dec, 0.0, None, ALU.max))
                pool.tensor_tensor(lg_ax, lg_ax, lg_r2, ALU.add).then_inc(ax_ready, 1)

            def log_decays():
                pool.wait_ge(e_ready, 1)
                link(pool.tensor_scalar(lg_s, lg_e, 2.0, None, ALU.add))
                link(pool.tensor_tensor(lg_s, lg_s, one_neg, ALU.pow))
                link(pool.tensor_tensor(lg_s, lg_s, lg_e, ALU.mult))
                link(pool.tensor_tensor(lg_z, lg_s, lg_s, ALU.mult))
                link(pool.tensor_scalar(lg_p, lg_z, 1.0 / 17, 1.0 / 15, ALU.mult, ALU.add))
                for n in (13, 11, 9, 7, 5, 3, 1):
                    link(pool.tensor_tensor(lg_p, lg_p, lg_z, ALU.mult))
                    link(pool.tensor_scalar(lg_p, lg_p, 1.0 / n, None, ALU.add))
                link(pool.tensor_tensor(lg_p, lg_p, lg_s, ALU.mult))
                link(pool.tensor_scalar(lg_p, lg_p, 2.0, None, ALU.mult))
                link(pool.tensor_tensor(lg_p, lg_p, lg_r2, ALU.add))
                pool.tensor_scalar(lg, lg_p, -1.0, None, ALU.mult).then_inc(lg_ready, 1)

            def prep(t, p, ph):
                pool.wait_ge(ss_ready[t], p + 1)
                link(pool.tensor_scalar(ms[t], ss[t], 1.0 / D, EPS, ALU.mult, ALU.add))
                pool.tensor_tensor(rr[t], ms[t], half_neg[:, 0:1], ALU.pow).then_inc(r_ready[t], 1)
                if t == 1 and p == 0:
                    tables()
                if t == 1 and p == B_INDEX + 1:
                    log_decays()

            def tail(t, k, ph):
                if k < POST_NORMS:
                    pool.wait_ge(pss_ready[t], k + 1)
                    link(pool.tensor_scalar(pms[t], pss[t], 1.0 / D, EPS, ALU.mult, ALU.add))
                    pool.tensor_tensor(prr[t], pms[t], half_neg[:, 0:1], ALU.pow).then_inc(pr_ready[t], 1)
                    if t == 1:
                        pool.wait_ge(h_ready[0], k + 1)
                        pool.wait_ge(h_ready[1], k + 1)
                        pool.dma_start(post[:], posts_in[k + 1].partition_broadcast(P)).then_inc(post_loaded, 16)

            def LAT(t, ph):
                pool.wait_ge(lat_ss[t], 2)
                link(pool.tensor_scalar(lms[t][:, 0:1], lss[t][:, 0:1], 1.0 / Q_RANK, EPS, ALU.mult, ALU.add))
                link(pool.tensor_scalar(lms[t][:, 1:2], lss[t][:, 1:2], 1.0 / KV_RANK, EPS, ALU.mult, ALU.add))
                pool.tensor_tensor(lrr[t], lms[t], half_neg[:, 0:2], ALU.pow).then_inc(lr_ready[t], 1)

            def decay(hd, ph):
                d, f, b = dm[hd % 2], lg[:, hd:hd + 1], lg[:, 8 + hd:9 + hd]
                if hd == 0:
                    pool.wait_ge(lg_ready, 1)
                    pool.wait_ge(rrope_done[1], 2)
                if hd >= 2:
                    pool.wait_ge(sd_ready, 2 * (hd - 1))
                link(pool.tensor_scalar(d[:, P:3 * P], rel[:, 0:2 * P], f, None, ALU.mult))
                link(pool.tensor_scalar(d[:, 0:P], rel[:, 3 * P:4 * P], b, None, ALU.mult))
                link(pool.tensor_scalar(dtmp[:], rel[:, 2 * P:3 * P], b, None, ALU.mult))
                pool.tensor_tensor(d[:, P:2 * P], d[:, P:2 * P], dtmp[:], ALU.add).then_inc(dm_arg, 1)
                pool.wait_ge(dm_arg, hd + 1)

            def GN(t, ph):
                pool.wait_ge(gn_var[t], 1)
                link(pool.tensor_scalar(gn[t][:, 2, :], gn[t][:, 1, :], 1.0 / HD, EPS, ALU.mult, ALU.add))
                pool.tensor_tensor(gn[t][:, 3, :], gn[t][:, 2, :], half_neg, ALU.pow).then_inc(gn_r[t], 1)

            parts = {f.__name__: f for f in (start, prep, tail, LAT, decay, GN)}
            in_loop = ("G", "D", "T")

            def step(name, *args, ph=None):
                if name in parts:
                    parts[name](*args, ph)
            walk(NoLoop(), lambda name, *a, ph=None: None if name in in_loop else step(name, *a, ph=ph))

        @block.scalar
        def _(sc):
            def split_high(c, static, shift):
                sc.wait_ge(w_loaded[static % RAW], 16 * (static // RAW + 1) + shift * (16 * RING // RAW))
                if static >= RING:
                    sc.wait_ge(w_freed, c - RING + 1)
                sc.activation(w_high[:, slot(static):slot(static) + CHUNK],
                              raw[:, static % RAW * CHUNK:(static % RAW + 1) * CHUNK], ACT.Copy).then_inc(w_high_done, 1)

            def refill(first, n, shift=0):
                for c in range(first + RING, first + RING + n):
                    if c < N_CHUNKS:
                        split_high(c + shift * RING, c, shift)

            def start(ph):
                sc.preload_act_table(ACT.Silu)

            def fill(first, n, ph):
                for c in range(first, first + n):
                    split_high(c, c, 0)

            def prep(t, p, ph):
                if p == 0:
                    sc.wait_ge(x_loaded[t], 16)
                else:
                    sc.wait_ge(h_ready[t], p)
                sc.activation(junk[t][:], h[t][:], ACT.Square, accum_out=ss[t]).then_inc(ss_ready[t], 1)
                if p == LAST:
                    return
                sets = [(xTh, hg)] + ([(x2h, hg)] if p == B_INDEX else [])
                n = xT_base(p)
                for high, _ in sets:
                    for half in range(2):
                        n += 1
                        sc.wait_ge(hg_ready[t], n)
                        sc.activation(high[t][:, 4 * half:4 * half + 4, :].rearrange("p k r -> p (k r)"),
                                      hg[t][:, 512 * half:512 * half + 512], ACT.Copy).then_inc(xh_ready[t], 1)

            def tail(t, k, ph):
                if k < POST_NORMS:
                    branch_done(sc, t, k)
                    sc.activation(junk[t][:], pD[t][:], ACT.Square, accum_out=pss[t]).then_inc(pss_ready[t], 1)

            def G(t, b, shift, ph):
                n = ph.first_block + b + 1 + shift * (RING // (ph.cg + ph.kd))
                if t == 1:
                    refill(ph.g_chunk(b), ph.cg, shift)
                    sc.wait_ge(w_freed, freed_by(ph, b, False) + shift * RING)
                else:
                    sc.wait_ge(g_done0, n)
                if b == 0:
                    sc.wait_ge(r_ready[t], ph.index + 1)
                sc.activation(gate[t][:], pG[t][:, 0:256], ACT.Copy if ph.mixer else ACT.Silu,
                              scale=rr[t]).then_inc(gate_ready[t], 1)

            def Dn(t, b, shift, ph):
                if t == 1:
                    refill(ph.d_chunk(b), ph.kd, shift)

            def T(t, b, shift, ph):
                n = ph.first_block + b + 1 + shift * (RING // (ph.cg + ph.kd))
                sc.wait_ge(actT_psum[t], n)
                if ph.mixer:
                    if b < 3 and t == 0:
                        sc.wait_ge(halo_zero, b + 1)
                    if t == 0 and b >= 3:
                        sc.wait_ge(conv_done[1], 4 * (b - 2))
                    sc.activation(cv[b % 3][:, 2 + P * t:2 + P * (t + 1)], pT[t][:, P:2 * P], ACT.Copy).then_inc(cuT_ready[t], 1)
                    sc.wait_ge(conv_done[t], 4 * (b + 1))
                    sc.activation(aTh[t][:, 0, :], yT[t][:], ACT.Copy).then_inc(ah_ready[t], 1)
                else:
                    sc.activation(aTh[t][:].rearrange("p k r -> p (k r)"), pT[t][:, 0:256], ACT.Copy).then_inc(ah_ready[t], 1)
                if ph is FFN1 and t == 0 and b == 0:
                    sc.wait_ge(trig_ready, 1)
                    sc.activation(sinT, ang, ACT.Sin).then_inc(sincos_ready, 1)
                    sc.activation(cosT, cang, ACT.Sin).then_inc(sincos_ready, 1)

            def proj(j, t, c, ph):
                if t == 1:
                    refill(B_FIRST + 4 * j + c, 1)
                if c == 3:
                    proj_done(sc, j, t)
                    if j == 0:
                        sc.wait_ge(r_ready[t], B_INDEX + 1)
                    src = pG[t][:] if j == 2 else pD[t][:, 512 * j:512 * j + 512]
                    sc.activation(qkv[t][:, 512 * j:512 * j + 512], src, ACT.Copy, scale=rr[t]).then_inc(qkv_ready[t], 1)

            def QKT(t, ph):
                sc.wait_ge(qkT_psum[t], 1)
                sc.activation(kT[:, :, P * t:P * (t + 1)], pT[t][:, 0:256].rearrange("p (a r) -> p a r", a=2),
                              ACT.Copy).then_inc(kqT_act[t], 1)
                sc.wait_ge(qkT_psum[t], 2)
                sc.activation(qT[t][:, 0:4, :].rearrange("p a r -> p (a r)"), pG[t][:], ACT.Copy).then_inc(kqT_act[t], 1)

            def E(t, u, ph):
                v, m, half = 8 * t + u, u // 2, u % 2
                keys = slice(P * (1 - t), SEQ)
                sc.wait_ge(sm_ready, v + 1)
                if v >= 2:
                    sc.wait_ge(pT_psum, v - 1)
                for x in range(2):
                    col = 2 * (2 * m + x) + half
                    sc.activation(pr[v % 2][:, x, keys], sm[v % 2][:, x, keys], ACT.Exp, bias=negm[t][:, col:col + 1],
                                  accum_out=lsum[t][:, col:col + 1]).then_inc(p_ready, 1)

            def AO(t, half, ph):
                sc.wait_ge(es_arg[t], half + 1)
                cols = slice(8 * half, 8 * half + 8)
                sc.activation(esink[t][:, cols], esink[t][:, cols], ACT.Exp).then_inc(es_ready[t], 1)
                if t == 0 and half == 0:
                    sc.wait_ge(ax_ready, 1)
                    sc.activation(lg_e, lg_ax, ACT.Exp, scale=-1.0).then_inc(e_ready, 1)

            def AT(t, ph):
                for half in range(2):
                    sc.wait_ge(aoT_psum[t], half + 1)
                    sc.activation(xTh[t][:, 4 * half:4 * half + 4, :].rearrange("p k r -> p (k r)"),
                                  (pT, pG)[half][t][:], ACT.Copy).then_inc(aoh_ready[t], 1)

            def O(t, kt, ph):
                if t == 1:
                    refill(B_WO + kt, 1)

            def X(i, t, c, ph):
                if t == 1:
                    refill(C_X[i] + c, 1)
                if c == 3 and i < 4:
                    x_product(sc, i, t)
                    if i == 0:
                        sc.wait_ge(r_ready[t], C_INDEX + 1)
                    dst = [lat[t][:], rqk[t][:, 0:512], rqk[t][:, 512:1024], rv[t][:]][i]
                    sc.activation(dst, pD[t][:, 0:LATENT if i == 0 else 512], ACT.Copy, scale=rr[t]).then_inc(x_out[t], 1)

            def LAT(t, ph):
                sc.wait_ge(x_out[t], 1)
                sc.activation(junk[t][:, 0:Q_RANK], lat[t][:, 0:Q_RANK], ACT.Square, accum_out=lss[t][:, 0:1]).then_inc(lat_ss[t], 1)
                sc.activation(junk[t][:, Q_RANK:Q_RANK + KV_RANK], lat[t][:, Q_RANK:Q_RANK + KV_RANK], ACT.Square,
                              accum_out=lss[t][:, 1:2]).then_inc(lat_ss[t], 1)
                sc.wait_ge(latf_ready[t], 1)
                if t == 1:
                    sc.wait_ge(u_done0, 1)
                sc.activation(latTh[:], latf[:], ACT.Copy).then_inc(lath_ready[t], 1)

            def U(t, ph):
                if t == 1:
                    refill(C_U, 3)
                    sc.wait_ge(w_freed, C_U + 3)
                    sc.wait_ge(mT_psum[0], 2)
                else:
                    sc.wait_ge(u_done0, 1)
                sc.wait_ge(lr_ready[t], 1)
                for half in range(2):
                    sc.activation(mq[:, 4 * half:4 * half + 4, :], (pG, pT)[half][0][:, 0:384].rearrange("p (a f) -> p a f", a=4),
                                  ACT.Copy, scale=lrr[t][:, 0:1]).then_inc(u_out[t], 1)
                sc.activation(mk[:, :, 0:NOPE], pG[1][:].rearrange("p (a f) -> p a f", a=8), ACT.Copy,
                              scale=lrr[t][:, 1:2]).then_inc(u_out[t], 1)
                sc.activation(mv[t][:], pT[1][:], ACT.Copy, scale=lrr[t][:, 1:2]).then_inc(u_out[t], 1)

            def MT(t, ph):
                sc.wait_ge(mT_psum[t], 1)
                for half in range(2):
                    sc.activation(mqT[:, 4 * half:4 * half + 4, P * t:P * (t + 1)],
                                  (pG, pT)[half][0][0:QK, :].rearrange("p (a r) -> p a r", a=4), ACT.Copy).then_inc(mqT_ready[t], 1)

            def ME(v, ph):
                t, j = v // 4, v % 4
                sc.wait_ge(mmax_ready, v + 1)
                if v >= 2:
                    sc.wait_ge(mpT_psum, v - 1)
                for x in range(2):
                    hd = 2 * j + x
                    sc.activation(mp[v % 2][:, x, :], pG[v % 2][:, SEQ * x:SEQ * (x + 1)], ACT.Exp, bias=negm[t][:, hd:hd + 1],
                                  scale=MLA_SCALE, accum_out=lsum[t][:, hd:hd + 1]).then_inc(mp_ready, 1)

            def RT(t, ph):
                sc.wait_ge(rT_psum[t], 1)
                sc.activation(rqT[:, :, P * t:P * (t + 1)], pG[0][:].rearrange("p (a r) -> p a r", a=4),
                              ACT.Copy).then_inc(rqT_ready[t], 1)

            def decay(hd, ph):
                sc.wait_ge(dm_arg, hd + 1)
                sc.activation(dm[hd % 2][:], dm[hd % 2][:], ACT.Exp).then_inc(dm_ready, 1)

            def gate_r(t, ph):
                if t == 1:
                    sc.wait_ge(w_freed, C_X[4] + 4)
                else:
                    sc.wait_ge(x_done0, 5)
                sc.wait_ge(rT_psum[t], 2)
                sc.activation(rqk[t][:, 512:1024], pD[t][:, 0:512], ACT.Silu, scale=rr[t]).then_inc(rgate[t], 1)

            def MAT(t, ph):
                sc.wait_ge(catT_psum[t], 1)
                sc.activation(xTh[t][:, 0:4, :].rearrange("p k r -> p (k r)"), pD[t][:, 512:1024], ACT.Copy).then_inc(cath_ready[t], 1)

            def RAT(t, ph):
                sc.wait_ge(catT_psum[t], 2)
                sc.activation(xTh[t][:, 4:8, :].rearrange("p k r -> p (k r)"), pG[t][:], ACT.Copy).then_inc(cath_ready[t], 1)

            def Oc(t, kt, ph):
                if t == 1:
                    refill(C_WO + kt, 1)

            parts = dict(start=start, fill=fill, prep=prep, tail=tail, G=G, D=Dn, T=T, proj=proj, QKT=QKT, E=E, AO=AO, AT=AT,
                         O=O, X=X, LAT=LAT, U=U, MT=MT, ME=ME, RT=RT, decay=decay, gate=gate_r, MAT=MAT, RAT=RAT, Oc=Oc)
            walk(sc, lambda name, *a, ph=None: parts[name](*a, ph) if name in parts else None)

        @block.vector
        def _(ve):
            links = [0]

            def chain(ins):
                links[0] += 1
                return ins.then_inc(ve_chain, 1)

            def joined():
                ve.wait_ge(ve_chain, links[0])

            def split_low(c, static):
                ve.wait_ge(w_high_done, c + 1)
                ve.tensor_tensor(w_low[:, slot(static):slot(static) + CHUNK],
                                 raw[:, static % RAW * CHUNK:(static % RAW + 1) * CHUNK],
                                 w_high[:, slot(static):slot(static) + CHUNK].bitcast(F32), ALU.subtract).then_inc(w_split, 1)

            def refill(first, n, shift=0):
                for c in range(first + RING, first + RING + n):
                    if c < N_CHUNKS:
                        split_low(c + shift * RING, c)

            def start(ph):
                ve.wait_ge(consts_loaded, 16)
                ve.wait_ge(feats_loaded, 16)
                ve.wait_ge(table_loaded, 16)
                ve.tensor_scalar(nsink[:], table[:, T_SINK:T_SINK + 16], -1.0, None, ALU.mult).then_inc(nsink_ready, 1)

            def fill(first, n, ph):
                for c in range(first, first + n):
                    split_low(c, c)

            def prep(t, p, ph):
                if p == LAST:
                    final(t)
                    return
                n = xT_base(p)
                sets = [(GAIN[p], xTh, xTl)] + ([(GAIN["q"], x2h, x2l)] if p == B_INDEX else [])
                for col, high, low in sets:
                    if n > xT_base(p):
                        ve.wait_ge(xT_ready[t], n)
                    for half in range(2):
                        ve.wait_ge(hT_psum[t], 2 * p + half + 1)
                        g = feats[:, col + 4 * half:col + 4 * half + 4].unsqueeze(2).broadcast_to([P, 4, P])
                        ve.tensor_tensor(hg[t][:, 512 * half:512 * half + 512].rearrange("p (k r) -> p k r", k=4),
                                         (pG, pT)[half][t][:].rearrange("p (k r) -> p k r", k=4), g,
                                         ALU.mult).then_inc(hg_ready[t], 1)
                    for half in range(2):
                        n += 1
                        ve.wait_ge(xh_ready[t], n)
                        ve.tensor_tensor(low[t][:, 4 * half:4 * half + 4, :].rearrange("p k r -> p (k r)"),
                                         hg[t][:, 512 * half:512 * half + 512],
                                         high[t][:, 4 * half:4 * half + 4, :].rearrange("p k r -> p (k r)").bitcast(F32),
                                         ALU.subtract).then_inc(xT_ready[t], 1)

            def final(t):
                ve.wait_ge(r_ready[t], LAST + 1)
                ve.wait_ge(post_loaded, 16 * (POST_NORMS + 1))
                ve.scalar_tensor_tensor(hg[t][:], h[t][:], rr[t], post[:], ALU.mult, ALU.mult).then_inc(out_ready[t], 1)

            def tail(t, k, ph):
                if k < POST_NORMS:
                    ve.wait_ge(pr_ready[t], k + 1)
                    ve.wait_ge(post_loaded, 16 * (k + 1))
                    chain(ve.scalar_tensor_tensor(hg[t][:], pD[t][:], prr[t], post[:], ALU.mult, ALU.mult))
                    joined()
                    ve.tensor_tensor(h[t][:], h[t][:], hg[t][:], ALU.add).then_inc(h_ready[t], 1)
                else:
                    branch_done(ve, t, k)
                    ve.scalar_tensor_tensor(h[t][:], pD[t][:], 1.0 if k == C_INDEX else 0.5, h[t][:],
                                            ALU.mult, ALU.add).then_inc(h_ready[t], 1)

            def G(t, b, shift, ph):
                n = ph.first_block + b + 1 + shift * (RING // (ph.cg + ph.kd))
                if t == 1:
                    refill(ph.g_chunk(b), ph.cg, shift)
                ve.wait_ge(gate_ready[t], n)
                if ph.mixer:
                    ve.scalar_tensor_tensor(act[t][:, 0:P], pG[t][:, 256:384], rr[t], gate[t][:, P:2 * P],
                                            ALU.mult, ALU.mult).then_inc(act_ready[t], 1)
                else:
                    ve.scalar_tensor_tensor(act[t][:], pG[t][:, 256:512], rr[t], gate[t][:],
                                            ALU.mult, ALU.mult).then_inc(act_ready[t], 1)

            def Dn(t, b, shift, ph):
                if t == 1:
                    refill(ph.d_chunk(b), ph.kd, shift)

            def T(t, b, shift, ph):
                n = ph.first_block + b + 1 + shift * (RING // (ph.cg + ph.kd))
                if ph.mixer:
                    ve.wait_ge(cuT_ready[t], b + 1)
                    taps = [feats[:, CONV + 3 * b + w:CONV + 3 * b + w + 1] for w in range(3)]
                    src = [cv[b % 3][:, P * t + w:P * t + w + P] for w in range(3)]
                    done = 4 * b
                    ve.tensor_scalar(yT[t][:], src[0], taps[0], None, ALU.mult).then_inc(conv_done[t], 1)
                    for w in (1, 2):
                        ve.wait_ge(conv_done[t], done + w)
                        ve.scalar_tensor_tensor(yT[t][:], src[w], taps[w], yT[t][:], ALU.mult, ALU.add).then_inc(conv_done[t], 1)
                    ve.wait_ge(conv_done[t], done + 3)
                    ve.tensor_tensor(yT[t][:], pT[t][:, 0:P], yT[t][:], ALU.mult).then_inc(conv_done[t], 1)
                    ve.wait_ge(ah_ready[t], n)
                    ve.tensor_tensor(aTl[t][:, 0, :], yT[t][:], aTh[t][:, 0, :].bitcast(F32), ALU.subtract).then_inc(aT_ready[t], 1)
                else:
                    ve.wait_ge(ah_ready[t], n)
                    ve.tensor_tensor(aTl[t][:].rearrange("p k r -> p (k r)"), pT[t][:, 0:256],
                                     aTh[t][:].rearrange("p k r -> p (k r)").bitcast(F32), ALU.subtract).then_inc(aT_ready[t], 1)

            def proj(j, t, c, ph):
                if t == 1:
                    refill(B_FIRST + 4 * j + c, 1)

            def rope(t, ph):
                ve.wait_ge(qkv_ready[t], 3)
                qk = qkv[t][:, 256:1536].rearrange("p (a f) -> p a f", f=HD)
                a, b = qk[:, :, 0:ROT_HALF], qk[:, :, ROT_HALF:2 * ROT_HALF]
                co, si = (rope1[:, t, i, :].unsqueeze(1).broadcast_to([P, 20, ROT_HALF]) for i in range(2))
                for i, (u, w) in enumerate(((a, co), (b, si), (b, co), (a, si))):
                    chain(ve.tensor_tensor(rtmp[i][:], u, w, ALU.mult))
                joined()
                ve.tensor_tensor(a, rtmp[0][:], rtmp[1][:], ALU.subtract).then_inc(rope_done, 1)
                ve.tensor_tensor(b, rtmp[2][:], rtmp[3][:], ALU.add).then_inc(rope_done, 1)

            def QKT(t, ph):
                ve.wait_ge(qkT_psum[t], 3)
                ve.tensor_copy(qT[t][:, 4:8, :].rearrange("p a r -> p (a r)"), pD[t][:, 0:512]).then_inc(kqT_dve[t], 1)

            def S(t, u, ph):
                v, m, half = 8 * t + u, u // 2, u % 2
                keys = slice(P * (1 - t), SEQ)
                nk = P * (1 + t)
                bank = (pT, pG)[half][t]
                ve.wait_ge(s_done, v + 1)
                if v >= 2:
                    ve.wait_ge(p_ready, 2 * (v - 1))
                for x in range(2):
                    col = 2 * (2 * m + x) + half
                    chain(ve.tensor_tensor_reduce(sm[v % 2][:, x, keys], bank[:, SEQ * x:SEQ * x + nk], mask[:, keys], HD ** -0.5,
                                                  NEG, ALU.add, ALU.max, mx[t][:, col:col + 1]))
                joined()
                if v == 0:
                    ve.wait_ge(nsink_ready, 1)
                cols = slice(4 * m + half, 4 * m + half + 3, 2)
                ve.scalar_tensor_tensor(negm[t][:, cols], mx[t][:, cols], -1.0, nsink[:, cols], ALU.mult, ALU.min).then_inc(sm_ready, 1)

            def PT(t, u, ph):
                v = 8 * t + u
                ve.wait_ge(pT_psum, v + 1)
                if v >= 2:
                    ve.wait_ge(pv_done, v - 1)
                n = 2 * P * (1 + t)
                ve.tensor_copy(prT[v % 2][:, 0:n], pD[t][:, 0:n]).then_inc(pT_ready, 1)

            def AO(t, half, ph):
                cols = slice(8 * half, 8 * half + 8)
                ve.tensor_tensor(esink[t][:, cols], negm[t][:, cols], table[:, T_SINK + 8 * half:T_SINK + 8 * half + 8],
                                 ALU.add).then_inc(es_arg[t], 1)
                ve.wait_ge(es_ready[t], half + 1)
                ve.wait_ge(p_ready, 16 * t + 8 * (half + 1))
                chain(ve.tensor_tensor(lsum[t][:, cols], lsum[t][:, cols], esink[t][:, cols], ALU.add))
                joined()
                chain(ve.reciprocal(lrec[t][:, cols], lsum[t][:, cols]))
                joined()
                ve.wait_ge(pv_done, 8 * t + 4 * half + 4)
                ve.tensor_tensor(qkv[t][:, 512 + 512 * half:1024 + 512 * half].rearrange("p (a f) -> p a f", f=HD),
                                 pD[t][:, 512:1024].rearrange("p (a f) -> p a f", f=HD),
                                 lrec[t][:, cols].unsqueeze(2).broadcast_to([P, 8, HD]), ALU.mult).then_inc(ao_ready[t], 1)

            def AT(t, ph):
                for half in range(2):
                    ve.wait_ge(aoh_ready[t], half + 1)
                    ve.tensor_tensor(xTl[t][:, 4 * half:4 * half + 4, :].rearrange("p k r -> p (k r)"), (pT, pG)[half][t][:],
                                     xTh[t][:, 4 * half:4 * half + 4, :].rearrange("p k r -> p (k r)").bitcast(F32),
                                     ALU.subtract).then_inc(aoT_ready[t], 1)

            def O(t, kt, ph):
                if t == 1:
                    refill(B_WO + kt, 1)

            def X(i, t, c, ph):
                if t == 1:
                    refill(C_X[i] + c, 1)

            def LAT(t, ph):
                ve.wait_ge(latT_psum[t], 1)
                g = feats[:, GAIN_LAT:GAIN_LAT + 3].unsqueeze(2).broadcast_to([P, 3, P])
                ve.tensor_tensor(latf[:], pD[t][:, 512:896].rearrange("p (k r) -> p k r", k=3), g, ALU.mult).then_inc(latf_ready[t], 1)
                ve.wait_ge(lath_ready[t], 1)
                ve.tensor_tensor(latTl[:], latf[:], latTh[:].bitcast(F32), ALU.subtract).then_inc(latT_ready[t], 1)

            def rotate(x1, x2, co, si, tmp):
                chain(ve.tensor_tensor(tmp[0], x1, co, ALU.mult))
                chain(ve.tensor_tensor(tmp[1], x2, si, ALU.mult))
                chain(ve.tensor_tensor(tmp[2], x1, si, ALU.mult))
                chain(ve.tensor_tensor(tmp[3], x2, co, ALU.mult))
                joined()
                chain(ve.tensor_tensor(x1, tmp[0], tmp[1], ALU.subtract))
                return ve.tensor_tensor(x2, tmp[2], tmp[3], ALU.add)

            def U(t, ph):
                if t == 1:
                    refill(C_U, 3)
                else:
                    ve.wait_ge(sincos_ready, 2)
                half = PE_DIM // 2
                co, si = (x[:, t, 0:32:2] for x in (cos2, sin2))
                kp = lat[t][:, Q_RANK + KV_RANK:LATENT]
                tmp = [mpT[0][:, i * 128:i * 128 + 128].rearrange("p (a f) -> p a f", a=8) for i in range(4)]
                chain(rotate(kp[:, 0:half], kp[:, half:PE_DIM], co, si, [x[:, 0, :] for x in tmp]))
                joined()
                ve.wait_ge(u_out[t], 4)
                ve.tensor_copy(mk[:, :, NOPE:QK], kp.unsqueeze(1).broadcast_to([P, MLA_HEADS, PE_DIM])).then_inc(mqk_ready[t], 1)
                wide = [x.unsqueeze(1).broadcast_to([P, 8, half]) for x in (co, si)]
                rotate(mq[:, :, NOPE:NOPE + half], mq[:, :, NOPE + half:QK], *wide, tmp).then_inc(mqk_ready[t], 1)

            def MT(t, ph):
                ve.wait_ge(mT_psum[t], 2)
                for half in range(2):
                    ve.tensor_copy(mkT[:, 4 * half:4 * half + 4, P * t:P * (t + 1)],
                                   (pG, pT)[half][1][0:QK, :].rearrange("p (a r) -> p a r", a=4)).then_inc(mkT_ready[t], 1)

            def MS(v, ph):
                t, j = v // 4, v % 4
                ve.wait_ge(ms_psum, v + 1)
                chain(ve.tensor_reduce(mx[t][:, 2 * j:2 * j + 2], pG[v % 2][:].rearrange("p (x k) -> p x k", x=2), AX.X, ALU.max,
                                       negate=True))
                joined()
                ve.tensor_scalar(negm[t][:, 2 * j:2 * j + 2], mx[t][:, 2 * j:2 * j + 2], MLA_SCALE, None, ALU.mult).then_inc(mmax_ready, 1)

            def MPT(v, ph):
                ve.wait_ge(mpT_psum, v + 1)
                if v >= 2:
                    ve.wait_ge(mpv_done, v - 1)
                ve.tensor_copy(mpT[v % 2][:], pT[v % 2][:]).then_inc(mpT_ready, 1)

            def MN(t, ph):
                ve.wait_ge(mp_ready, 8 * (t + 1))
                chain(ve.reciprocal(lrec[t][:, 0:8], lsum[t][:, 0:8]))
                joined()
                ve.wait_ge(mpv_done, 4 * (t + 1))
                ve.tensor_tensor(mo[t][:].rearrange("p (a f) -> p a f", f=HD), pD[t][:, 512:1024].rearrange("p (a f) -> p a f", f=HD),
                                 lrec[t][:, 0:8].unsqueeze(2).broadcast_to([P, 8, HD]), ALU.mult).then_inc(mo_ready[t], 1)

            def RROPE(t, part, ph):
                if part == 0:
                    ve.wait_ge(x_out[t], 3)
                if t or part:
                    ve.wait_ge(rrope_done[t if part else 0], 1 if part else 2)
                z = rqk[t][:, 512 * part:512 * part + 512].rearrange("p (a f) -> p a f", f=HD)
                co, si = (x[:, t, :].unsqueeze(1).broadcast_to([P, 8, RHALF]) for x in (cos2, sin2))
                rotate(z[:, :, 0:RHALF], z[:, :, RHALF:HD], co, si, [x[:] for x in ttmp]).then_inc(rrope_done[t], 1)

            def RT(t, ph):
                ve.wait_ge(rT_psum[t], 2)
                ve.tensor_copy(rkT[:, :, P * t:P * (t + 1)], pG[1][:].rearrange("p (a r) -> p a r", a=4)).then_inc(rkT_ready[t], 1)

            def RM(hd, ph):
                ve.wait_ge(rs_psum, hd + 1)
                ve.wait_ge(dm_ready, hd + 1)
                if hd >= 2:
                    ve.wait_ge(rpv_done, hd - 1)
                for jt in range(2):
                    ve.scalar_tensor_tensor(sd[hd % 2][:, jt, :], pG[hd % 2][:, SEQ * jt:SEQ * (jt + 1)], HD ** -0.5,
                                            dm[hd % 2][:, P * (1 - jt):P * (3 - jt)], ALU.mult, ALU.mult).then_inc(sd_ready, 1)

            def GN(t, ph):
                o = pT[t][:].rearrange("p (a f) -> p a f", f=HD)
                ro = rqk[t][:, 0:512].rearrange("p (a f) -> p a f", f=HD)
                gated = rqk[t][:, 512:1024].rearrange("p (a f) -> p a f", f=HD)
                sq = mpT[t][:].rearrange("p (a f) -> p a f", f=HD)
                ve.wait_ge(rpv_done, 8)
                chain(ve.tensor_reduce(gn[t][:, 0, :], o, AX.X, ALU.add))
                joined()
                chain(ve.tensor_scalar(gn[t][:, 0, :], gn[t][:, 0, :], 1.0 / HD, None, ALU.mult))
                joined()
                chain(ve.tensor_tensor(ro, o, gn[t][:, 0, :].unsqueeze(2).broadcast_to([P, 8, HD]), ALU.subtract))
                joined()
                chain(ve.tensor_tensor(sq, ro, ro, ALU.mult))
                joined()
                ve.tensor_reduce(gn[t][:, 1, :], sq, AX.X, ALU.add).then_inc(gn_var[t], 1)
                ve.wait_ge(rgate[t], 1)
                chain(ve.tensor_tensor(gated, gated, ro, ALU.mult))
                joined()
                ve.wait_ge(gn_r[t], 1)
                ve.tensor_tensor(ro, gated, gn[t][:, 3, :].unsqueeze(2).broadcast_to([P, 8, HD]), ALU.mult).then_inc(ro_ready[t], 1)

            def MAT(t, ph):
                ve.wait_ge(cath_ready[t], 1)
                ve.tensor_tensor(xTl[t][:, 0:4, :].rearrange("p k r -> p (k r)"), pD[t][:, 512:1024],
                                 xTh[t][:, 0:4, :].rearrange("p k r -> p (k r)").bitcast(F32), ALU.subtract).then_inc(catT_ready[t], 1)

            def RAT(t, ph):
                ve.wait_ge(cath_ready[t], 2)
                ve.tensor_tensor(xTl[t][:, 4:8, :].rearrange("p k r -> p (k r)"), pG[t][:],
                                 xTh[t][:, 4:8, :].rearrange("p k r -> p (k r)").bitcast(F32), ALU.subtract).then_inc(catT_ready[t], 1)

            def Oc(t, kt, ph):
                if t == 1:
                    refill(C_WO + kt, 1)

            parts = dict(start=start, fill=fill, prep=prep, tail=tail, G=G, D=Dn, T=T, proj=proj, rope=rope, QKT=QKT, S=S, PT=PT,
                         AO=AO, AT=AT, O=O, X=X, LAT=LAT, U=U, MT=MT, MS=MS, MPT=MPT, MN=MN, RROPE=RROPE, RT=RT, RM=RM, GN=GN,
                         MAT=MAT, RAT=RAT, Oc=Oc)
            walk(ve, lambda name, *a, ph=None: parts[name](*a, ph) if name in parts else None)

        @block.tensor
        def _(pe):
            def three_passes(dst, ah, al, where, n, start, stop):
                hi, lo = w_high[:, where:where + n], w_low[:, where:where + n]
                pe.matmul(dst, ah, hi, start=start, stop=False)
                pe.matmul(dst, ah, lo, start=False, stop=False)
                return pe.matmul(dst, al, hi, start=False, stop=stop)

            def turn(dst, src):
                return pe.transpose(dst, src, ident)

            def start(ph):
                pe.wait_ge(consts_loaded, 16)

            def prep(t, p, ph):
                if p == LAST:
                    return
                if p == 0:
                    pe.wait_ge(x_loaded[t], 16)
                else:
                    pe.wait_ge(h_ready[t], p)
                for kt in range(KT):
                    mm = turn((pG, pT)[kt // 4][t][:, kt % 4 * P:(kt % 4 + 1) * P], h[t][:, kt * P:(kt + 1) * P])
                    if kt % 4 == 3:
                        mm.then_inc(hT_psum[t], 1)

            def G(t, b, shift, ph):
                c0 = ph.g_chunk(b)
                have = 0
                for kt in range(KT):
                    if b == 0 and kt % 4 == 0:
                        pe.wait_ge(xT_ready[t], xT_base(ph.index) + kt // 4 + 1)
                    need = ((kt + 1) * ph.cols - 1) // CHUNK + 1
                    if need > have and t == 0:
                        pe.wait_ge(w_split, c0 + need + shift * RING)
                    mm = three_passes(pG[t][:, 0:ph.cols], xTh[t][:, kt, :], xTl[t][:, kt, :], slot(c0 + kt * ph.cols // CHUNK) + kt * ph.cols % CHUNK, ph.cols,
                                      kt == 0, kt == KT - 1)
                    have = need
                    if t == 1 and (kt + 1) * ph.cols // CHUNK > kt * ph.cols // CHUNK:
                        mm.then_inc(w_freed, 1)
                    if t == 0 and kt == KT - 1:
                        mm.then_inc(g_done0, 1)

            def T(t, b, shift, ph):
                n = ph.first_block + b + 1 + shift * (RING // (ph.cg + ph.kd))
                pe.wait_ge(act_ready[t], n)
                if ph.mixer:
                    turn(pT[t][:, 0:P], gate[t][:, 0:P])
                    turn(pT[t][:, P:2 * P], act[t][:, 0:P]).then_inc(actT_psum[t], 1)
                else:
                    turn(pT[t][:, 0:P], act[t][:, 0:P])
                    turn(pT[t][:, P:2 * P], act[t][:, P:2 * P]).then_inc(actT_psum[t], 1)

            def Dn(t, b, shift, ph):
                n = ph.first_block + b + 1 + shift * (RING // (ph.cg + ph.kd))
                pe.wait_ge(aT_ready[t], n)
                for k in range(ph.kd):
                    c = ph.d_chunk(b) + k
                    if t == 0:
                        pe.wait_ge(w_split, c + 1 + shift * RING)
                    for half in range(2):
                        mm = three_passes(pD[t][:, 512 * half:512 * half + 512], aTh[t][:, k, :], aTl[t][:, k, :],
                                          slot(c) + 512 * half, 512, b == 0 and k == 0, b == ph.nb - 1 and k == ph.kd - 1)
                    if t == 1:
                        mm.then_inc(w_freed, 1)
                    elif b == ph.nb - 1 and k == ph.kd - 1:
                        mm.then_inc(d_done0, 1)

            def proj(j, t, c, ph):
                dst = pG[t][:] if j == 2 else pD[t][:, 512 * j:512 * j + 512]
                high, low = (x2h, x2l) if j else (xTh, xTl)
                if c % 2 == 0:
                    pe.wait_ge(xT_ready[t], xT_base(B_INDEX) + (2 if j else 0) + c // 2 + 1)
                if j == 2 and c == 0:
                    pe.wait_ge(xT_ready[t], xT_base(B_INDEX) + 4)
                w = B_FIRST + 4 * j + c
                if t == 0:
                    pe.wait_ge(w_split, w + 1)
                for i in range(2):
                    kt = 2 * c + i
                    mm = three_passes(dst, high[t][:, kt, :], low[t][:, kt, :], slot(w) + 512 * i, 512, kt == 0, kt == KT - 1)
                if t == 1:
                    mm.then_inc(w_freed, 1)
                elif c == 3:
                    mm.then_inc(q_done0, 1)

            def QKT(t, ph):
                pe.wait_ge(rope_done, 2 * (t + 1))
                for i in range(2):
                    mm = turn(pT[t][:, P * i:P * (i + 1)], qkv[t][:, 256 + P * i:256 + P * (i + 1)])
                mm.then_inc(qkT_psum[t], 1)
                for i in range(PAIRS):
                    mm = turn((pG[t], pD[t])[i // 4][:, i % 4 * P:(i % 4 + 1) * P], qkv[t][:, 512 + P * i:512 + P * (i + 1)])
                    if i % 4 == 3:
                        mm.then_inc(qkT_psum[t], 1)

            def S(t, u, ph):
                v, m, half = 8 * t + u, u // 2, u % 2
                if u == 0:
                    pe.wait_ge(kqT_act[t], 2)
                    pe.wait_ge(kqT_dve[t], 1)
                if u >= 2:
                    pe.wait_ge(sm_ready, v - 1)
                part = slice(HD * half, HD * half + HD)
                for x in range(2):
                    i = 2 * m + x
                    nk = P * (1 + t)
                    mm = pe.matmul((pT, pG)[half][t][:, SEQ * x:SEQ * x + nk], qT[t][part, i, :], kT[part, i // 4, 0:nk],
                                   start=True, stop=True)
                mm.then_inc(s_done, 1)

            def PT(t, u, ph):
                v = 8 * t + u
                pe.wait_ge(p_ready, 2 * (v + 1))
                if u >= 1:
                    pe.wait_ge(pT_ready, v)
                n = 0
                for x in range(2):
                    for kt in range(1 - t, 2):
                        mm = turn(pD[t][:, P * n:P * (n + 1)], pr[v % 2][:, x, P * kt:P * (kt + 1)])
                        n += 1
                mm.then_inc(pT_psum, 1)

            def PV(t, u, ph):
                v, m, half = 8 * t + u, u // 2, u % 2
                pe.wait_ge(pT_ready, v + 1)
                if u == 4:
                    pe.wait_ge(ao_ready[t], 1)
                n = 0
                for x in range(2):
                    i = 2 * m + x
                    kv = 2 * (i // 4) + half
                    dst = pD[t][:, 512 + i % 4 * P + HD * half:512 + i % 4 * P + HD * half + HD]
                    for kt in range(1 + t):
                        mm = pe.matmul(dst, prT[v % 2][:, P * n:P * (n + 1)], qkv[kt][:, HD * kv:HD * kv + HD],
                                       start=kt == 0, stop=kt == t)
                        n += 1
                mm.then_inc(pv_done, 1)

            def AT(t, ph):
                pe.wait_ge(ao_ready[t], 2)
                for kt in range(KT):
                    mm = turn((pT, pG)[kt // 4][t][:, kt % 4 * P:(kt % 4 + 1) * P], qkv[t][:, 512 + P * kt:512 + P * (kt + 1)])
                    if kt % 4 == 3:
                        mm.then_inc(aoT_psum[t], 1)

            def out_product(t, kt, w):
                for half in range(2):
                    mm = three_passes(pD[t][:, 512 * half:512 * half + 512], xTh[t][:, kt, :], xTl[t][:, kt, :],
                                      slot(w) + 512 * half, 512, kt == 0, kt == KT - 1)
                if t == 1:
                    mm.then_inc(w_freed, 1)
                elif kt == KT - 1:
                    mm.then_inc(d_done0, 1)

            def O(t, kt, ph):
                if kt % 4 == 0:
                    pe.wait_ge(aoT_ready[t], kt // 4 + 1)
                if t == 0:
                    pe.wait_ge(w_split, B_WO + kt + 1)
                out_product(t, kt, B_WO + kt)

            def X(i, t, c, ph):
                n = LATENT if i == 0 else 512
                if i == 0 and c % 2 == 0:
                    pe.wait_ge(xT_ready[t], xT_base(C_INDEX) + c // 2 + 1)
                if c == 0 and i > 0:
                    pe.wait_ge(x_out[t], i)
                w = C_X[i] + c
                if t == 0:
                    pe.wait_ge(w_split, w + 1)
                for k in range(2):
                    kt = 2 * c + k
                    mm = three_passes(pD[t][:, 0:n], xTh[t][:, kt, :], xTl[t][:, kt, :], slot(w) + 512 * k, n, kt == 0, kt == KT - 1)
                if t == 1:
                    mm.then_inc(w_freed, 1)
                elif c == 3:
                    mm.then_inc(x_done0, 1)

            def LAT_(t, ph):
                pe.wait_ge(x_out[t], 1)
                for k in range(3):
                    mm = turn(pD[t][:, 512 + P * k:512 + P * (k + 1)], lat[t][:, P * k:P * (k + 1)])
                mm.then_inc(latT_psum[t], 1)

            def U(t, ph):
                pe.wait_ge(latT_ready[t], 1)
                if t == 1:
                    pe.wait_ge(mqT_ready[0], 2)
                    pe.wait_ge(mkT_ready[0], 2)
                else:
                    pe.wait_ge(xT_ready[1], xT_base(C_INDEX) + 2)
                for k in range(3):
                    w = C_U + k
                    if t == 0:
                        pe.wait_ge(w_split, w + 1)
                    for half in range(2):
                        if k < 2:
                            mm = three_passes((pG, pT)[half][0][:, 0:384], latTh[:, k, :], latTl[:, k, :], slot(w) + 384 * half, 384,
                                              k == 0, k == 1)
                        else:
                            mm = three_passes((pG, pT)[half][1][:], latTh[:, k, :], latTl[:, k, :], slot(w) + 512 * half, 512, True, True)
                    if t == 1:
                        mm.then_inc(w_freed, 1)
                if t == 0:
                    mm.then_inc(u_done0, 1)

            def MT(t, ph):
                pe.wait_ge(mqk_ready[t], 2)
                for i, src in enumerate((mq, mk)):
                    for hd in range(MLA_HEADS):
                        mm = turn((pG, pT)[hd // 4][i][0:QK, hd % 4 * P:(hd % 4 + 1) * P], src[:, hd, :])
                    mm.then_inc(mT_psum[t], 1)

            def MS(v, ph):
                t, j = v // 4, v % 4
                if v == 0:
                    for r in range(2):
                        pe.wait_ge(mqT_ready[r], 2)
                        pe.wait_ge(mkT_ready[r], 2)
                if v >= 2:
                    pe.wait_ge(mp_ready, 2 * (v - 1))
                for x in range(2):
                    hd = 2 * j + x
                    mm = pe.matmul(pG[v % 2][:, SEQ * x:SEQ * (x + 1)], mqT[:, hd, P * t:P * (t + 1)], mkT[:, hd, :],
                                   start=True, stop=True)
                mm.then_inc(ms_psum, 1)

            def MPT(v, ph):
                pe.wait_ge(mp_ready, 2 * (v + 1))
                if v >= 2:
                    pe.wait_ge(mpT_ready, v - 1)
                for x in range(2):
                    for kt in range(2):
                        mm = turn(pT[v % 2][:, (2 * x + kt) * P:(2 * x + kt + 1) * P], mp[v % 2][:, x, P * kt:P * (kt + 1)])
                mm.then_inc(mpT_psum, 1)

            def MPV(v, ph):
                t, j = v // 4, v % 4
                pe.wait_ge(mpT_ready, v + 1)
                for x in range(2):
                    hd = 2 * j + x
                    for kt in range(2):
                        mm = pe.matmul(pD[t][:, 512 + HD * hd:512 + HD * (hd + 1)], mpT[v % 2][:, (2 * x + kt) * P:(2 * x + kt + 1) * P],
                                       mv[kt][:, HD * hd:HD * (hd + 1)], start=kt == 0, stop=kt == 1)
                mm.then_inc(mpv_done, 1)

            def RT(t, ph):
                pe.wait_ge(rrope_done[t], 2)
                if t == 0:
                    pe.wait_ge(mp_ready, 16)
                else:
                    pe.wait_ge(rqT_ready[0], 1)
                    pe.wait_ge(rkT_ready[0], 1)
                for i in range(2):
                    for k in range(4):
                        mm = turn(pG[i][:, P * k:P * (k + 1)], rqk[t][:, 512 * i + P * k:512 * i + P * (k + 1)])
                    mm.then_inc(rT_psum[t], 1)

            def RS(hd, ph):
                if hd == 0:
                    pe.wait_ge(rqT_ready[1], 1)
                    pe.wait_ge(rkT_ready[1], 1)
                if hd >= 2:
                    pe.wait_ge(sd_ready, 2 * (hd - 1))
                part = slice(HD * (hd % 2), HD * (hd % 2) + HD)
                for jt in range(2):
                    mm = pe.matmul(pG[hd % 2][:, SEQ * jt:SEQ * (jt + 1)], rkT[part, hd // 2, P * jt:P * (jt + 1)],
                                   rqT[part, hd // 2, :], start=True, stop=True)
                mm.then_inc(rs_psum, 1)

            def RPV(hd, ph):
                pe.wait_ge(sd_ready, 2 * (hd + 1))
                if hd == 0:
                    pe.wait_ge(mpT_ready, 8)
                    pe.wait_ge(x_out[0], 4)
                    pe.wait_ge(x_out[1], 4)
                for t in range(2):
                    for jt in range(2):
                        mm = pe.matmul(pT[t][:, HD * hd:HD * (hd + 1)], sd[hd % 2][:, jt, P * t:P * (t + 1)],
                                       rv[jt][:, HD * hd:HD * (hd + 1)], start=jt == 0, stop=jt == 1)
                mm.then_inc(rpv_done, 1)

            def MAT(t, ph):
                pe.wait_ge(mo_ready[t], 1)
                for k in range(4):
                    mm = turn(pD[t][:, 512 + P * k:512 + P * (k + 1)], mo[t][:, P * k:P * (k + 1)])
                mm.then_inc(catT_psum[t], 1)

            def RAT(t, ph):
                pe.wait_ge(ro_ready[t], 1)
                for k in range(4):
                    mm = turn(pG[t][:, P * k:P * (k + 1)], rqk[t][:, P * k:P * (k + 1)])
                mm.then_inc(catT_psum[t], 1)

            def Oc(t, kt, ph):
                if kt == 0:
                    pe.wait_ge(rgate[t], 1)
                if kt % 4 == 0:
                    pe.wait_ge(catT_ready[t], kt // 4 + 1)
                if t == 0:
                    pe.wait_ge(w_split, C_WO + kt + 1)
                out_product(t, kt, C_WO + kt)

            parts = dict(start=start, prep=prep, G=G, D=Dn, T=T, proj=proj, QKT=QKT, S=S, PT=PT, PV=PV, AT=AT, O=O, X=X, LAT=LAT_,
                         U=U, MT=MT, MS=MS, MPT=MPT, MPV=MPV, RT=RT, RS=RS, RPV=RPV, MAT=MAT, RAT=RAT, Oc=Oc)
            walk(pe, lambda name, *a, ph=None: parts[name](*a, ph) if name in parts else None)


class NoLoop:

    def Fori(self, first, last):
        return ExitStack()



def weight_chunks(w):
    parts = []

    def sliced(cols, pad=0):
        if pad:
            cols = np.concatenate([cols, np.zeros((cols.shape[0], pad), cols.dtype)], axis=1)
        wide = cols.reshape(KT, P, -1).transpose(1, 0, 2).reshape(P, -1)
        return list(wide.reshape(P, -1, CHUNK).transpose(1, 0, 2))

    def blocks(ph, inputs, output):
        found = {}
        wide = ph.cols // len(inputs)
        for b in range(ph.nb):
            cols = np.concatenate([m[:, wide * b:wide * (b + 1)] for m in inputs], axis=1)
            for i, c in enumerate(sliced(cols)):
                found[ph.g_chunk(b) + i] = c
            for k in range(ph.kd):
                row = P * (ph.kd * b + k)
                found[ph.d_chunk(b) + k] = output[row:row + P]
        parts.extend(found[c] for c in sorted(found))

    a_in = w["a_w_in"][0]
    blocks(MIX, [a_in[:, D * i:D * (i + 1)] for i in range(3)], w["a_w_out"][0])

    def ffn(ph, layer):
        both = w["ffn_w_gate_up"][layer]
        f = both.shape[1] // 2
        blocks(ph, [both[:, :f], both[:, f:]], w["ffn_w_down"][layer])

    ffn(FFN1, 0)
    kv = w["w_kv"]
    parts.extend(sliced(np.concatenate([kv[:, 256:], kv[:, :256]], axis=1)))
    order = [head_at(i, p) for i in range(PAIRS) for p in range(2)]
    q = w["b_w_q"][0].reshape(D, HEADS, HD)[:, order, :].reshape(D, D)
    for j in range(2):
        parts.extend(sliced(q[:, 512 * j:512 * j + 512]))
    parts.extend(w["b_w_o"][0].reshape(HEADS, HD, D)[order].reshape(KT, P, D))
    ffn(FFN2, 1)
    blocks(FFN3, [w["ffn1_w_gate_2"][0], w["ffn1_w_up_2"][0]], w["ffn1_w_down_2"][0])
    w_in = w["w_in_2"][0]
    parts.extend(sliced(w_in[:, 0:LATENT], 512 - LATENT))
    uq, ukv = w["w_uq_2"][0], w["w_ukv_2"][0].reshape(KV_RANK, MLA_HEADS, 2, HD)
    pad = np.zeros((P, CHUNK - uq.shape[1]), uq.dtype)
    parts.extend(np.concatenate([uq[P * k:P * (k + 1)], pad], axis=1) for k in range(2))
    parts.append(ukv.transpose(0, 2, 1, 3).reshape(P, CHUNK))
    for i in range(4):
        parts.extend(sliced(w_in[:, LATENT + 512 * i:LATENT + 512 * (i + 1)]))
    parts.extend(w["w_o_2"][0].reshape(KT, P, D))
    blocks(FFN4, [w["ffn2_w_gate_2"][0], w["ffn2_w_up_2"][0]], w["ffn2_w_down_2"][0])
    return np.ascontiguousarray(np.stack(parts))


def shape_constants():
    f32 = np.float32
    c = np.zeros((P, CONSTS), f32)
    c[:, C_ID:C_ID + P] = np.eye(P)
    inv = (f32(500000.0) ** (-np.arange(0, 16, 2, dtype=f32) / f32(16))).astype(f32)
    angle = (np.arange(SEQ, dtype=f32)[:, None] * inv[None, :]).astype(f32)
    tab = np.stack([np.cos(angle), np.sin(angle)], axis=1).astype(f32)
    c[:, C_ROPE:C_ROPE + 32] = tab.reshape(2, P, 16).transpose(1, 0, 2).reshape(P, 32)
    i, j = np.arange(P)[:, None], np.arange(P)[None, :]
    c[:, C_MASK:C_MASK + P] = np.where(j > i, 0.0, NEG)
    c[:, C_MASK + P:C_MASK + 2 * P] = np.where(j <= i, 0.0, NEG)
    c[:, C_INV:C_INV + 32] = (f32(10000.0) ** (-np.arange(32, dtype=f32) / f32(32)))[None, :]
    dist = j - i
    c[:, C_REL:C_REL + 4 * P] = np.concatenate(
        [np.maximum(dist, 0), dist + P, np.maximum(-dist, 0), P - dist], axis=1)
    return c


def kernel(**inputs):
    import concourse.bacc as bacc
    from concourse.bass_utils import run_bass_kernel_spmd

    w = {k: np.asarray(v) for k, v in inputs.items()}

    def by_feature(g):
        return np.asarray(g).reshape(-1, P).T

    feats = np.ascontiguousarray(np.concatenate(
        [by_feature(g) for g in (w["a_pre_norm"][0], w["ffn_pre_norm"][0], w["kv_norm"], w["b_pre_norm"][0], w["ffn_pre_norm"][1],
                                 w["ffn1_norm_2"][0], w["mix_norm_2"][0], w["ffn2_norm_2"][0], w["q_norm_2"][0], w["kv_norm_2"][0])]
        + [w["a_conv_w"][0].reshape(3, KT, P).transpose(2, 1, 0).reshape(P, 24)], axis=1))
    order = [head_at(i, p) for i in range(PAIRS) for p in range(2)]
    row = np.concatenate([w["b_sinks"][0][order], w["ret_decay_fwd_2"][0], w["ret_decay_bwd_2"][0]])
    arrays = {
        "x": np.ascontiguousarray(w["x"][0]),
        "stream": weight_chunks(w),
        "feats": feats,
        "consts": shape_constants(),
        "table": np.ascontiguousarray(np.broadcast_to(row, (P, TAB))),
        "positions": np.ascontiguousarray(w["positions_2"].reshape(2, P).T),
        "posts": np.ascontiguousarray(np.stack([w["a_post_norm"][0], w["ffn_post_norm"][0], w["b_post_norm"][0],
                                                w["ffn_post_norm"][1], w["final_norm_2"]])),
    }
    nc = bacc.Bacc("TRN2", target_bir_lowering=False, num_devices=1)
    args = [nc.dram_tensor(f"in_{k}", a.shape, mybir.dt.from_np(a.dtype), kind="ExternalInput").ap() for k, a in arrays.items()]
    out = nc.dram_tensor("out", (SEQ, D), F32, kind="ExternalOutput").ap()
    build(nc, *args, out)
    result = run_bass_kernel_spmd(nc, [{f"in_{k}": a for k, a in arrays.items()}], core_ids=[0])
    return result.results[0]["out"].reshape(1, SEQ, D)
```

```python
import math
from contextlib import ExitStack

import numpy as np

import concourse.bass as bass
from concourse import mybir

F32 = mybir.dt.float32
F32R = mybir.dt.float32r
BF16 = mybir.dt.bfloat16
I32 = mybir.dt.int32
ALU = mybir.AluOpType
ACT = mybir.ActivationFunctionType
AX = mybir.AxisListType

P = 128
D = 1024
KT = D // P
SEQ = 256
EPS = 1e-6
NEG = -1e30

HEADS, KV_HEADS, HD = 16, 4, 64
PAIRS = HEADS // 2
ROT_HALF = 8
MLA_HEADS, NOPE, PE_DIM, QK = 8, 64, 32, 96
Q_RANK, KV_RANK = 256, 128
LATENT = Q_RANK + KV_RANK + PE_DIM
RET_HEADS, RHALF = 8, 32
MLA_SCALE = QK ** -0.5

CHUNK = 1024
RING = 12
RAW = 4


class Phase:

    def __init__(self, mixer, index, first_chunk, first_block):
        self.mixer, self.index = mixer, index
        self.nb, self.cols, self.kd = (8, 384, 1) if mixer else (11, 512, 2)
        self.cg = KT * self.cols // CHUNK
        self.first_chunk, self.first_block = first_chunk, first_block
        self.chunks = self.nb * (self.cg + self.kd)

    def g_chunk(self, b):
        return self.first_chunk + b * self.cg + max(b - 1, 0) * self.kd

    def d_chunk(self, b):
        return self.first_chunk + min(b + 2, self.nb) * self.cg + b * self.kd


MIX = Phase(True, 0, 0, 0)
FFN1 = Phase(False, 1, MIX.chunks, MIX.nb)
B_FIRST = FFN1.first_chunk + FFN1.chunks
B_WO = B_FIRST + 12
FFN2 = Phase(False, 3, B_WO + 8, FFN1.first_block + FFN1.nb)
FFN3 = Phase(False, 4, FFN2.first_chunk + FFN2.chunks, FFN2.first_block + FFN2.nb)
C_FIRST = FFN3.first_chunk + FFN3.chunks
C_X = [C_FIRST, C_FIRST + 4, C_FIRST + 8, C_FIRST + 15, C_FIRST + 19]
C_U = C_FIRST + 12
C_WO = C_X[4] + 4
FFN4 = Phase(False, 6, C_WO + 8, FFN3.first_block + FFN3.nb)
N_CHUNKS = FFN4.first_chunk + FFN4.chunks
B_INDEX, C_INDEX, LAST = 2, 5, 7
POST_NORMS = 4

GAIN = {0: 0, 1: 8, 2: 16, "q": 24, 3: 32, 4: 40, 5: 48, 6: 56}
GAIN_LAT = 64
CONV = 67
FEATS = CONV + 24
C_ID, C_ROPE, C_MASK, C_INV, C_REL = 0, 128, 160, 416, 448
CONSTS = C_REL + 4 * P
T_SINK, T_DECAY, TAB = 0, 16, 32


def head_at(i, p):
    return (2 * (i // 4) + p) * 4 + i % 4



FILL = {0: ((0, 4), (4, 2)), 1: ((6, 1), (7, 5))}


def walk_block_step(ph, s, shift, step):
    if ph.mixer and s in FILL:
        step("fill", *FILL[s][0])
    step("G", 0, s, shift)
    if ph.mixer and s in FILL:
        step("fill", *FILL[s][1])
    if s == 0:
        step("prep", 1, ph.index)
    if s >= 1:
        step("D", 0, s - 1, shift)
    step("T", 0, s, shift)
    if s >= 1:
        walk_follower(ph, s - 1, shift, step)


def walk_follower(ph, b, shift, step):
    step("R", ph.g_chunk(b), ph.cg - 1, shift)
    step("G", 1, b, shift)
    step("R", ph.g_chunk(b) + ph.cg - 1, 1, shift)
    if b >= 1:
        step("D", 1, b - 1, shift)
    step("T", 1, b, shift)
    if b >= 1 and b < ph.nb - 1:
        step("R", ph.d_chunk(b - 1), ph.kd, shift)


def walk_phase(eng, ph, step, trips):
    per = RING // (ph.cg + ph.kd)
    start = 3 if trips else ph.nb
    for s in range(start):
        walk_block_step(ph, s, 0, step)
    if trips:
        with eng.Fori(0, trips) as turn:
            for s in range(start, start + per):
                walk_block_step(ph, s, turn, step)
        for s in range(start + per * trips, ph.nb):
            walk_block_step(ph, s, 0, step)
    last = ph.nb - 1
    step("D", 0, last, 0)
    step("tail", 0, ph.index)
    walk_follower(ph, last, 0, step)
    step("prep", 0, ph.index + 1)
    step("R", ph.d_chunk(last - 1), ph.kd, 0)
    step("D", 1, last, 0)
    step("tail", 1, ph.index)
    step("R", ph.d_chunk(last), ph.kd, 0)


def walk_attention(step):
    def project(j, t, c):
        step("proj", j, t, c)
        if t == 1:
            step("R", B_FIRST + 4 * j + c, 1, 0)

    def output(t, kt):
        step("O", t, kt)
        if t == 1:
            step("R", B_WO + kt, 1, 0)

    for c in range(4):
        project(0, 0, c)
    step("prep", 1, B_INDEX)
    for c in range(4):
        project(1, 0, c)
    step("rope", 0, 0)
    for c in range(4):
        project(2, 0, c)
    step("rope", 0, 1)
    for c in range(2):
        project(0, 1, c)
    step("QKT", 0, 0)
    for c in range(2, 4):
        project(0, 1, c)
    step("QKT", 0, 1)
    project(1, 1, 0)
    beside = {v: [] for v in range(16)}
    for v, (j, c) in enumerate([(1, 1), (1, 2), (1, 3), (2, 0), (2, 1), (2, 2), (2, 3)]):
        beside[v].append(lambda j=j, c=c: project(j, 1, c))
    beside[4].append(lambda: step("rope", 1, 0))
    beside[5].insert(0, lambda: step("QKT", 1, 0))
    beside[7].append(lambda: step("rope", 1, 1))
    beside[8].append(lambda: step("QKT", 1, 1))
    beside[9] += [lambda: step("AT", 0, 0), lambda: step("AT", 0, 1)]
    for kt in range(5):
        beside[11 + kt].append(lambda kt=kt: output(0, kt))
    beside[14].append(lambda: step("AT", 1, 0))
    step("S", 0)
    step("E", 0)
    step("S", 1)
    for v in range(16):
        if v < 15:
            step("E", v + 1)
        step("PT", v)
        for part in beside[v]:
            part()
        if v < 14:
            step("S", v + 2)
        if v >= 1:
            step("PV", v - 1)
            if v % 4 == 0:
                step("AO", v // 4 - 1)
    step("PV", 15)
    step("AO", 3)
    for kt in range(5, 8):
        output(0, kt)
    step("tail", 0, B_INDEX)
    step("AT", 1, 1)
    for kt in range(5):
        output(1, kt)
    step("prep", 0, B_INDEX + 1)
    for kt in range(5, 8):
        output(1, kt)
    step("tail", 1, B_INDEX)


def walk_latent(step):
    def project(i, t, c):
        step("X", i, t, c)
        if t == 1:
            step("R", C_X[i] + c, 1, 0)

    def output(t, kt):
        step("Oc", t, kt)
        if t == 1:
            step("R", C_WO + kt, 1, 0)

    def projects(i, t):
        for c in range(4):
            project(i, t, c)

    projects(0, 0)
    step("prep", 1, C_INDEX)
    projects(1, 0)
    projects(0, 1)
    step("LAT", 0)
    projects(2, 0)
    step("U", 0)
    projects(1, 1)
    step("LAT", 1)
    step("MT", 0)
    projects(2, 1)
    step("U", 1)
    step("R", C_U, 3, 0)
    projects(3, 0)
    step("MT", 1)
    beside = [(3, 1, c) for c in range(4)] + [(4, 0, c) for c in range(4)] + [(4, 1, c) for c in range(4)]
    step("MS", 0)
    step("ME", 0)
    step("MS", 1)
    for v in range(8):
        if v < 7:
            step("ME", v + 1)
        step("MPT", v)
        for _ in range(1 + v % 2):
            project(*beside.pop(0))
        if v < 6:
            step("MS", v + 2)
        if v == 7:
            step("RT", 0)
        if v >= 1:
            step("MPV", v - 1)
        if v == 4:
            step("MN", 0)
        if 2 <= v < 6:
            step("RROPE", (v - 2) // 2, v % 2)
    step("MPV", 7)
    step("gate", 0)
    step("MAT", 0)
    step("RT", 1)
    step("MN", 1)
    step("gate", 1)
    for hd in range(8):
        step("decay", hd)
    step("silu",)
    output(0, 0)
    step("RS", 0)
    step("RS", 1)
    for hd in range(8):
        step("RM", hd)
        if hd < 3:
            output(0, hd + 1)
        if hd == 3:
            step("MAT", 1)
        if hd in (5, 7):
            output(1, hd // 2 - 2)
        step("RPV", hd)
        if hd < 6:
            step("RS", hd + 2)
        if hd % 4 == 3:
            step("GN", hd // 4)
    for kt in range(2, 4):
        output(1, kt)
    step("RAT", 0)
    step("RAT", 1)
    for kt in range(4, 8):
        output(0, kt)
    step("tail", 0, C_INDEX)
    for kt in range(4, 7):
        output(1, kt)
    step("prep", 0, C_INDEX + 1)
    output(1, 7)
    step("tail", 1, C_INDEX)


def walk(eng, step):
    step("start",)
    step("prep", 0, 0)
    walk_phase(eng, MIX, lambda *a: step(*a, ph=MIX), 0)
    walk_phase(eng, FFN1, lambda *a: step(*a, ph=FFN1), 4)
    walk_attention(lambda *a: step(*a, ph=None))
    walk_phase(eng, FFN2, lambda *a: step(*a, ph=FFN2), 4)
    walk_phase(eng, FFN3, lambda *a: step(*a, ph=FFN3), 4)
    walk_latent(lambda *a: step(*a, ph=None))
    walk_phase(eng, FFN4, lambda *a: step(*a, ph=FFN4), 3)
    step("prep", 1, LAST)


def two_pi_parts():
    parts, rest = [], 2 * math.pi
    for _ in range(5):
        unit = 2.0 ** (math.floor(math.log2(rest)) - 6)
        parts.append(math.floor(rest / unit) * unit)
        rest -= parts[-1]
    return parts


def build(nc, x_in, stream, feats_in, consts_in, table_in, pos_in, posts_in, out):
    with ExitStack() as ctx:
        def sem(name):
            return ctx.enter_context(nc.semaphore(name))

        def rows2(name):
            return [sem(f"{name}{t}") for t in range(2)]

        at = [(nc.sbuf_base + 63) // 64 * 64]

        def place(name, shape, dt, offset=None):
            size = int(np.prod(shape[1:])) * (2 if dt == BF16 else 4)
            if offset is None:
                offset = at[0]
                at[0] += (size + 63) // 64 * 64
            assert offset + size <= nc.sbuf_usable_end, (name, offset + size)
            return nc.alloc_sbuf_tensor_at(name, shape, dt, offset=offset)

        raw = place("raw", [P, RAW * CHUNK], F32)
        w_high = place("w_high", [P, RING * CHUNK], F32R)
        w_low = place("w_low", [P, RING * CHUNK], F32R)
        xTh = [place(f"xTh{t}", [P, KT, P], F32R) for t in range(2)]
        xTl = [place(f"xTl{t}", [P, KT, P], F32R) for t in range(2)]
        h = [place(f"h{t}", [P, D], F32) for t in range(2)]
        post = place("post", [P, D], F32)
        junk = [place(f"junk{t}", [P, D], BF16) for t in range(2)]
        consts = place("consts", [P, CONSTS], F32)
        feats = place("feats", [P, FEATS], F32)
        table = place("table", [P, TAB], F32)
        stat = place("stat", [P, 64], F32)
        pos_i = place("pos_i", [P, 2], I32)
        trig = place("trig", [P, 8, 64], F32)
        decay_t = place("decay_t", [P, 8, 16], F32)
        mx = [place(f"mx{t}", [P, 16], F32) for t in range(2)]
        negm = [place(f"negm{t}", [P, 16], F32) for t in range(2)]
        lsum = [place(f"lsum{t}", [P, 16], F32) for t in range(2)]
        esink = [place(f"esink{t}", [P, 16], F32) for t in range(2)]
        lrec = [place(f"lrec{t}", [P, 16], F32) for t in range(2)]
        gn = [place(f"gn{i}", [P, 4, 8], F32) for i in range(2)]
        nsink = place("nsink", [P, 16], F32)
        actT_at = at[0]
        aTh = [place(f"aTh{t}", [P, 2, P], F32R) for t in range(2)]
        aTl = [place(f"aTl{t}", [P, 2, P], F32R) for t in range(2)]
        latTh = place("latTh", [P, 3, P], F32R, actT_at)
        latTl = place("latTl", [P, 3, P], F32R, actT_at + 3 * P * 4)
        union = at[0]

        hg = [place(f"hg{t}", [P, D], F32) for t in range(2)]
        gate = [place(f"gate{t}", [P, 256], F32) for t in range(2)]
        act = [place(f"act{t}", [P, 256], F32) for t in range(2)]
        cv = [place(f"cv{i}", [P, SEQ + 2], F32) for i in range(3)]
        yT = [place(f"yT{t}", [P, P], F32) for t in range(2)]

        at[0] = union
        qT = [place(f"qT{t}", [P, PAIRS, P], F32) for t in range(2)]
        qkv = [place(f"qkv{t}", [P, 1536], F32) for t in range(2)]
        kT = place("kT", [P, 2, SEQ], F32)
        x2h = [place(f"x2h{t}", [P, KT, P], F32R) for t in range(2)]
        x2l = [place(f"x2l{t}", [P, KT, P], F32R) for t in range(2)]
        sm = [place(f"sm{i}", [P, 2, SEQ], F32) for i in range(2)]
        pr = [place(f"pr{i}", [P, 2, SEQ], F32) for i in range(2)]
        prT = [place(f"prT{i}", [P, 4 * P], F32) for i in range(2)]
        rtmp = [place(f"rtmp{i}", [P, 12, ROT_HALF], F32) for i in range(4)]

        at[0] = union
        mqT = place("mqT", [QK, MLA_HEADS, SEQ], F32)
        rqT = place("rqT", [P, 4, SEQ], F32, union)
        rkT = place("rkT", [P, 4, SEQ], F32, union + 4 * SEQ * 4)
        mkT_at = at[0]
        mkT = place("mkT", [QK, MLA_HEADS, SEQ], F32)
        lat_at = at[0]
        lat = [place(f"lat{t}", [P, LATENT], F32) for t in range(2)]
        ttmp = [place(f"ttmp{i}", [P, 8, RHALF], F32, lat_at + i * 1024 if i < 3 else None) for i in range(4)]
        mq_at = at[0]
        mq = place("mq", [P, MLA_HEADS, QK], F32)
        mk = place("mk", [P, MLA_HEADS, QK], F32)
        mo = [place(f"mo{t}", [P, 512], F32, mq_at + t * MLA_HEADS * QK * 4) for t in range(2)]
        mv = [place(f"mv{t}", [P, 512], F32) for t in range(2)]
        rqk_both = place("rqk", [P, 2, 1024], F32)
        rqk = [rqk_both[:, t, :] for t in range(2)]
        rv = [place(f"rv{t}", [P, 512], F32) for t in range(2)]
        p_at = at[0]
        mp = [place(f"mp{i}", [P, 2, SEQ], F32) for i in range(2)]
        sd = [place(f"sd{i}", [P, 2, SEQ], F32, p_at + i * 2 * SEQ * 4) for i in range(2)]
        latf = place("latf", [P, 3, P], F32, p_at)
        mpT_at = at[0]
        mpT = [place(f"mpT{i}", [P, 4 * P], F32) for i in range(2)]
        dm_at = [lat_at, lat_at + 1536] + [mkT_at + 1536 * i for i in range(5)] + [mpT_at + 2048]
        dm = [place(f"dm{i}", [P, 3 * P], F32, dm_at[i]) for i in range(8)]
        dtmp = place("dtmp", [P, P], F32)

        ident = consts[:, C_ID:C_ID + P]
        rope1 = consts[:, C_ROPE:C_ROPE + 32].rearrange("p (t c f) -> p t c f", t=2, c=2)
        mask = consts[:, C_MASK:C_MASK + SEQ]
        inv_freq = consts[:, C_INV:C_INV + 32]
        rel = consts[:, C_REL:C_REL + 4 * P]
        ss = [stat[:, 50 + 2 * t:52 + 2 * t] for t in range(2)]
        ms = [stat[:, 2 + t:3 + t] for t in range(2)]
        rr = [stat[:, 4 + t:5 + t] for t in range(2)]
        pss = [stat[:, 54 + 2 * t:56 + 2 * t] for t in range(2)]
        pms = [stat[:, 8 + t:9 + t] for t in range(2)]
        prr = [stat[:, 10 + t:11 + t] for t in range(2)]
        lss = [stat[:, 12 + 2 * t:14 + 2 * t] for t in range(2)]
        lms = [stat[:, 16 + 2 * t:18 + 2 * t] for t in range(2)]
        lrr = [stat[:, 20 + 2 * t:22 + 2 * t] for t in range(2)]
        half_neg = stat[:, 24:32]
        one_neg = stat[:, 32:48]
        pos_f = stat[:, 48:50]
        ang, kang, tang, cang, cosT, sinT = (trig[:, i, :] for i in range(6))
        cos2 = cosT.rearrange("p (t f) -> p t f", t=2)
        sin2 = sinT.rearrange("p (t f) -> p t f", t=2)
        lg_r2, lg_ax, lg_e, lg_s, lg_z, lg_p, lg = (decay_t[:, i, :] for i in range(7))

        pD = [ctx.enter_context(nc.psum_tensor(f"pD{t}", [P, D], F32)) for t in range(2)]
        pG = [ctx.enter_context(nc.psum_tensor(f"pG{t}", [P, 512], F32)) for t in range(2)]
        pT = [ctx.enter_context(nc.psum_tensor(f"pT{t}", [P, 512], F32)) for t in range(2)]

        w_loaded = [sem(f"w_loaded{i}") for i in range(RAW)]
        w_high_done = sem("w_high_done")
        w_split = sem("w_split")
        w_freed = sem("w_freed")
        x_loaded = rows2("x_loaded")
        feats_loaded, ident_loaded, consts_loaded = sem("feats_loaded"), sem("ident_loaded"), sem("consts_loaded")
        table_loaded, pos_loaded = sem("table_loaded"), sem("pos_loaded")
        post_loaded = sem("post_loaded")
        out_ready, out_stored = rows2("out_ready"), sem("out_stored")
        h_ready, ss_ready, r_ready = (rows2(n) for n in ("h_ready", "ss_ready", "r_ready"))
        pss_ready, pr_ready = (rows2(n) for n in ("pss_ready", "pr_ready"))
        hT_psum, hg_ready, xh_ready, xT_ready = (rows2(n) for n in ("hT_psum", "hg_ready", "xh_ready", "xT_ready"))
        g_done0, d_done0 = sem("g_done0"), sem("d_done0")
        d_half = rows2("d_half")
        gate_ready, act_ready, actT_psum = (rows2(n) for n in ("gate_ready", "act_ready", "actT_psum"))
        cuT_ready, conv_done, ah_ready, aT_ready = (rows2(n) for n in ("cuT_ready", "conv_done", "ah_ready", "aT_ready"))
        halo_zero = sem("halo_zero")
        q_done0 = sem("q_done0")
        qkv_ready, rope_done, qkT_psum = rows2("qkv_ready"), sem("rope_done"), rows2("qkT_psum")
        kqT_act, kqT_dve = rows2("kqT_act"), rows2("kqT_dve")
        s_done, sm_ready, p_ready = sem("s_done"), sem("sm_ready"), sem("p_ready")
        pT_psum, pT_ready, pv_done = sem("pT_psum"), sem("pT_ready"), sem("pv_done")
        es_arg, es_ready, ao_ready = (rows2(n) for n in ("es_arg", "es_ready", "ao_ready"))
        aoT_psum, aoh_ready, aoT_ready = (rows2(n) for n in ("aoT_psum", "aoh_ready", "aoT_ready"))
        nsink_ready = sem("nsink_ready")
        x_done0, u_done0 = sem("x_done0"), sem("u_done0")
        x_out, lat_ss, lr_ready = (rows2(n) for n in ("x_out", "lat_ss", "lr_ready"))
        latT_psum, latf_ready, lath_ready, latT_ready = (rows2(n) for n in ("latT_psum", "latf_ready", "lath_ready", "latT_ready"))
        u_out, mqk_ready, mT_psum = (rows2(n) for n in ("u_out", "mqk_ready", "mT_psum"))
        mqT_ready, mkT_ready = rows2("mqT_ready"), rows2("mkT_ready")
        ms_psum, mmax_ready, mp_ready = sem("ms_psum"), sem("mmax_ready"), sem("mp_ready")
        mpT_psum, mpT_ready, mpv_done = sem("mpT_psum"), sem("mpT_ready"), sem("mpv_done")
        mo_ready = rows2("mo_ready")
        rrope_done = rows2("rrope_done")
        rT_psum, rqT_ready, rkT_ready = rows2("rT_psum"), rows2("rqT_ready"), rows2("rkT_ready")
        dm_arg, dm_ready = sem("dm_arg"), sem("dm_ready")
        rs_psum, sd_ready, rpv_done = sem("rs_psum"), sem("sd_ready"), sem("rpv_done")
        rgate, silu_ready = rows2("rgate"), sem("silu_ready")
        gn_var, gn_r, ro_ready = sem("gn_var"), sem("gn_r"), sem("ro_ready")
        catT_psum, cath_ready, catT_ready = (rows2(n) for n in ("catT_psum", "cath_ready", "catT_ready"))
        trig_ready, sincos_ready = sem("trig_ready"), sem("sincos_ready")
        pool_chain, ve_chain = sem("pool_chain"), sem("ve_chain")
        ax_ready, e_ready, lg_ready = sem("ax_ready"), sem("e_ready"), sem("lg_ready")
        pows_ready = sem("pows_ready")

        def slot(c):
            return (c + 1) % RING * CHUNK

        def xT_base(p):
            return 2 * p + (2 if p > B_INDEX else 0)

        def freed_by(ph, b, out_part):
            return ph.d_chunk(b) + ph.kd if out_part else ph.g_chunk(b) + ph.cg

        def branch_done(eng, t, k, half):
            if half == 0:
                eng.wait_ge(d_half[t], k + 1)
            elif t == 0:
                eng.wait_ge(d_done0, k + 1)
            else:
                eng.wait_ge(w_freed, [FFN1.first_chunk, B_FIRST, FFN2.first_chunk, FFN3.first_chunk,
                                      C_FIRST, FFN4.first_chunk, N_CHUNKS][k])

        def turned_bank(v):
            return pT[1][:] if v % 2 else pD[v // 8][:, 0:512]

        def ao_bank(t, half):
            return ((pD[0][:, 0:512], pD[0][:, 512:1024]), (pG[1][:], pT[0][:]))[t][half]

        def proj_done(eng, j, t):
            if t == 0:
                eng.wait_ge(q_done0, j + 1)
            else:
                eng.wait_ge(w_freed, B_FIRST + 4 * (j + 1))

        def x_product(eng, i, t):
            if t == 0:
                eng.wait_ge(x_done0, i + 1)
            else:
                eng.wait_ge(w_freed, C_X[i] + 4)

        block = ctx.enter_context(nc.Block())

        @block.sync
        def _(sp):
            sp.dma_start(h[0][:], x_in[0:P, :]).then_inc(x_loaded[0], 16)
            sp.dma_start(ident, consts_in[:, C_ID:C_ID + P]).then_inc(ident_loaded, 16)
            sp.dma_start(feats[:], feats_in).then_inc(feats_loaded, 16)
            for c in range(RAW):
                sp.dma_start(raw[:, c * CHUNK:(c + 1) * CHUNK], stream[c]).then_inc(w_loaded[c], 16)
            sp.dma_start(h[1][:], x_in[P:2 * P, :]).then_inc(x_loaded[1], 16)
            turns = N_CHUNKS // RAW
            with sp.Fori(1, turns) as turn:
                for i in range(RAW):
                    sp.wait_ge(w_split, turn * RAW + (i - RAW + 1))
                    sp.dma_start(raw[:, i * CHUNK:(i + 1) * CHUNK],
                                 stream[bass.ds(turn * RAW + i, 1)].rearrange("o p n -> p (o n)")
                                 ).then_inc(w_loaded[i], 16)
            for c in range(turns * RAW, N_CHUNKS):
                sp.wait_ge(w_split, c - RAW + 1)
                i = c % RAW
                sp.dma_start(raw[:, i * CHUNK:(i + 1) * CHUNK], stream[c]).then_inc(w_loaded[i], 16)
            for t in range(2):
                for half in range(2):
                    sp.wait_ge(out_ready[t], half + 1)
                    sp.dma_start(out[P * t:P * (t + 1), 512 * half:512 * half + 512],
                                 hg[t][:, 512 * half:512 * half + 512]).then_inc(out_stored, 16)
            sp.wait_ge(out_stored, 64)

        @block.gpsimd
        def _(pool):
            links = [0]

            def link(ins):
                links[0] += 1
                ins.then_inc(pool_chain, 1)
                pool.wait_ge(pool_chain, links[0])

            def start(ph):
                pool.memset(half_neg, -0.5).then_inc(pows_ready, 1)
                pool.memset(one_neg, -1.0).then_inc(pows_ready, 1)
                pool.wait_ge(w_loaded[0], 16)
                pool.dma_start(table[:], table_in).then_inc(table_loaded, 16)
                pool.dma_start(consts[:, P:CONSTS], consts_in[:, P:CONSTS]).then_inc(consts_loaded, 16)
                pool.dma_start(pos_i[:], pos_in).then_inc(pos_loaded, 16)
                pool.dma_start(post[:], posts_in[0].partition_broadcast(P)).then_inc(post_loaded, 16)
                for i in range(3):
                    pool.memset(cv[i][:, 0:2], 0.0).then_inc(halo_zero, 1)
                pool.wait_ge(pows_ready, 2)

            def tables():
                pool.wait_ge(pos_loaded, 16)
                pool.wait_ge(consts_loaded, 16)
                link(pool.tensor_copy(pos_f, pos_i[:]))
                for t in range(2):
                    link(pool.tensor_scalar(ang[:, 32 * t:32 * t + 32], inv_freq, pos_f[:, t:t + 1], None, ALU.mult))
                magic = 1.5 * 2.0 ** 23
                for unit in (4096.0, 1.0):
                    link(pool.tensor_scalar(kang, ang, 1.0 / (unit * 2 * math.pi), magic, ALU.mult, ALU.add))
                    link(pool.tensor_scalar(kang, kang, magic, None, ALU.subtract))
                    for part in two_pi_parts():
                        link(pool.tensor_scalar(tang, kang, -part * unit, None, ALU.mult))
                        link(pool.tensor_tensor(ang, ang, tang, ALU.add))
                link(pool.tensor_scalar(cang, ang, math.pi / 2, None, ALU.add))
                link(pool.tensor_scalar(tang, cang, math.pi, -2 * math.pi, ALU.is_gt, ALU.mult))
                link(pool.tensor_tensor(cang, cang, tang, ALU.add))
                link(pool.tensor_scalar(cang, cang, 3.1415925, -3.1415925, ALU.min, ALU.max))
                pool.tensor_scalar(ang, ang, 3.1415925, -3.1415925, ALU.min, ALU.max).then_inc(trig_ready, 1)
                pool.wait_ge(table_loaded, 16)
                dec = table[:, T_DECAY:T_DECAY + 16]
                link(pool.tensor_scalar(lg_r2, dec, -1.0, 0.0, ALU.mult, ALU.max))
                link(pool.tensor_scalar(lg_ax, dec, 0.0, None, ALU.max))
                pool.tensor_tensor(lg_ax, lg_ax, lg_r2, ALU.add).then_inc(ax_ready, 1)

            def log_decays():
                pool.wait_ge(e_ready, 1)
                link(pool.tensor_scalar(lg_s, lg_e, 2.0, None, ALU.add))
                link(pool.tensor_tensor(lg_s, lg_s, one_neg, ALU.pow))
                link(pool.tensor_tensor(lg_s, lg_s, lg_e, ALU.mult))
                link(pool.tensor_tensor(lg_z, lg_s, lg_s, ALU.mult))
                link(pool.tensor_scalar(lg_p, lg_z, 1.0 / 17, 1.0 / 15, ALU.mult, ALU.add))
                for n in (13, 11, 9, 7, 5, 3, 1):
                    link(pool.tensor_tensor(lg_p, lg_p, lg_z, ALU.mult))
                    link(pool.tensor_scalar(lg_p, lg_p, 1.0 / n, None, ALU.add))
                link(pool.tensor_tensor(lg_p, lg_p, lg_s, ALU.mult))
                link(pool.tensor_scalar(lg_p, lg_p, 2.0, None, ALU.mult))
                link(pool.tensor_tensor(lg_p, lg_p, lg_r2, ALU.add))
                pool.tensor_scalar(lg, lg_p, -1.0, None, ALU.mult).then_inc(lg_ready, 1)

            def prep(t, p, ph):
                pool.wait_ge(ss_ready[t], 2 * (p + 1))
                link(pool.tensor_scalar(ms[t], ss[t][:, 0:1], ss[t][:, 1:2], EPS, ALU.add, ALU.add))
                pool.tensor_tensor(rr[t], ms[t], half_neg[:, 0:1], ALU.pow).then_inc(r_ready[t], 1)
                if t == 1 and p == 0:
                    tables()
                if t == 1 and p == B_INDEX + 1:
                    log_decays()

            def tail(t, k, ph):
                if k < POST_NORMS:
                    pool.wait_ge(pss_ready[t], 2 * (k + 1))
                    link(pool.tensor_scalar(pms[t], pss[t][:, 0:1], pss[t][:, 1:2], EPS, ALU.add, ALU.add))
                    pool.tensor_tensor(prr[t], pms[t], half_neg[:, 0:1], ALU.pow).then_inc(pr_ready[t], 1)
                    if t == 1:
                        pool.wait_ge(h_ready[0], 2 * (k + 1))
                        pool.wait_ge(h_ready[1], 2 * (k + 1))
                        pool.dma_start(post[:], posts_in[k + 1].partition_broadcast(P)).then_inc(post_loaded, 16)

            def LAT(t, ph):
                pool.wait_ge(lat_ss[t], 2)
                link(pool.tensor_scalar(lms[t][:, 0:1], lss[t][:, 0:1], 1.0 / Q_RANK, EPS, ALU.mult, ALU.add))
                link(pool.tensor_scalar(lms[t][:, 1:2], lss[t][:, 1:2], 1.0 / KV_RANK, EPS, ALU.mult, ALU.add))
                pool.tensor_tensor(lrr[t], lms[t], half_neg[:, 0:2], ALU.pow).then_inc(lr_ready[t], 1)

            def decay(hd, ph):
                d, f, b = dm[hd], lg[:, hd:hd + 1], lg[:, 8 + hd:9 + hd]
                if hd == 0:
                    pool.wait_ge(lg_ready, 1)
                    pool.wait_ge(rrope_done[1], 2)
                if hd == 2:
                    pool.wait_ge(ms_psum, 8)
                if hd == 7:
                    pool.wait_ge(mpv_done, 8)
                if hd > 0:
                    pool.wait_ge(dm_arg, hd)
                link(pool.tensor_scalar(d[:, P:3 * P], rel[:, 0:2 * P], f, None, ALU.mult))
                link(pool.tensor_scalar(d[:, 0:P], rel[:, 3 * P:4 * P], b, None, ALU.mult))
                link(pool.tensor_scalar(dtmp[:], rel[:, 2 * P:3 * P], b, None, ALU.mult))
                pool.tensor_tensor(d[:, P:2 * P], d[:, P:2 * P], dtmp[:], ALU.add).then_inc(dm_arg, 1)

            def GN(part, ph):
                g = gn[part]
                pool.wait_ge(gn_var, part + 1)
                link(pool.tensor_scalar(g[:, 2, :], g[:, 1, :], 1.0 / HD, EPS, ALU.mult, ALU.add))
                pool.tensor_tensor(g[:, 3, :], g[:, 2, :], half_neg, ALU.pow).then_inc(gn_r, 1)

            parts = {f.__name__: f for f in (start, prep, tail, LAT, decay, GN)}
            in_loop = ("G", "D", "T", "R")

            def step(name, *args, ph=None):
                if name in parts:
                    parts[name](*args, ph)
            walk(NoLoop(), lambda name, *a, ph=None: None if name in in_loop else step(name, *a, ph=ph))

        @block.scalar
        def _(sc):
            def split_high(c, static, shift):
                sc.wait_ge(w_loaded[static % RAW], 16 * (static // RAW + 1) + shift * (16 * RING // RAW))
                if static >= RING:
                    sc.wait_ge(w_freed, c - RING + 1)
                sc.activation(w_high[:, slot(static):slot(static) + CHUNK],
                              raw[:, static % RAW * CHUNK:(static % RAW + 1) * CHUNK], ACT.Copy).then_inc(w_high_done, 1)

            def refill(first, n, shift, ph):
                for c in range(first + RING, first + RING + n):
                    if c < N_CHUNKS:
                        split_high(c + shift * RING, c, shift)

            def start(ph):
                sc.preload_act_table(ACT.Silu)

            def fill(first, n, ph):
                for c in range(first, first + n):
                    split_high(c, c, 0)

            def prep(t, p, ph):
                def square(half):
                    if p == 0:
                        sc.wait_ge(x_loaded[t], 16)
                    else:
                        sc.wait_ge(h_ready[t], 2 * (p - 1) + half + 1)
                    cols = slice(512 * half, 512 * half + 512)
                    sc.activation(junk[t][:, cols], h[t][:, cols], ACT.Square, scale=D ** -0.5,
                                  accum_out=ss[t][:, half:half + 1]).then_inc(ss_ready[t], 1)

                square(0)
                if p < LAST:
                    n = xT_base(p)
                    for high in [xTh] + ([x2h] if p == B_INDEX else []):
                        for half in range(2):
                            n += 1
                            sc.wait_ge(hg_ready[t], n)
                            sc.activation(high[t][:, 4 * half:4 * half + 4, :].rearrange("p k r -> p (k r)"),
                                          hg[t][:, 512 * half:512 * half + 512], ACT.Copy).then_inc(xh_ready[t], 1)
                            if n == xT_base(p) + 2:
                                square(1)
                else:
                    square(1)

            def tail(t, k, ph):
                if k < POST_NORMS:
                    for half in range(2):
                        branch_done(sc, t, k, half)
                        cols = slice(512 * half, 512 * half + 512)
                        sc.activation(junk[t][:, cols], pD[t][:, cols], ACT.Square, scale=D ** -0.5,
                                      accum_out=pss[t][:, half:half + 1]).then_inc(pss_ready[t], 1)

            def G(t, b, shift, ph):
                n = ph.first_block + b + 1 + shift * (RING // (ph.cg + ph.kd))
                if t == 1:
                    sc.wait_ge(w_freed, freed_by(ph, b, False) + shift * RING)
                else:
                    sc.wait_ge(g_done0, n)
                if b == 0:
                    sc.wait_ge(r_ready[t], ph.index + 1)
                sc.activation(gate[t][:], pG[t][:, 0:256], ACT.Copy if ph.mixer else ACT.Silu,
                              scale=rr[t]).then_inc(gate_ready[t], 1)

            def T(t, b, shift, ph):
                n = ph.first_block + b + 1 + shift * (RING // (ph.cg + ph.kd))
                sc.wait_ge(actT_psum[t], n)
                if ph.mixer:
                    if b < 3 and t == 0:
                        sc.wait_ge(halo_zero, b + 1)
                    if t == 0 and b >= 3:
                        sc.wait_ge(conv_done[1], 4 * (b - 2))
                    sc.activation(cv[b % 3][:, 2 + P * t:2 + P * (t + 1)], pT[t][:, P:2 * P], ACT.Copy).then_inc(cuT_ready[t], 1)
                    sc.wait_ge(conv_done[t], 4 * (b + 1))
                    sc.activation(aTh[t][:, 0, :], yT[t][:], ACT.Copy).then_inc(ah_ready[t], 1)
                else:
                    sc.activation(aTh[t][:].rearrange("p k r -> p (k r)"), pT[t][:, 0:256], ACT.Copy).then_inc(ah_ready[t], 1)
                if ph is FFN1 and t == 0 and b == 0:
                    sc.wait_ge(trig_ready, 1)
                    sc.activation(sinT, ang, ACT.Sin).then_inc(sincos_ready, 1)
                    sc.activation(cosT, cang, ACT.Sin).then_inc(sincos_ready, 1)

            def proj(j, t, c, ph):
                if c == 3:
                    proj_done(sc, j, t)
                    if j == 0:
                        sc.wait_ge(r_ready[t], B_INDEX + 1)
                    src = pG[t][:] if j == 2 else pD[t][:, 512 * j:512 * j + 512]
                    sc.activation(qkv[t][:, 512 * j:512 * j + 512], src, ACT.Copy, scale=rr[t]).then_inc(qkv_ready[t], 1)

            def QKT(t, part, ph):
                sc.wait_ge(qkT_psum[t], 2 * part + 1)
                if part == 0:
                    sc.activation(kT[:, :, P * t:P * (t + 1)], pD[t][:, 0:256].rearrange("p (a r) -> p a r", a=2),
                                  ACT.Copy).then_inc(kqT_act[t], 1)
                else:
                    sc.activation(qT[t][:, 4:8, :].rearrange("p a r -> p (a r)"), pG[t][:], ACT.Copy).then_inc(kqT_act[t], 1)

            def E(v, ph):
                t, m, half = v // 8, v % 8 // 2, v % 2
                keys = slice(P * (1 - t), SEQ)
                sc.wait_ge(sm_ready, v + 1)
                if v >= 2:
                    sc.wait_ge(pT_psum, v - 1)
                for x in range(2):
                    col = 2 * (2 * m + x) + half
                    sc.activation(pr[v % 2][:, x, keys], sm[v % 2][:, x, keys], ACT.Exp, bias=negm[t][:, col:col + 1],
                                  accum_out=lsum[t][:, col:col + 1]).then_inc(p_ready, 1)

            def AO(quarter, ph):
                t, half = quarter // 2, quarter % 2
                sc.wait_ge(es_arg[t], half + 1)
                cols = slice(8 * half, 8 * half + 8)
                sc.activation(esink[t][:, cols], esink[t][:, cols], ACT.Exp).then_inc(es_ready[t], 1)
                if t == 0 and half == 0:
                    sc.wait_ge(ax_ready, 1)
                    sc.activation(lg_e, lg_ax, ACT.Exp, scale=-1.0).then_inc(e_ready, 1)

            def AT(t, half, ph):
                sc.wait_ge(aoT_psum[t], half + 1)
                sc.activation(xTh[t][:, 4 * half:4 * half + 4, :].rearrange("p k r -> p (k r)"),
                              ao_bank(t, half), ACT.Copy).then_inc(aoh_ready[t], 1)

            def X(i, t, c, ph):
                if c == 3 and i < 4:
                    x_product(sc, i, t)
                    if i == 0:
                        sc.wait_ge(r_ready[t], C_INDEX + 1)
                    dst = [lat[t][:], rqk[t][:, 0:512], rqk[t][:, 512:1024], rv[t][:]][i]
                    sc.activation(dst, pD[t][:, 0:LATENT if i == 0 else 512], ACT.Copy, scale=rr[t]).then_inc(x_out[t], 1)

            def LAT(t, ph):
                sc.wait_ge(x_out[t], 1)
                sc.activation(junk[t][:, 0:Q_RANK], lat[t][:, 0:Q_RANK], ACT.Square, accum_out=lss[t][:, 0:1]).then_inc(lat_ss[t], 1)
                sc.activation(junk[t][:, Q_RANK:Q_RANK + KV_RANK], lat[t][:, Q_RANK:Q_RANK + KV_RANK], ACT.Square,
                              accum_out=lss[t][:, 1:2]).then_inc(lat_ss[t], 1)
                sc.wait_ge(latf_ready[t], 1)
                if t == 1:
                    sc.wait_ge(u_done0, 1)
                sc.activation(latTh[:], latf[:], ACT.Copy).then_inc(lath_ready[t], 1)

            def U(t, ph):
                if t == 1:
                    sc.wait_ge(w_freed, C_U + 3)
                    sc.wait_ge(mT_psum[0], 2)
                else:
                    sc.wait_ge(u_done0, 1)
                sc.wait_ge(lr_ready[t], 1)
                for half in range(2):
                    sc.activation(mq[:, 4 * half:4 * half + 4, :], (pG, pT)[half][0][:, 0:384].rearrange("p (a f) -> p a f", a=4),
                                  ACT.Copy, scale=lrr[t][:, 0:1]).then_inc(u_out[t], 1)
                sc.activation(mk[:, :, 0:NOPE], pG[1][:].rearrange("p (a f) -> p a f", a=8), ACT.Copy,
                              scale=lrr[t][:, 1:2]).then_inc(u_out[t], 1)
                sc.activation(mv[t][:], pT[1][:], ACT.Copy, scale=lrr[t][:, 1:2]).then_inc(u_out[t], 1)

            def MT(t, ph):
                sc.wait_ge(mT_psum[t], 1)
                for half in range(2):
                    sc.activation(mqT[:, 4 * half:4 * half + 4, P * t:P * (t + 1)],
                                  (pG, pT)[half][0][0:QK, :].rearrange("p (a r) -> p a r", a=4), ACT.Copy).then_inc(mqT_ready[t], 1)

            def ME(v, ph):
                t, j = v // 4, v % 4
                sc.wait_ge(mmax_ready, v + 1)
                if v >= 2:
                    sc.wait_ge(mpT_psum, v - 1)
                for x in range(2):
                    hd = 2 * j + x
                    sc.activation(mp[v % 2][:, x, :], pG[v % 2][:, SEQ * x:SEQ * (x + 1)], ACT.Exp, bias=negm[t][:, hd:hd + 1],
                                  scale=MLA_SCALE, accum_out=lsum[t][:, hd:hd + 1]).then_inc(mp_ready, 1)

            def RT(t, ph):
                sc.wait_ge(rT_psum[t], 1)
                sc.activation(rqT[:, :, P * t:P * (t + 1)], pG[0][:].rearrange("p (a r) -> p a r", a=4),
                              ACT.Copy).then_inc(rqT_ready[t], 1)

            def decay(hd, ph):
                sc.wait_ge(dm_arg, hd + 1)
                sc.activation(dm[hd][:], dm[hd][:], ACT.Exp).then_inc(dm_ready, 1)

            def gate_r(t, ph):
                x_product(sc, 4, t)
                sc.wait_ge(rT_psum[t], 2)
                sc.activation(rqk[t][:, 512:1024], pD[t][:, 0:512], ACT.Copy, scale=rr[t]).then_inc(rgate[t], 1)

            def silu(ph):
                for t in range(2):
                    sc.wait_ge(rgate[t], 1)
                sc.activation(rqk_both[:, :, 512:1024], rqk_both[:, :, 512:1024], ACT.Silu).then_inc(silu_ready, 1)

            def MAT(t, ph):
                sc.wait_ge(catT_psum[t], 1)
                sc.activation(xTh[t][:, 0:4, :].rearrange("p k r -> p (k r)"), pD[t][:, 512:1024], ACT.Copy).then_inc(cath_ready[t], 1)

            def RAT(t, ph):
                sc.wait_ge(catT_psum[t], 2)
                sc.activation(xTh[t][:, 4:8, :].rearrange("p k r -> p (k r)"), pG[t][:], ACT.Copy).then_inc(cath_ready[t], 1)

            parts = dict(start=start, fill=fill, R=refill, prep=prep, tail=tail, G=G, T=T, proj=proj, QKT=QKT, E=E, AO=AO, AT=AT,
                         X=X, LAT=LAT, U=U, MT=MT, ME=ME, RT=RT, decay=decay, gate=gate_r, silu=silu, MAT=MAT, RAT=RAT)
            walk(sc, lambda name, *a, ph=None: parts[name](*a, ph) if name in parts else None)

        @block.vector
        def _(ve):
            links = [0]

            def chain(ins):
                links[0] += 1
                return ins.then_inc(ve_chain, 1)

            def joined():
                ve.wait_ge(ve_chain, links[0])

            def split_low(c, static):
                ve.wait_ge(w_high_done, c + 1)
                ve.tensor_tensor(w_low[:, slot(static):slot(static) + CHUNK],
                                 raw[:, static % RAW * CHUNK:(static % RAW + 1) * CHUNK],
                                 w_high[:, slot(static):slot(static) + CHUNK].bitcast(F32), ALU.subtract).then_inc(w_split, 1)

            def refill(first, n, shift, ph):
                for c in range(first + RING, first + RING + n):
                    if c < N_CHUNKS:
                        split_low(c + shift * RING, c)

            def start(ph):
                ve.wait_ge(feats_loaded, 16)

            def sinks():
                ve.wait_ge(consts_loaded, 16)
                ve.wait_ge(table_loaded, 16)
                ve.tensor_scalar(nsink[:], table[:, T_SINK:T_SINK + 16], -1.0, None, ALU.mult).then_inc(nsink_ready, 1)

            def fill(first, n, ph):
                for c in range(first, first + n):
                    split_low(c, c)

            def prep(t, p, ph):
                if p == LAST:
                    final(t)
                    return
                if p == 1 and t == 0:
                    sinks()
                n = xT_base(p)
                sets = [(GAIN[p], xTh, xTl)] + ([(GAIN["q"], x2h, x2l)] if p == B_INDEX else [])
                for col, high, low in sets:
                    if n > xT_base(p):
                        ve.wait_ge(xT_ready[t], n)
                    for half in range(2):
                        ve.wait_ge(hT_psum[t], 2 * p + half + 1)
                        g = feats[:, col + 4 * half:col + 4 * half + 4].unsqueeze(2).broadcast_to([P, 4, P])
                        ve.tensor_tensor(hg[t][:, 512 * half:512 * half + 512].rearrange("p (k r) -> p k r", k=4),
                                         (pG, pT)[half][t][:].rearrange("p (k r) -> p k r", k=4), g,
                                         ALU.mult).then_inc(hg_ready[t], 1)
                    for half in range(2):
                        n += 1
                        ve.wait_ge(xh_ready[t], n)
                        ve.tensor_tensor(low[t][:, 4 * half:4 * half + 4, :].rearrange("p k r -> p (k r)"),
                                         hg[t][:, 512 * half:512 * half + 512],
                                         high[t][:, 4 * half:4 * half + 4, :].rearrange("p k r -> p (k r)").bitcast(F32),
                                         ALU.subtract).then_inc(xT_ready[t], 1)

            def final(t):
                ve.wait_ge(r_ready[t], LAST + 1)
                ve.wait_ge(post_loaded, 16 * (POST_NORMS + 1))
                for half in range(2):
                    cols = slice(512 * half, 512 * half + 512)
                    ve.scalar_tensor_tensor(hg[t][:, cols], h[t][:, cols], rr[t], post[:, cols], ALU.mult, ALU.mult).then_inc(out_ready[t], 1)

            def tail(t, k, ph):
                halves = [slice(0, 512), slice(512, 1024)]
                if k < POST_NORMS:
                    ve.wait_ge(post_loaded, 16 * (k + 1))
                    for half, cols in enumerate(halves):
                        ve.wait_ge(pss_ready[t], 2 * k + half + 1)
                        chain(ve.tensor_tensor(hg[t][:, cols], pD[t][:, cols], post[:, cols], ALU.mult))
                    joined()
                    ve.wait_ge(pr_ready[t], k + 1)
                    for cols in halves:
                        ve.scalar_tensor_tensor(h[t][:, cols], hg[t][:, cols], prr[t], h[t][:, cols],
                                                ALU.mult, ALU.add).then_inc(h_ready[t], 1)
                else:
                    for half, cols in enumerate(halves):
                        branch_done(ve, t, k, half)
                        ve.scalar_tensor_tensor(h[t][:, cols], pD[t][:, cols], 1.0 if k == C_INDEX else 0.5, h[t][:, cols],
                                                ALU.mult, ALU.add).then_inc(h_ready[t], 1)

            def G(t, b, shift, ph):
                n = ph.first_block + b + 1 + shift * (RING // (ph.cg + ph.kd))
                ve.wait_ge(gate_ready[t], n)
                if ph.mixer:
                    ve.scalar_tensor_tensor(act[t][:, 0:P], pG[t][:, 256:384], rr[t], gate[t][:, P:2 * P],
                                            ALU.mult, ALU.mult).then_inc(act_ready[t], 1)
                else:
                    ve.scalar_tensor_tensor(act[t][:], pG[t][:, 256:512], rr[t], gate[t][:],
                                            ALU.mult, ALU.mult).then_inc(act_ready[t], 1)

            def T(t, b, shift, ph):
                n = ph.first_block + b + 1 + shift * (RING // (ph.cg + ph.kd))
                if ph.mixer:
                    ve.wait_ge(cuT_ready[t], b + 1)
                    taps = [feats[:, CONV + 3 * b + w:CONV + 3 * b + w + 1] for w in range(3)]
                    src = [cv[b % 3][:, P * t + w:P * t + w + P] for w in range(3)]
                    done = 4 * b
                    ve.tensor_scalar(yT[t][:], src[0], taps[0], None, ALU.mult).then_inc(conv_done[t], 1)
                    for w in (1, 2):
                        ve.wait_ge(conv_done[t], done + w)
                        ve.scalar_tensor_tensor(yT[t][:], src[w], taps[w], yT[t][:], ALU.mult, ALU.add).then_inc(conv_done[t], 1)
                    ve.wait_ge(conv_done[t], done + 3)
                    ve.tensor_tensor(yT[t][:], pT[t][:, 0:P], yT[t][:], ALU.mult).then_inc(conv_done[t], 1)
                    ve.wait_ge(ah_ready[t], n)
                    ve.tensor_tensor(aTl[t][:, 0, :], yT[t][:], aTh[t][:, 0, :].bitcast(F32), ALU.subtract).then_inc(aT_ready[t], 1)
                else:
                    ve.wait_ge(ah_ready[t], n)
                    ve.tensor_tensor(aTl[t][:].rearrange("p k r -> p (k r)"), pT[t][:, 0:256],
                                     aTh[t][:].rearrange("p k r -> p (k r)").bitcast(F32), ALU.subtract).then_inc(aT_ready[t], 1)

            def rope(t, part, ph):
                ve.wait_ge(qkv_ready[t], 2 + part)
                if part or t:
                    ve.wait_ge(rope_done, 2 * (2 * t + part))
                n = 8 if part else 12
                qk = qkv[t][:, (1024 if part else 256):(1536 if part else 1024)].rearrange("p (a f) -> p a f", f=HD)
                a, b = qk[:, :, 0:ROT_HALF], qk[:, :, ROT_HALF:2 * ROT_HALF]
                co, si = (rope1[:, t, i, :].unsqueeze(1).broadcast_to([P, n, ROT_HALF]) for i in range(2))
                tmp = [x[:, 0:n, :] for x in rtmp]
                for i, (u, w) in enumerate(((a, co), (b, si), (b, co), (a, si))):
                    chain(ve.tensor_tensor(tmp[i], u, w, ALU.mult))
                joined()
                ve.tensor_tensor(a, tmp[0], tmp[1], ALU.subtract).then_inc(rope_done, 1)
                ve.tensor_tensor(b, tmp[2], tmp[3], ALU.add).then_inc(rope_done, 1)

            def QKT(t, part, ph):
                if part == 0:
                    ve.wait_ge(qkT_psum[t], 2)
                    ve.tensor_copy(qT[t][:, 0:4, :].rearrange("p a r -> p (a r)"), pD[t][:, 512:1024]).then_inc(kqT_dve[t], 1)

            def S(v, ph):
                t, m, half = v // 8, v % 8 // 2, v % 2
                keys = slice(P * (1 - t), SEQ)
                nk = P * (1 + t)
                bank = (pT, pG)[half][0]
                ve.wait_ge(s_done, v + 1)
                if v >= 2:
                    ve.wait_ge(p_ready, 2 * (v - 1))
                for x in range(2):
                    col = 2 * (2 * m + x) + half
                    chain(ve.tensor_tensor_reduce(sm[v % 2][:, x, keys], bank[:, SEQ * x:SEQ * x + nk], mask[:, keys], HD ** -0.5,
                                                  NEG, ALU.add, ALU.max, mx[t][:, col:col + 1]))
                joined()
                if v == 0:
                    ve.wait_ge(nsink_ready, 1)
                cols = slice(4 * m + half, 4 * m + half + 3, 2)
                ve.scalar_tensor_tensor(negm[t][:, cols], mx[t][:, cols], -1.0, nsink[:, cols], ALU.mult, ALU.min).then_inc(sm_ready, 1)

            def PT(v, ph):
                t = v // 8
                ve.wait_ge(pT_psum, v + 1)
                if v >= 2:
                    ve.wait_ge(pv_done, v - 1)
                n = 2 * P * (1 + t)
                ve.tensor_copy(prT[v % 2][:, 0:n], turned_bank(v)[:, 0:n]).then_inc(pT_ready, 1)

            def AO(quarter, ph):
                t, half = quarter // 2, quarter % 2
                cols = slice(8 * half, 8 * half + 8)
                ve.tensor_tensor(esink[t][:, cols], negm[t][:, cols], table[:, T_SINK + 8 * half:T_SINK + 8 * half + 8],
                                 ALU.add).then_inc(es_arg[t], 1)
                ve.wait_ge(es_ready[t], half + 1)
                ve.wait_ge(p_ready, 16 * t + 8 * (half + 1))
                chain(ve.tensor_tensor(lsum[t][:, cols], lsum[t][:, cols], esink[t][:, cols], ALU.add))
                joined()
                chain(ve.reciprocal(lrec[t][:, cols], lsum[t][:, cols]))
                joined()
                ve.wait_ge(pv_done, 8 * t + 4 * half + 4)
                ve.tensor_tensor(qkv[t][:, 512 + 512 * half:1024 + 512 * half].rearrange("p (a f) -> p a f", f=HD),
                                 pD[t][:, 512:1024].rearrange("p (a f) -> p a f", f=HD),
                                 lrec[t][:, cols].unsqueeze(2).broadcast_to([P, 8, HD]), ALU.mult).then_inc(ao_ready[t], 1)

            def AT(t, half, ph):
                ve.wait_ge(aoh_ready[t], half + 1)
                ve.tensor_tensor(xTl[t][:, 4 * half:4 * half + 4, :].rearrange("p k r -> p (k r)"), ao_bank(t, half),
                                 xTh[t][:, 4 * half:4 * half + 4, :].rearrange("p k r -> p (k r)").bitcast(F32),
                                 ALU.subtract).then_inc(aoT_ready[t], 1)

            def LAT(t, ph):
                ve.wait_ge(latT_psum[t], 1)
                g = feats[:, GAIN_LAT:GAIN_LAT + 3].unsqueeze(2).broadcast_to([P, 3, P])
                ve.tensor_tensor(latf[:], pD[t][:, 512:896].rearrange("p (k r) -> p k r", k=3), g, ALU.mult).then_inc(latf_ready[t], 1)
                ve.wait_ge(lath_ready[t], 1)
                ve.tensor_tensor(latTl[:], latf[:], latTh[:].bitcast(F32), ALU.subtract).then_inc(latT_ready[t], 1)

            def rotate(x1, x2, co, si, tmp):
                chain(ve.tensor_tensor(tmp[0], x1, co, ALU.mult))
                chain(ve.tensor_tensor(tmp[1], x2, si, ALU.mult))
                chain(ve.tensor_tensor(tmp[2], x1, si, ALU.mult))
                chain(ve.tensor_tensor(tmp[3], x2, co, ALU.mult))
                joined()
                chain(ve.tensor_tensor(x1, tmp[0], tmp[1], ALU.subtract))
                return ve.tensor_tensor(x2, tmp[2], tmp[3], ALU.add)

            def U(t, ph):
                if t == 0:
                    ve.wait_ge(sincos_ready, 2)
                half = PE_DIM // 2
                co, si = (x[:, t, 0:32:2] for x in (cos2, sin2))
                kp = lat[t][:, Q_RANK + KV_RANK:LATENT]
                tmp = [mpT[0][:, i * 128:i * 128 + 128].rearrange("p (a f) -> p a f", a=8) for i in range(4)]
                chain(rotate(kp[:, 0:half], kp[:, half:PE_DIM], co, si, [x[:, 0, :] for x in tmp]))
                joined()
                ve.wait_ge(u_out[t], 4)
                ve.tensor_copy(mk[:, :, NOPE:QK], kp.unsqueeze(1).broadcast_to([P, MLA_HEADS, PE_DIM])).then_inc(mqk_ready[t], 1)
                wide = [x.unsqueeze(1).broadcast_to([P, 8, half]) for x in (co, si)]
                rotate(mq[:, :, NOPE:NOPE + half], mq[:, :, NOPE + half:QK], *wide, tmp).then_inc(mqk_ready[t], 1)

            def MT(t, ph):
                ve.wait_ge(mT_psum[t], 2)
                for half in range(2):
                    ve.tensor_copy(mkT[:, 4 * half:4 * half + 4, P * t:P * (t + 1)],
                                   (pG, pT)[half][1][0:QK, :].rearrange("p (a r) -> p a r", a=4)).then_inc(mkT_ready[t], 1)

            def MS(v, ph):
                t, j = v // 4, v % 4
                ve.wait_ge(ms_psum, v + 1)
                chain(ve.tensor_reduce(mx[t][:, 2 * j:2 * j + 2], pG[v % 2][:].rearrange("p (x k) -> p x k", x=2), AX.X, ALU.max,
                                       negate=True))
                joined()
                ve.tensor_scalar(negm[t][:, 2 * j:2 * j + 2], mx[t][:, 2 * j:2 * j + 2], MLA_SCALE, None, ALU.mult).then_inc(mmax_ready, 1)

            def MPT(v, ph):
                ve.wait_ge(mpT_psum, v + 1)
                if v >= 2:
                    ve.wait_ge(mpv_done, v - 1)
                ve.tensor_copy(mpT[v % 2][:], pT[v % 2][:]).then_inc(mpT_ready, 1)

            def MN(t, ph):
                ve.wait_ge(mp_ready, 8 * (t + 1))
                chain(ve.reciprocal(lrec[t][:, 0:8], lsum[t][:, 0:8]))
                joined()
                ve.wait_ge(mpv_done, 4 * (t + 1))
                ve.tensor_tensor(mo[t][:].rearrange("p (a f) -> p a f", f=HD), pD[t][:, 512:1024].rearrange("p (a f) -> p a f", f=HD),
                                 lrec[t][:, 0:8].unsqueeze(2).broadcast_to([P, 8, HD]), ALU.mult).then_inc(mo_ready[t], 1)

            def RROPE(t, part, ph):
                if part == 0:
                    ve.wait_ge(x_out[t], 3)
                if t or part:
                    ve.wait_ge(rrope_done[t if part else 0], 1 if part else 2)
                z = rqk[t][:, 512 * part:512 * part + 512].rearrange("p (a f) -> p a f", f=HD)
                co, si = (x[:, t, :].unsqueeze(1).broadcast_to([P, 8, RHALF]) for x in (cos2, sin2))
                rotate(z[:, :, 0:RHALF], z[:, :, RHALF:HD], co, si, [x[:] for x in ttmp]).then_inc(rrope_done[t], 1)

            def RT(t, ph):
                ve.wait_ge(rT_psum[t], 2)
                ve.tensor_copy(rkT[:, :, P * t:P * (t + 1)], pG[1][:].rearrange("p (a r) -> p a r", a=4)).then_inc(rkT_ready[t], 1)

            def RM(hd, ph):
                ve.wait_ge(rs_psum, hd + 1)
                ve.wait_ge(dm_ready, hd + 1)
                if hd >= 2:
                    ve.wait_ge(rpv_done, hd - 1)
                for jt in range(2):
                    ve.scalar_tensor_tensor(sd[hd % 2][:, jt, :], pG[hd % 2][:, SEQ * jt:SEQ * (jt + 1)], HD ** -0.5,
                                            dm[hd][:, P * (1 - jt):P * (3 - jt)], ALU.mult, ALU.mult).then_inc(sd_ready, 1)

            def GN(part, ph):
                def heads(x):
                    return x.rearrange("p t (a f) -> p t a f", f=HD)

                def over(i):
                    return gn[part][:, i, :].rearrange("p (t a) -> p t a", t=2).unsqueeze(3).broadcast_to([P, 2, 4, HD])

                o = heads(pT[part][:].rearrange("p (t n) -> p t n", t=2))
                ro = heads(rqk_both[:, :, 256 * part:256 * part + 256])
                gated = heads(rqk_both[:, :, 512 + 256 * part:768 + 256 * part])
                sq = mpT[0][:].rearrange("p (t n) -> p t n", t=2)
                sq = heads(sq)
                flat = "p (g f) -> p g f"
                ve.wait_ge(rpv_done, 4 * part + 4)
                chain(ve.tensor_reduce(gn[part][:, 0, :], pT[part][:].rearrange(flat, f=HD), AX.X, ALU.add))
                joined()
                chain(ve.tensor_scalar(gn[part][:, 0, :], gn[part][:, 0, :], 1.0 / HD, None, ALU.mult))
                joined()
                if part == 0:
                    for t in range(2):
                        ve.wait_ge(rT_psum[t], 2)
                chain(ve.tensor_tensor(ro, o, over(0), ALU.subtract))
                joined()
                if part == 1:
                    ve.wait_ge(gn_var, 1)
                chain(ve.tensor_tensor(sq, ro, ro, ALU.mult))
                joined()
                ve.tensor_reduce(gn[part][:, 1, :], mpT[0][:].rearrange(flat, f=HD), AX.X, ALU.add).then_inc(gn_var, 1)
                ve.wait_ge(silu_ready, 1)
                chain(ve.tensor_tensor(gated, gated, ro, ALU.mult))
                joined()
                ve.wait_ge(gn_r, part + 1)
                ve.tensor_tensor(ro, gated, over(3), ALU.mult).then_inc(ro_ready, 1)

            def MAT(t, ph):
                ve.wait_ge(cath_ready[t], 1)
                ve.tensor_tensor(xTl[t][:, 0:4, :].rearrange("p k r -> p (k r)"), pD[t][:, 512:1024],
                                 xTh[t][:, 0:4, :].rearrange("p k r -> p (k r)").bitcast(F32), ALU.subtract).then_inc(catT_ready[t], 1)

            def RAT(t, ph):
                ve.wait_ge(cath_ready[t], 2)
                ve.tensor_tensor(xTl[t][:, 4:8, :].rearrange("p k r -> p (k r)"), pG[t][:],
                                 xTh[t][:, 4:8, :].rearrange("p k r -> p (k r)").bitcast(F32), ALU.subtract).then_inc(catT_ready[t], 1)

            parts = dict(start=start, fill=fill, R=refill, prep=prep, tail=tail, G=G, T=T, rope=rope, QKT=QKT, S=S, PT=PT,
                         AO=AO, AT=AT, LAT=LAT, U=U, MT=MT, MS=MS, MPT=MPT, MN=MN, RROPE=RROPE, RT=RT, RM=RM, GN=GN,
                         MAT=MAT, RAT=RAT)
            walk(ve, lambda name, *a, ph=None: parts[name](*a, ph) if name in parts else None)

        @block.tensor
        def _(pe):
            def three_passes(dst, ah, al, where, n, start, stop):
                hi, lo = w_high[:, where:where + n], w_low[:, where:where + n]
                pe.matmul(dst, ah, hi, start=start, stop=False)
                pe.matmul(dst, ah, lo, start=False, stop=False)
                return pe.matmul(dst, al, hi, start=False, stop=stop)

            def turn(dst, src):
                return pe.transpose(dst, src, ident)

            def start(ph):
                pe.wait_ge(ident_loaded, 16)

            def prep(t, p, ph):
                if p == LAST:
                    return
                if p == 0:
                    pe.wait_ge(x_loaded[t], 16)
                for kt in range(KT):
                    if p > 0 and kt % 4 == 0:
                        pe.wait_ge(h_ready[t], 2 * (p - 1) + kt // 4 + 1)
                    mm = turn((pG, pT)[kt // 4][t][:, kt % 4 * P:(kt % 4 + 1) * P], h[t][:, kt * P:(kt + 1) * P])
                    if kt % 4 == 3:
                        mm.then_inc(hT_psum[t], 1)

            def G(t, b, shift, ph):
                c0 = ph.g_chunk(b)
                have = 0
                for kt in range(KT):
                    if b == 0 and kt % 4 == 0:
                        pe.wait_ge(xT_ready[t], xT_base(ph.index) + kt // 4 + 1)
                    need = ((kt + 1) * ph.cols - 1) // CHUNK + 1
                    if need > have and t == 0:
                        pe.wait_ge(w_split, c0 + need + shift * RING)
                    mm = three_passes(pG[t][:, 0:ph.cols], xTh[t][:, kt, :], xTl[t][:, kt, :], slot(c0 + kt * ph.cols // CHUNK) + kt * ph.cols % CHUNK, ph.cols,
                                      kt == 0, kt == KT - 1)
                    have = need
                    if t == 1 and (kt + 1) * ph.cols // CHUNK > kt * ph.cols // CHUNK:
                        mm.then_inc(w_freed, 1)
                    if t == 0 and kt == KT - 1:
                        mm.then_inc(g_done0, 1)

            def T(t, b, shift, ph):
                n = ph.first_block + b + 1 + shift * (RING // (ph.cg + ph.kd))
                pe.wait_ge(act_ready[t], n)
                if ph.mixer:
                    turn(pT[t][:, 0:P], gate[t][:, 0:P])
                    turn(pT[t][:, P:2 * P], act[t][:, 0:P]).then_inc(actT_psum[t], 1)
                else:
                    turn(pT[t][:, 0:P], act[t][:, 0:P])
                    turn(pT[t][:, P:2 * P], act[t][:, P:2 * P]).then_inc(actT_psum[t], 1)

            def Dn(t, b, shift, ph):
                n = ph.first_block + b + 1 + shift * (RING // (ph.cg + ph.kd))
                pe.wait_ge(aT_ready[t], n)
                last = b == ph.nb - 1
                order = [(k, half) for k in range(ph.kd) for half in range(2)]
                if last:
                    order.sort(key=lambda x: x[1])
                for i, (k, half) in enumerate(order):
                    c = ph.d_chunk(b) + k
                    if t == 0 and (half == 0 or not last):
                        pe.wait_ge(w_split, c + 1 + shift * RING)
                    mm = three_passes(pD[t][:, 512 * half:512 * half + 512], aTh[t][:, k, :], aTl[t][:, k, :],
                                      slot(c) + 512 * half, 512, b == 0 and k == 0, last and k == ph.kd - 1)
                    if t == 1 and half == 1:
                        mm.then_inc(w_freed, 1)
                    elif last and k == ph.kd - 1:
                        mm.then_inc(d_done0 if half else d_half[t], 1)

            def proj(j, t, c, ph):
                dst = pG[t][:] if j == 2 else pD[t][:, 512 * j:512 * j + 512]
                high, low = (x2h, x2l) if j else (xTh, xTl)
                if c % 2 == 0:
                    pe.wait_ge(xT_ready[t], xT_base(B_INDEX) + (2 if j else 0) + c // 2 + 1)
                if j == 2 and c == 0:
                    pe.wait_ge(xT_ready[t], xT_base(B_INDEX) + 4)
                w = B_FIRST + 4 * j + c
                if t == 0:
                    pe.wait_ge(w_split, w + 1)
                for i in range(2):
                    kt = 2 * c + i
                    mm = three_passes(dst, high[t][:, kt, :], low[t][:, kt, :], slot(w) + 512 * i, 512, kt == 0, kt == KT - 1)
                if t == 1:
                    mm.then_inc(w_freed, 1)
                elif c == 3:
                    mm.then_inc(q_done0, 1)

            def QKT(t, part, ph):
                pe.wait_ge(rope_done, 2 * (2 * t + part + 1))
                if part == 0:
                    for i in range(2):
                        mm = turn(pD[t][:, P * i:P * (i + 1)], qkv[t][:, 256 + P * i:256 + P * (i + 1)])
                    mm.then_inc(qkT_psum[t], 1)
                for i in range(4):
                    first = 512 + 512 * part + P * i
                    mm = turn((pG[t][:] if part else pD[t][:, 512:1024])[:, i * P:(i + 1) * P], qkv[t][:, first:first + P])
                mm.then_inc(qkT_psum[t], 1)

            def S(v, ph):
                t, m, half = v // 8, v % 8 // 2, v % 2
                if v % 8 == 0:
                    pe.wait_ge(kqT_act[t], 1)
                    pe.wait_ge(kqT_dve[t], 1)
                if v == 1 or v % 8 == 4:
                    pe.wait_ge(kqT_act[t], 2)
                if v >= 2:
                    pe.wait_ge(sm_ready, v - 1)
                part = slice(HD * half, HD * half + HD)
                for x in range(2):
                    i = 2 * m + x
                    nk = P * (1 + t)
                    mm = pe.matmul((pT, pG)[half][0][:, SEQ * x:SEQ * x + nk], qT[t][part, i, :], kT[part, i // 4, 0:nk],
                                   start=True, stop=True)
                mm.then_inc(s_done, 1)

            def PT(v, ph):
                t = v // 8
                pe.wait_ge(p_ready, 2 * (v + 1))
                if v >= 2:
                    pe.wait_ge(pT_ready, v - 1)
                n = 0
                for x in range(2):
                    for kt in range(1 - t, 2):
                        mm = turn(turned_bank(v)[:, P * n:P * (n + 1)], pr[v % 2][:, x, P * kt:P * (kt + 1)])
                        n += 1
                mm.then_inc(pT_psum, 1)

            def PV(v, ph):
                t, u, m, half = v // 8, v % 8, v % 8 // 2, v % 2
                pe.wait_ge(pT_ready, v + 1)
                if u == 4:
                    pe.wait_ge(ao_ready[t], 1)
                n = 0
                for x in range(2):
                    i = 2 * m + x
                    kv = 2 * (i // 4) + half
                    dst = pD[t][:, 512 + i % 4 * P + HD * half:512 + i % 4 * P + HD * half + HD]
                    for kt in range(1 + t):
                        mm = pe.matmul(dst, prT[v % 2][:, P * n:P * (n + 1)], qkv[kt][:, HD * kv:HD * kv + HD],
                                       start=kt == 0, stop=kt == t)
                        n += 1
                mm.then_inc(pv_done, 1)

            def AT(t, half, ph):
                pe.wait_ge(ao_ready[t], half + 1)
                if half == 0 and t == 0:
                    pe.wait_ge(pT_ready, 8)
                for k in range(4):
                    first = 512 + 512 * half + P * k
                    mm = turn(ao_bank(t, half)[:, k * P:(k + 1) * P], qkv[t][:, first:first + P])
                mm.then_inc(aoT_psum[t], 1)

            def out_product(t, kt, w):
                for half in range(2):
                    mm = three_passes(pD[t][:, 512 * half:512 * half + 512], xTh[t][:, kt, :], xTl[t][:, kt, :],
                                      slot(w) + 512 * half, 512, kt == 0, kt == KT - 1)
                    if kt == KT - 1 and half == 0:
                        mm.then_inc(d_half[t], 1)
                if t == 1:
                    mm.then_inc(w_freed, 1)
                elif kt == KT - 1:
                    mm.then_inc(d_done0, 1)

            def O(t, kt, ph):
                if kt == 0 and t == 0:
                    pe.wait_ge(aoT_ready[t], 2)
                elif kt % 4 == 0:
                    pe.wait_ge(aoT_ready[t], kt // 4 + 1)
                if t == 0:
                    pe.wait_ge(w_split, B_WO + kt + 1)
                out_product(t, kt, B_WO + kt)

            def X(i, t, c, ph):
                n = LATENT if i == 0 else 512
                if i == 0 and c % 2 == 0:
                    pe.wait_ge(xT_ready[t], xT_base(C_INDEX) + c // 2 + 1)
                if c == 0 and i > 0:
                    pe.wait_ge(x_out[t], i)
                w = C_X[i] + c
                if t == 0:
                    pe.wait_ge(w_split, w + 1)
                for k in range(2):
                    kt = 2 * c + k
                    mm = three_passes(pD[t][:, 0:n], xTh[t][:, kt, :], xTl[t][:, kt, :], slot(w) + 512 * k, n, kt == 0, kt == KT - 1)
                if t == 1:
                    mm.then_inc(w_freed, 1)
                elif c == 3:
                    mm.then_inc(x_done0, 1)

            def LAT_(t, ph):
                pe.wait_ge(x_out[t], 1)
                for k in range(3):
                    mm = turn(pD[t][:, 512 + P * k:512 + P * (k + 1)], lat[t][:, P * k:P * (k + 1)])
                mm.then_inc(latT_psum[t], 1)

            def U(t, ph):
                pe.wait_ge(latT_ready[t], 1)
                if t == 1:
                    pe.wait_ge(mqT_ready[0], 2)
                    pe.wait_ge(mkT_ready[0], 2)
                else:
                    pe.wait_ge(xT_ready[1], xT_base(C_INDEX) + 2)
                for k in range(3):
                    w = C_U + k
                    if t == 0:
                        pe.wait_ge(w_split, w + 1)
                    for half in range(2):
                        if k < 2:
                            mm = three_passes((pG, pT)[half][0][:, 0:384], latTh[:, k, :], latTl[:, k, :], slot(w) + 384 * half, 384,
                                              k == 0, k == 1)
                        else:
                            mm = three_passes((pG, pT)[half][1][:], latTh[:, k, :], latTl[:, k, :], slot(w) + 512 * half, 512, True, True)
                    if t == 1:
                        mm.then_inc(w_freed, 1)
                if t == 0:
                    mm.then_inc(u_done0, 1)

            def MT(t, ph):
                pe.wait_ge(mqk_ready[t], 2)
                for i, src in enumerate((mq, mk)):
                    for hd in range(MLA_HEADS):
                        mm = turn((pG, pT)[hd // 4][i][0:QK, hd % 4 * P:(hd % 4 + 1) * P], src[:, hd, :])
                    mm.then_inc(mT_psum[t], 1)

            def MS(v, ph):
                t, j = v // 4, v % 4
                if v == 0:
                    for r in range(2):
                        pe.wait_ge(mqT_ready[r], 2)
                        pe.wait_ge(mkT_ready[r], 2)
                if v >= 2:
                    pe.wait_ge(mp_ready, 2 * (v - 1))
                for x in range(2):
                    hd = 2 * j + x
                    mm = pe.matmul(pG[v % 2][:, SEQ * x:SEQ * (x + 1)], mqT[:, hd, P * t:P * (t + 1)], mkT[:, hd, :],
                                   start=True, stop=True)
                mm.then_inc(ms_psum, 1)

            def MPT(v, ph):
                pe.wait_ge(mp_ready, 2 * (v + 1))
                if v >= 2:
                    pe.wait_ge(mpT_ready, v - 1)
                for x in range(2):
                    for kt in range(2):
                        mm = turn(pT[v % 2][:, (2 * x + kt) * P:(2 * x + kt + 1) * P], mp[v % 2][:, x, P * kt:P * (kt + 1)])
                mm.then_inc(mpT_psum, 1)

            def MPV(v, ph):
                t, j = v // 4, v % 4
                pe.wait_ge(mpT_ready, v + 1)
                for x in range(2):
                    hd = 2 * j + x
                    for kt in range(2):
                        mm = pe.matmul(pD[t][:, 512 + HD * hd:512 + HD * (hd + 1)], mpT[v % 2][:, (2 * x + kt) * P:(2 * x + kt + 1) * P],
                                       mv[kt][:, HD * hd:HD * (hd + 1)], start=kt == 0, stop=kt == 1)
                mm.then_inc(mpv_done, 1)

            def RT(t, ph):
                pe.wait_ge(rrope_done[t], 2)
                if t == 0:
                    pe.wait_ge(mp_ready, 16)
                else:
                    pe.wait_ge(rqT_ready[0], 1)
                    pe.wait_ge(rkT_ready[0], 1)
                for i in range(2):
                    for k in range(4):
                        mm = turn(pG[i][:, P * k:P * (k + 1)], rqk[t][:, 512 * i + P * k:512 * i + P * (k + 1)])
                    mm.then_inc(rT_psum[t], 1)

            def RS(hd, ph):
                if hd == 0:
                    pe.wait_ge(rqT_ready[1], 1)
                    pe.wait_ge(rkT_ready[1], 1)
                if hd >= 2:
                    pe.wait_ge(sd_ready, 2 * (hd - 1))
                part = slice(HD * (hd % 2), HD * (hd % 2) + HD)
                for jt in range(2):
                    mm = pe.matmul(pG[hd % 2][:, SEQ * jt:SEQ * (jt + 1)], rkT[part, hd // 2, P * jt:P * (jt + 1)],
                                   rqT[part, hd // 2, :], start=True, stop=True)
                mm.then_inc(rs_psum, 1)

            def RPV(hd, ph):
                pe.wait_ge(sd_ready, 2 * (hd + 1))
                if hd == 0:
                    pe.wait_ge(mpT_ready, 8)
                    pe.wait_ge(x_out[0], 4)
                    pe.wait_ge(x_out[1], 4)
                for t in range(2):
                    dst = pT[hd // 4][:, 256 * t + HD * (hd % 4):256 * t + HD * (hd % 4 + 1)]
                    for jt in range(2):
                        mm = pe.matmul(dst, sd[hd % 2][:, jt, P * t:P * (t + 1)],
                                       rv[jt][:, HD * hd:HD * (hd + 1)], start=jt == 0, stop=jt == 1)
                mm.then_inc(rpv_done, 1)

            def MAT(t, ph):
                pe.wait_ge(mo_ready[t], 1)
                for k in range(4):
                    mm = turn(pD[t][:, 512 + P * k:512 + P * (k + 1)], mo[t][:, P * k:P * (k + 1)])
                mm.then_inc(catT_psum[t], 1)

            def RAT(t, ph):
                pe.wait_ge(ro_ready, 2)
                for k in range(4):
                    mm = turn(pG[t][:, P * k:P * (k + 1)], rqk[t][:, P * k:P * (k + 1)])
                mm.then_inc(catT_psum[t], 1)

            def Oc(t, kt, ph):
                if kt == 0:
                    pe.wait_ge(rgate[t], 1)
                if kt % 4 == 0:
                    pe.wait_ge(catT_ready[t], kt // 4 + 1)
                if t == 0:
                    pe.wait_ge(w_split, C_WO + kt + 1)
                out_product(t, kt, C_WO + kt)

            parts = dict(start=start, prep=prep, G=G, D=Dn, T=T, proj=proj, QKT=QKT, S=S, PT=PT, PV=PV, AT=AT, O=O, X=X, LAT=LAT_,
                         U=U, MT=MT, MS=MS, MPT=MPT, MPV=MPV, RT=RT, RS=RS, RPV=RPV, MAT=MAT, RAT=RAT, Oc=Oc)
            walk(pe, lambda name, *a, ph=None: parts[name](*a, ph) if name in parts else None)


class NoLoop:

    def Fori(self, first, last):
        return ExitStack()



def weight_chunks(w):
    parts = []

    def sliced(cols, pad=0):
        if pad:
            cols = np.concatenate([cols, np.zeros((cols.shape[0], pad), cols.dtype)], axis=1)
        wide = cols.reshape(KT, P, -1).transpose(1, 0, 2).reshape(P, -1)
        return list(wide.reshape(P, -1, CHUNK).transpose(1, 0, 2))

    def blocks(ph, inputs, output):
        found = {}
        wide = ph.cols // len(inputs)
        for b in range(ph.nb):
            cols = np.concatenate([m[:, wide * b:wide * (b + 1)] for m in inputs], axis=1)
            for i, c in enumerate(sliced(cols)):
                found[ph.g_chunk(b) + i] = c
            for k in range(ph.kd):
                row = P * (ph.kd * b + k)
                found[ph.d_chunk(b) + k] = output[row:row + P]
        parts.extend(found[c] for c in sorted(found))

    a_in = w["a_w_in"][0]
    blocks(MIX, [a_in[:, D * i:D * (i + 1)] for i in range(3)], w["a_w_out"][0])

    def ffn(ph, layer):
        both = w["ffn_w_gate_up"][layer]
        f = both.shape[1] // 2
        blocks(ph, [both[:, :f], both[:, f:]], w["ffn_w_down"][layer])

    ffn(FFN1, 0)
    kv = w["w_kv"]
    parts.extend(sliced(np.concatenate([kv[:, 256:], kv[:, :256]], axis=1)))
    order = [head_at(i, p) for i in range(PAIRS) for p in range(2)]
    q = w["b_w_q"][0].reshape(D, HEADS, HD)[:, order, :].reshape(D, D)
    for j in range(2):
        parts.extend(sliced(q[:, 512 * j:512 * j + 512]))
    parts.extend(w["b_w_o"][0].reshape(HEADS, HD, D)[order].reshape(KT, P, D))
    ffn(FFN2, 1)
    blocks(FFN3, [w["ffn1_w_gate_2"][0], w["ffn1_w_up_2"][0]], w["ffn1_w_down_2"][0])
    w_in = w["w_in_2"][0]
    parts.extend(sliced(w_in[:, 0:LATENT], 512 - LATENT))
    uq, ukv = w["w_uq_2"][0], w["w_ukv_2"][0].reshape(KV_RANK, MLA_HEADS, 2, HD)
    pad = np.zeros((P, CHUNK - uq.shape[1]), uq.dtype)
    for i in range(4):
        if i == 2:
            parts.extend(np.concatenate([uq[P * k:P * (k + 1)], pad], axis=1) for k in range(2))
            parts.append(ukv.transpose(0, 2, 1, 3).reshape(P, CHUNK))
        parts.extend(sliced(w_in[:, LATENT + 512 * i:LATENT + 512 * (i + 1)]))
    parts.extend(w["w_o_2"][0].reshape(KT, P, D))
    blocks(FFN4, [w["ffn2_w_gate_2"][0], w["ffn2_w_up_2"][0]], w["ffn2_w_down_2"][0])
    return np.ascontiguousarray(np.stack(parts))


def shape_constants():
    f32 = np.float32
    c = np.zeros((P, CONSTS), f32)
    c[:, C_ID:C_ID + P] = np.eye(P)
    inv = (f32(500000.0) ** (-np.arange(0, 16, 2, dtype=f32) / f32(16))).astype(f32)
    angle = (np.arange(SEQ, dtype=f32)[:, None] * inv[None, :]).astype(f32)
    tab = np.stack([np.cos(angle), np.sin(angle)], axis=1).astype(f32)
    c[:, C_ROPE:C_ROPE + 32] = tab.reshape(2, P, 16).transpose(1, 0, 2).reshape(P, 32)
    i, j = np.arange(P)[:, None], np.arange(P)[None, :]
    c[:, C_MASK:C_MASK + P] = np.where(j > i, 0.0, NEG)
    c[:, C_MASK + P:C_MASK + 2 * P] = np.where(j <= i, 0.0, NEG)
    c[:, C_INV:C_INV + 32] = (f32(10000.0) ** (-np.arange(32, dtype=f32) / f32(32)))[None, :]
    dist = j - i
    c[:, C_REL:C_REL + 4 * P] = np.concatenate(
        [np.maximum(dist, 0), dist + P, np.maximum(-dist, 0), P - dist], axis=1)
    return c


def kernel(**inputs):
    import concourse.bacc as bacc
    from concourse.bass_utils import run_bass_kernel_spmd

    w = {k: np.asarray(v) for k, v in inputs.items()}

    def by_feature(g):
        return np.asarray(g).reshape(-1, P).T

    feats = np.ascontiguousarray(np.concatenate(
        [by_feature(g) for g in (w["a_pre_norm"][0], w["ffn_pre_norm"][0], w["kv_norm"], w["b_pre_norm"][0], w["ffn_pre_norm"][1],
                                 w["ffn1_norm_2"][0], w["mix_norm_2"][0], w["ffn2_norm_2"][0], w["q_norm_2"][0], w["kv_norm_2"][0])]
        + [w["a_conv_w"][0].reshape(3, KT, P).transpose(2, 1, 0).reshape(P, 24)], axis=1))
    order = [head_at(i, p) for i in range(PAIRS) for p in range(2)]
    row = np.concatenate([w["b_sinks"][0][order], w["ret_decay_fwd_2"][0], w["ret_decay_bwd_2"][0]])
    arrays = {
        "x": np.ascontiguousarray(w["x"][0]),
        "stream": weight_chunks(w),
        "feats": feats,
        "consts": shape_constants(),
        "table": np.ascontiguousarray(np.broadcast_to(row, (P, TAB))),
        "positions": np.ascontiguousarray(w["positions_2"].reshape(2, P).T),
        "posts": np.ascontiguousarray(np.stack([w["a_post_norm"][0], w["ffn_post_norm"][0], w["b_post_norm"][0],
                                                w["ffn_post_norm"][1], w["final_norm_2"]])),
    }
    nc = bacc.Bacc("TRN2", target_bir_lowering=False, num_devices=1)
    args = [nc.dram_tensor(f"in_{k}", a.shape, mybir.dt.from_np(a.dtype), kind="ExternalInput").ap() for k, a in arrays.items()]
    out = nc.dram_tensor("out", (SEQ, D), F32, kind="ExternalOutput").ap()
    build(nc, *args, out)
    result = run_bass_kernel_spmd(nc, [{f"in_{k}": a for k, a in arrays.items()}], core_ids=[0])
    return result.results[0]["out"].reshape(1, SEQ, D)
```

```python
import math
from contextlib import ExitStack

import numpy as np

import concourse.bass as bass
from concourse import mybir

F32 = mybir.dt.float32
F32R = mybir.dt.float32r
BF16 = mybir.dt.bfloat16
I32 = mybir.dt.int32
ALU = mybir.AluOpType
ACT = mybir.ActivationFunctionType
AX = mybir.AxisListType

P = 128
D = 1024
KT = D // P
SEQ = 256
EPS = 1e-6
NEG = -1e30

HEADS, KV_HEADS, HD = 16, 4, 64
PAIRS = HEADS // 2
ROT_HALF = 8
MLA_HEADS, NOPE, PE_DIM, QK = 8, 64, 32, 96
Q_RANK, KV_RANK = 256, 128
LATENT = Q_RANK + KV_RANK + PE_DIM
RET_HEADS, RHALF = 8, 32
MLA_SCALE = QK ** -0.5

CHUNK = 1024
RING = 12
RAW = 4


class Phase:

    def __init__(self, mixer, index, first_chunk, first_block):
        self.mixer, self.index = mixer, index
        self.nb, self.cols, self.kd = (8, 384, 1) if mixer else (11, 512, 2)
        self.cg = KT * self.cols // CHUNK
        self.first_chunk, self.first_block = first_chunk, first_block
        self.chunks = self.nb * (self.cg + self.kd)

    def g_chunk(self, b):
        return self.first_chunk + b * self.cg + max(b - 1, 0) * self.kd

    def d_chunk(self, b):
        return self.first_chunk + min(b + 2, self.nb) * self.cg + b * self.kd


MIX = Phase(True, 0, 0, 0)
FFN1 = Phase(False, 1, MIX.chunks, MIX.nb)
B_FIRST = FFN1.first_chunk + FFN1.chunks
B_WO = B_FIRST + 12
FFN2 = Phase(False, 3, B_WO + 8, FFN1.first_block + FFN1.nb)
FFN3 = Phase(False, 4, FFN2.first_chunk + FFN2.chunks, FFN2.first_block + FFN2.nb)
C_FIRST = FFN3.first_chunk + FFN3.chunks
C_X = [C_FIRST, C_FIRST + 4, C_FIRST + 8, C_FIRST + 15, C_FIRST + 19]
C_U = C_FIRST + 12
C_WO = C_X[4] + 4
FFN4 = Phase(False, 6, C_WO + 8, FFN3.first_block + FFN3.nb)
N_CHUNKS = FFN4.first_chunk + FFN4.chunks
B_INDEX, C_INDEX, LAST = 2, 5, 7
POST_NORMS = 4

GAIN = {0: 0, 1: 8, 2: 16, "q": 24, 3: 32, 4: 40, 5: 48, 6: 56}
GAIN_LAT = 64
CONV = 67
FEATS = CONV + 24
C_ID, C_ROPE, C_MASK, C_INV, C_REL = 0, 128, 160, 416, 448
CONSTS = C_REL + 4 * P
T_SINK, T_DECAY, TAB = 0, 16, 32


def head_at(i, p):
    return (2 * (i // 4) + p) * 4 + i % 4



FILL = {("G", 0): (4, 1), ("T", 0): (5, 1), ("Y", 0): (6, 2), ("G", 1): (8, 1), ("T", 1): (9, 1), ("Y", 1): (10, 2)}

WINDOW_BESIDE = {1: [("proj", 1, 1, 3)], 2: [("proj", 2, 1, 0)], 3: [("proj", 2, 1, 1), ("rope", 1, 0)],
                 5: [("proj", 2, 1, 2), ("QKT", 1, 0)], 6: [("proj", 2, 1, 3), ("rope", 1, 1)], 7: [("QKT", 1, 1)],
                 9: [("AT", 0, 0), ("AT", 0, 1)]}
FIRST_OUTPUT = 10
WINDOW_REFILLS = (1, 2, 6, 11, 12, 13)


def walk_prep(step, t, phase):
    step("turn", t, phase)
    step("parts", t, phase)


def refill(step, freed, n=None):
    for _ in range(len(freed) if n is None else min(n, len(freed))):
        step("R", freed.pop(0), 1, 0)


def walk_block_step(ph, s, shift, step, freed):
    def fill(name):
        if ph.mixer and (name, s) in FILL:
            step("fill", *FILL[name, s])

    step("G", 0, s, shift)
    fill("G")
    if s == 2:
        step("T", 1, 0, shift)
        if ph.mixer:
            step("Y", 1, 0, shift)
    if s == 0 and not ph.mixer:
        walk_prep(step, 1, ph.index)
    if s >= 1:
        step("D", 0, s - 1, shift)
    step("T", 0, s, shift)
    refill(step, freed)
    fill("T")
    if ph.mixer:
        step("Y", 0, s, shift)
        fill("Y")
    if s >= 1:
        walk_follower(ph, s - 1, shift, step, freed)


def walk_follower(ph, b, shift, step, freed):
    g, first, last = ph.g_chunk(b), b == 0, b == ph.nb - 1
    early = (0 if ph.mixer else 2) if first or (last and ph.mixer) else 1 if ph.mixer else 3
    step("R", g, early, shift)
    step("G", 1, b, shift)
    if ph.mixer and first:
        step("R", g, 1, shift)
        early = 1
    if ph.mixer and last:
        step("join", 0, ph.index)
    if not ph.mixer:
        step("R", g + early, ph.cg - early, shift)
        early = ph.cg
    if not first:
        step("D", 1, b - 1, shift)
    if ph.mixer and not first and not last:
        step("R", g + early, ph.cg - early, shift)
        early = ph.cg
    if not first:
        step("T", 1, b, shift)
    if not first and not last:
        step("R", ph.d_chunk(b - 1), ph.kd, shift)
    if ph.mixer and not first:
        step("Y", 1, b, shift)
    if ph.mixer and (first or last):
        freed += range(g + early, g + ph.cg)


def walk_phase(eng, ph, step, trips, freed):
    per = RING // (ph.cg + ph.kd)
    start = 3 if trips else ph.nb
    for s in range(start):
        walk_block_step(ph, s, 0, step, freed)
    if trips:
        with eng.Fori(0, trips) as turn:
            for s in range(start, start + per):
                walk_block_step(ph, s, turn, step, freed)
        for s in range(start + per * trips, ph.nb):
            walk_block_step(ph, s, 0, step, freed)
    last = ph.nb - 1
    if ph is FFN4:
        walk_follower(ph, last, 0, step, freed)
        step("D", 0, last, 0)
        step("join", 0, ph.index)
        step("D", 1, last, 0)
        step("join", 1, ph.index)
        step("last", 0)
        step("last", 1)
        return
    step("D", 0, last, 0)
    step("tail", 0, ph.index)
    if not ph.mixer:
        step("join", 0, ph.index)
    walk_follower(ph, last, 0, step, freed)
    walk_prep(step, 0, ph.index + 1)
    step("D", 1, last, 0)
    step("tail", 1, ph.index)
    step("join", 1, ph.index)
    freed += [ph.d_chunk(b) + k for b in (last - 1, last) for k in range(ph.kd)]
    if ph in (MIX, FFN2):
        refill(step, freed, 2)


def walk_attention(step, freed):
    def project(j, t, c):
        step("proj", j, t, c)
        if t == 1:
            freed.append(B_FIRST + 4 * j + c)

    def projects(j, t, cs=range(4)):
        for c in cs:
            project(j, t, c)

    def output(t, kt):
        step("O", t, kt)
        if t == 1:
            freed.append(B_WO + kt)

    projects(0, 0, range(3))
    walk_prep(step, 1, B_INDEX)
    project(0, 0, 3)
    step("second", 0)
    refill(step, freed)
    projects(0, 1)
    step("second", 1)
    refill(step, freed, 2)
    projects(1, 0)
    step("rope", 0, 0)
    refill(step, freed)
    projects(2, 0)
    step("exp_table",)
    step("rope", 0, 1)
    project(1, 1, 0)
    step("QKT", 0, 0)
    refill(step, freed, 1)
    project(1, 1, 1)
    step("QKT", 0, 1)
    step("S", 0)
    step("E", 0)
    step("S", 1)
    project(1, 1, 2)
    for v in range(16):
        if v in WINDOW_REFILLS:
            refill(step, freed, 1)
        if v < 15:
            step("E", v + 1)
        step("PT", v)
        for name, *a in WINDOW_BESIDE.get(v, ()):
            if name == "proj":
                project(*a)
            else:
                step(name, *a)
        if v >= FIRST_OUTPUT:
            output(0, v - FIRST_OUTPUT)
        if v == 14:
            step("AT", 1, 0)
        if v < 14:
            step("S", v + 2)
        if v >= 1:
            step("PV", v - 1)
            if v % 4 == 0:
                step("AO", v // 4 - 1)
    step("PV", 15)
    step("AO", 3)
    for kt in range(16 - FIRST_OUTPUT, 8):
        output(0, kt)
    step("tail", 0, B_INDEX)
    step("join", 0, B_INDEX)
    step("AT", 1, 1)
    for kt in range(5):
        output(1, kt)
    refill(step, freed, 4)
    walk_prep(step, 0, B_INDEX + 1)
    for kt in range(5, 8):
        output(1, kt)
    step("tail", 1, B_INDEX)
    step("join", 1, B_INDEX)
    refill(step, freed, 2)


def walk_latent(step, freed):
    def project(i, t, c):
        step("X", i, t, c)
        if t == 1:
            freed.append(C_X[i] + c)

    def projects(i, t, cs=range(4)):
        for c in cs:
            project(i, t, c)
            if t == 1 and len(freed) > 1:
                refill(step, freed, 1)

    def output(t, kt):
        step("Oc", t, kt)
        if t == 1:
            freed.append(C_WO + kt)

    projects(0, 0)
    walk_prep(step, 1, C_INDEX)
    refill(step, freed, 2)
    projects(1, 0)
    step("LAT", 0)
    refill(step, freed)
    projects(0, 1)
    projects(2, 0)
    step("U", 0)
    projects(1, 1)
    step("LAT", 1)
    step("MT", 0)
    projects(2, 1)
    step("U", 1)
    step("exp_table",)
    freed += [C_U, C_U + 1, C_U + 2]
    projects(3, 0)
    step("MT", 1)
    for t in range(2):
        for part in range(2):
            step("RROPE", t, part)
    project(3, 1, 0)
    refill(step, freed, 1)
    step("MS", 0)
    step("ME", 0)
    step("MS", 1)
    beside = [(3, 1, c) for c in range(1, 4)] + [(4, 0, c) for c in range(4)] + [(4, 1, c) for c in range(4)]
    project(*beside.pop(0))
    refill(step, freed, 1)
    for v in range(8):
        refill(step, freed, 1)
        if v < 7:
            step("ME", v + 1)
        step("MPT", v)
        for _ in range(min(1 + v % 2, len(beside))):
            project(*beside.pop(0))
        if v < 6:
            step("MS", v + 2)
        refill(step, freed, 1)
        if v == 6:
            step("gate", 0)
        if v == 7:
            step("RT", 0)
            step("MAT", 0)
        if v >= 1:
            step("MPV", v - 1)
        if v == 4:
            step("MN", 0)
    step("MPV", 7)
    step("RT", 1)
    step("MN", 1)
    step("gate", 1)
    step("decay", 0)
    step("decay", 1)
    output(0, 0)
    step("MAT", 1)
    refill(step, freed)
    for hd in range(2, 8):
        step("decay", hd)
    step("silu",)
    step("RS", 0)
    step("RS", 1)
    for hd in range(8):
        step("RM", hd)
        if hd == 0:
            output(0, 1)
        step("RPV", hd)
        if hd < 6:
            step("RS", hd + 2)
        if hd == 4:
            step("GNmean", 0)
    step("GNvar", 0)
    step("GNmean", 1)
    step("GNvar", 1)
    step("GNout", 0)
    step("GNout", 1)
    for kt in range(2, 4):
        output(0, kt)
    for kt in range(3):
        output(1, kt)
    step("RAT", 0)
    output(1, 3)
    step("RAT", 1)
    refill(step, freed)
    for kt in range(4, 8):
        output(0, kt)
    step("tail", 0, C_INDEX)
    step("join", 0, C_INDEX)
    for kt in range(4, 6):
        output(1, kt)
    refill(step, freed, 1)
    walk_prep(step, 0, C_INDEX + 1)
    for kt in range(6, 8):
        output(1, kt)
    step("tail", 1, C_INDEX)
    step("join", 1, C_INDEX)
    refill(step, freed, 2)


def walk(eng, step):
    freed = []
    step("start",)
    step("turn", 0, 0)
    step("fill", 0, 1)
    step("parts", 0, 0)
    step("turn", 1, 0)
    step("fill", 1, 2)
    step("parts", 1, 0)
    step("fill", 3, 1)
    walk_phase(eng, MIX, lambda *a: step(*a, ph=MIX), 0, freed)
    walk_phase(eng, FFN1, lambda *a: step(*a, ph=FFN1), 4, freed)
    walk_attention(lambda *a: step(*a, ph=None), freed)
    walk_phase(eng, FFN2, lambda *a: step(*a, ph=FFN2), 4, freed)
    walk_phase(eng, FFN3, lambda *a: step(*a, ph=FFN3), 4, freed)
    walk_latent(lambda *a: step(*a, ph=None), freed)
    walk_phase(eng, FFN4, lambda *a: step(*a, ph=FFN4), 3, freed)


def two_pi_parts():
    parts, rest = [], 2 * math.pi
    for _ in range(5):
        unit = 2.0 ** (math.floor(math.log2(rest)) - 6)
        parts.append(math.floor(rest / unit) * unit)
        rest -= parts[-1]
    return parts


def build(nc, x_in, stream, feats_in, consts_in, table_in, pos_in, posts_in, out):
    with ExitStack() as ctx:
        def sem(name):
            return ctx.enter_context(nc.semaphore(name))

        def rows2(name):
            return [sem(f"{name}{t}") for t in range(2)]

        at = [(nc.sbuf_base + 63) // 64 * 64]

        def place(name, shape, dt, offset=None):
            size = int(np.prod(shape[1:])) * (2 if dt == BF16 else 4)
            if offset is None:
                offset = at[0]
                at[0] += (size + 63) // 64 * 64
            assert offset + size <= nc.sbuf_usable_end, (name, offset + size)
            return nc.alloc_sbuf_tensor_at(name, shape, dt, offset=offset)

        raw = place("raw", [P, RAW * CHUNK], F32)
        w_high = place("w_high", [P, RING * CHUNK], F32R)
        w_low = place("w_low", [P, RING * CHUNK], F32R)
        xTh = [place(f"xTh{t}", [P, KT, P], F32R) for t in range(2)]
        xTl = [place(f"xTl{t}", [P, KT, P], F32R) for t in range(2)]
        h = [place(f"h{t}", [P, D], F32) for t in range(2)]
        post = place("post", [P, D], F32)
        junk = [place(f"junk{t}", [P, D], BF16) for t in range(2)]
        consts = place("consts", [P, CONSTS], F32)
        feats = place("feats", [P, FEATS], F32)
        table = place("table", [P, TAB], F32)
        stat = place("stat", [P, 64], F32)
        pos_i = place("pos_i", [P, 2], I32)
        trig = place("trig", [P, 8, 64], F32)
        decay_t = place("decay_t", [P, 8, 16], F32)
        mx = [place(f"mx{t}", [P, 16], F32) for t in range(2)]
        negm = [place(f"negm{t}", [P, 16], F32) for t in range(2)]
        lsum = [place(f"lsum{t}", [P, 16], F32) for t in range(2)]
        esink = [place(f"esink{t}", [P, 16], F32) for t in range(2)]
        lrec = [place(f"lrec{t}", [P, 16], F32) for t in range(2)]
        gn = [place(f"gn{i}", [P, 4, 8], F32) for i in range(2)]
        nsink = place("nsink", [P, 16], F32)
        actT_at = at[0]
        aTh = [place(f"aTh{t}", [P, 2, P], F32R) for t in range(2)]
        aTl = [place(f"aTl{t}", [P, 2, P], F32R) for t in range(2)]
        latTh = place("latTh", [P, 3, P], F32R, actT_at)
        latTl = place("latTl", [P, 3, P], F32R, actT_at + 3 * P * 4)
        union = at[0]

        hg = [place(f"hg{t}", [P, D], F32) for t in range(2)]
        gate = [place(f"gate{t}", [P, 256], F32) for t in range(2)]
        act = [place(f"act{t}", [P, 256], F32) for t in range(2)]
        cv = [place(f"cv{i}", [P, SEQ + 2], F32) for i in range(3)]
        yT = [place(f"yT{t}", [P, P], F32) for t in range(2)]

        at[0] = union
        qT = [place(f"qT{t}", [P, PAIRS, P], F32) for t in range(2)]
        qkv = [place(f"qkv{t}", [P, 1536], F32) for t in range(2)]
        kT = place("kT", [P, 2, SEQ], F32)
        x2h = [place(f"x2h{t}", [P, KT, P], F32R) for t in range(2)]
        x2l = [place(f"x2l{t}", [P, KT, P], F32R) for t in range(2)]
        sm = [place(f"sm{i}", [P, 2, SEQ], F32) for i in range(2)]
        pr = [place(f"pr{i}", [P, 2, SEQ], F32) for i in range(2)]
        prT = [place(f"prT{i}", [P, 4 * P], F32) for i in range(2)]
        rtmp = [place(f"rtmp{i}", [P, 12, ROT_HALF], F32) for i in range(4)]

        at[0] = union
        mqT = place("mqT", [QK, MLA_HEADS, SEQ], F32)
        rqT = place("rqT", [P, 4, SEQ], F32, union)
        rkT = place("rkT", [P, 4, SEQ], F32, union + 4 * SEQ * 4)
        mkT_at = at[0]
        mkT = place("mkT", [QK, MLA_HEADS, SEQ], F32)
        lat_at = at[0]
        lat = [place(f"lat{t}", [P, LATENT], F32) for t in range(2)]
        ttmp = [place(f"ttmp{i}", [P, 8, RHALF], F32, lat_at + i * 1024 if i < 3 else None) for i in range(4)]
        mq_at = at[0]
        mq = place("mq", [P, MLA_HEADS, QK], F32)
        mk = place("mk", [P, MLA_HEADS, QK], F32)
        mo = [place(f"mo{t}", [P, 512], F32, mq_at + t * MLA_HEADS * QK * 4) for t in range(2)]
        mv = [place(f"mv{t}", [P, 512], F32) for t in range(2)]
        rqk_both = place("rqk", [P, 2, 1024], F32)
        rqk = [rqk_both[:, t, :] for t in range(2)]
        rv = [place(f"rv{t}", [P, 512], F32) for t in range(2)]
        p_at = at[0]
        mp = [place(f"mp{i}", [P, 2, SEQ], F32) for i in range(2)]
        sd = [place(f"sd{i}", [P, 2, SEQ], F32, p_at + i * 2 * SEQ * 4) for i in range(2)]
        latf = place("latf", [P, 3, P], F32, p_at)
        mpT_at = at[0]
        mpT = [place(f"mpT{i}", [P, 4 * P], F32) for i in range(2)]
        dm_at = [lat_at, lat_at + 1536] + [mkT_at + 1536 * i for i in range(5)] + [mpT_at + 2048]
        dm = [place(f"dm{i}", [P, 3 * P], F32, dm_at[i]) for i in range(8)]
        dtmp = [place(f"dtmp{i}", [P, P], F32) for i in range(2)]

        ident = consts[:, C_ID:C_ID + P]
        rope1 = consts[:, C_ROPE:C_ROPE + 32].rearrange("p (t c f) -> p t c f", t=2, c=2)
        mask = consts[:, C_MASK:C_MASK + SEQ]
        inv_freq = consts[:, C_INV:C_INV + 32]
        rel = consts[:, C_REL:C_REL + 4 * P]
        ss = [stat[:, 50 + 2 * t:52 + 2 * t] for t in range(2)]
        ms = [stat[:, 2 + t:3 + t] for t in range(2)]
        rr = [stat[:, 4 + t:5 + t] for t in range(2)]
        pss = [stat[:, 54 + 2 * t:56 + 2 * t] for t in range(2)]
        pms = [stat[:, 8 + t:9 + t] for t in range(2)]
        prr = [stat[:, 10 + t:11 + t] for t in range(2)]
        lss = [stat[:, 12 + 2 * t:14 + 2 * t] for t in range(2)]
        lms = [stat[:, 16 + 2 * t:18 + 2 * t] for t in range(2)]
        lrr = [stat[:, 20 + 2 * t:22 + 2 * t] for t in range(2)]
        half_neg = stat[:, 24:32]
        one_neg = stat[:, 32:48]
        pos_f = stat[:, 48:50]
        ang, kang, tang, cang, cosT, sinT = (trig[:, i, :] for i in range(6))
        cos2 = cosT.rearrange("p (t f) -> p t f", t=2)
        sin2 = sinT.rearrange("p (t f) -> p t f", t=2)
        lg_r2, lg_ax, lg_e, lg_s, lg_z, lg_p, lg = (decay_t[:, i, :] for i in range(7))

        pD = [ctx.enter_context(nc.psum_tensor(f"pD{t}", [P, D], F32)) for t in range(2)]
        pG = [ctx.enter_context(nc.psum_tensor(f"pG{t}", [P, 512], F32)) for t in range(2)]
        pT = [ctx.enter_context(nc.psum_tensor(f"pT{t}", [P, 512], F32)) for t in range(2)]

        w_loaded = [sem(f"w_loaded{i}") for i in range(RAW)]
        w_high_done = sem("w_high_done")
        w_split = sem("w_split")
        w_freed = sem("w_freed")
        x_loaded = rows2("x_loaded")
        feats_loaded, ident_loaded, consts_loaded = sem("feats_loaded"), sem("ident_loaded"), sem("consts_loaded")
        table_loaded, pos_loaded = sem("table_loaded"), sem("pos_loaded")
        post_loaded = sem("post_loaded")
        out_ready, out_stored = rows2("out_ready"), sem("out_stored")
        h_ready, ss_ready, r_ready = (rows2(n) for n in ("h_ready", "ss_ready", "r_ready"))
        pss_ready, pr_ready = (rows2(n) for n in ("pss_ready", "pr_ready"))
        hT_psum, hg_ready, xh_ready, xT_ready = (rows2(n) for n in ("hT_psum", "hg_ready", "xh_ready", "xT_ready"))
        g_done0, d_done0 = sem("g_done0"), sem("d_done0")
        d_half = rows2("d_half")
        gate_ready, act_ready, actT_psum = (rows2(n) for n in ("gate_ready", "act_ready", "actT_psum"))
        cuT_ready, conv_done, ah_ready, aT_ready = (rows2(n) for n in ("cuT_ready", "conv_done", "ah_ready", "aT_ready"))
        halo_zero = sem("halo_zero")
        q_done0 = sem("q_done0")
        qkv_ready, rope_done, qkT_psum = rows2("qkv_ready"), sem("rope_done"), rows2("qkT_psum")
        kqT_act, kqT_dve = rows2("kqT_act"), rows2("kqT_dve")
        s_done, sm_ready, p_ready = sem("s_done"), sem("sm_ready"), sem("p_ready")
        pT_psum, pT_ready, pv_done = sem("pT_psum"), sem("pT_ready"), sem("pv_done")
        es_arg, es_ready, ao_ready = (rows2(n) for n in ("es_arg", "es_ready", "ao_ready"))
        aoT_psum, aoh_ready, aoT_ready = (rows2(n) for n in ("aoT_psum", "aoh_ready", "aoT_ready"))
        nsink_ready = sem("nsink_ready")
        x_done0, u_done0 = sem("x_done0"), sem("u_done0")
        x_out, lat_ss, lr_ready = (rows2(n) for n in ("x_out", "lat_ss", "lr_ready"))
        latT_psum, latf_ready, lath_ready, latT_ready = (rows2(n) for n in ("latT_psum", "latf_ready", "lath_ready", "latT_ready"))
        u_out, mqk_ready, mT_psum = (rows2(n) for n in ("u_out", "mqk_ready", "mT_psum"))
        mqT_ready, mkT_ready = rows2("mqT_ready"), rows2("mkT_ready")
        ms_psum, mmax_ready, mp_ready = sem("ms_psum"), sem("mmax_ready"), sem("mp_ready")
        mpT_psum, mpT_ready, mpv_done = sem("mpT_psum"), sem("mpT_ready"), sem("mpv_done")
        mo_ready = rows2("mo_ready")
        rrope_done = rows2("rrope_done")
        rT_psum, rqT_ready, rkT_ready = rows2("rT_psum"), rows2("rqT_ready"), rows2("rkT_ready")
        dm_exp, dm_ready, rot_part = sem("dm_exp"), sem("dm_ready"), sem("rot_part")
        rs_psum, sd_ready, rpv_done = sem("rs_psum"), sem("sd_ready"), sem("rpv_done")
        rgate, silu_ready = rows2("rgate"), sem("silu_ready")
        gn_var, gn_r, ro_ready = sem("gn_var"), sem("gn_r"), sem("ro_ready")
        catT_psum, cath_ready, catT_ready = (rows2(n) for n in ("catT_psum", "cath_ready", "catT_ready"))
        trig_ready, sincos_ready = sem("trig_ready"), sem("sincos_ready")
        pool_chain, ve_chain = sem("pool_chain"), sem("ve_chain")
        ax_ready, e_ready, lg_ready = sem("ax_ready"), sem("e_ready"), sem("lg_ready")
        pows_ready = sem("pows_ready")

        def slot(c):
            return (c + 1) % RING * CHUNK

        def xT_base(p):
            return 2 * p + (2 if p > B_INDEX else 0)

        def freed_by(ph, b, out_part):
            return ph.d_chunk(b) + ph.kd if out_part else ph.g_chunk(b) + ph.cg

        def branch_done(eng, t, k, half):
            if half == 0:
                eng.wait_ge(d_half[t], k + 1)
            elif t == 0:
                eng.wait_ge(d_done0, k + 1)
            else:
                eng.wait_ge(w_freed, [FFN1.first_chunk, B_FIRST, FFN2.first_chunk, FFN3.first_chunk,
                                      C_FIRST, FFN4.first_chunk, N_CHUNKS][k])

        def turned_bank(v):
            return pT[1][:] if v % 2 else pD[v // 8][:, 0:512]

        def ao_bank(t, half):
            return ((pD[0][:, 0:512], pD[0][:, 512:1024]), (pG[1][:], pT[0][:]))[t][half]

        def proj_done(eng, j, t):
            if t == 0:
                eng.wait_ge(q_done0, j + 1)
            else:
                eng.wait_ge(w_freed, B_FIRST + 4 * (j + 1))

        def x_product(eng, i, t):
            if t == 0:
                eng.wait_ge(x_done0, i + 1)
            else:
                eng.wait_ge(w_freed, C_X[i] + 4)

        block = ctx.enter_context(nc.Block())

        @block.sync
        def _(sp):
            sp.dma_start(h[0][:], x_in[0:P, :]).then_inc(x_loaded[0], 16)
            sp.dma_start(ident, consts_in[:, C_ID:C_ID + P]).then_inc(ident_loaded, 16)
            sp.dma_start(feats[:], feats_in).then_inc(feats_loaded, 16)
            for c in range(RAW):
                sp.dma_start(raw[:, c * CHUNK:(c + 1) * CHUNK], stream[c]).then_inc(w_loaded[c], 16)
                if c == 0:
                    sp.dma_start(h[1][:], x_in[P:2 * P, :]).then_inc(x_loaded[1], 16)
            turns = N_CHUNKS // RAW
            with sp.Fori(1, turns) as turn:
                for i in range(RAW):
                    sp.wait_ge(w_split, turn * RAW + (i - RAW + 1))
                    sp.dma_start(raw[:, i * CHUNK:(i + 1) * CHUNK],
                                 stream[bass.ds(turn * RAW + i, 1)].rearrange("o p n -> p (o n)")
                                 ).then_inc(w_loaded[i], 16)
            for c in range(turns * RAW, N_CHUNKS):
                sp.wait_ge(w_split, c - RAW + 1)
                i = c % RAW
                sp.dma_start(raw[:, i * CHUNK:(i + 1) * CHUNK], stream[c]).then_inc(w_loaded[i], 16)
            for t in range(2):
                for half in range(2):
                    sp.wait_ge(out_ready[t], half + 1)
                    sp.dma_start(out[P * t:P * (t + 1), 512 * half:512 * half + 512],
                                 hg[t][:, 512 * half:512 * half + 512]).then_inc(out_stored, 16)
            sp.wait_ge(out_stored, 64)

        @block.gpsimd
        def _(pool):
            links = [0]

            def link(ins):
                links[0] += 1
                ins.then_inc(pool_chain, 1)
                pool.wait_ge(pool_chain, links[0])

            def start(ph):
                pool.memset(half_neg, -0.5).then_inc(pows_ready, 1)
                pool.memset(one_neg, -1.0).then_inc(pows_ready, 1)
                for i in range(3):
                    pool.memset(cv[i][:, 0:2], 0.0).then_inc(halo_zero, 1)
                pool.wait_ge(pows_ready, 2)

            def load_tables():
                pool.wait_ge(w_loaded[2], 32)
                pool.dma_start(table[:], table_in).then_inc(table_loaded, 16)
                pool.dma_start(consts[:, P:CONSTS], consts_in[:, P:CONSTS]).then_inc(consts_loaded, 16)
                pool.dma_start(pos_i[:], pos_in).then_inc(pos_loaded, 16)
                pool.dma_start(post[:], posts_in[0].partition_broadcast(P)).then_inc(post_loaded, 16)

            def tables():
                pool.wait_ge(pos_loaded, 16)
                pool.wait_ge(consts_loaded, 16)
                link(pool.tensor_copy(pos_f, pos_i[:]))
                for t in range(2):
                    link(pool.tensor_scalar(ang[:, 32 * t:32 * t + 32], inv_freq, pos_f[:, t:t + 1], None, ALU.mult))
                magic = 1.5 * 2.0 ** 23
                for unit in (4096.0, 1.0):
                    link(pool.tensor_scalar(kang, ang, 1.0 / (unit * 2 * math.pi), magic, ALU.mult, ALU.add))
                    link(pool.tensor_scalar(kang, kang, magic, None, ALU.subtract))
                    for part in two_pi_parts():
                        link(pool.tensor_scalar(tang, kang, -part * unit, None, ALU.mult))
                        link(pool.tensor_tensor(ang, ang, tang, ALU.add))
                link(pool.tensor_scalar(cang, ang, math.pi / 2, None, ALU.add))
                link(pool.tensor_scalar(tang, cang, math.pi, -2 * math.pi, ALU.is_gt, ALU.mult))
                link(pool.tensor_tensor(cang, cang, tang, ALU.add))
                link(pool.tensor_scalar(cang, cang, 3.1415925, -3.1415925, ALU.min, ALU.max))
                pool.tensor_scalar(ang, ang, 3.1415925, -3.1415925, ALU.min, ALU.max).then_inc(trig_ready, 1)
                pool.wait_ge(table_loaded, 16)
                dec = table[:, T_DECAY:T_DECAY + 16]
                link(pool.tensor_scalar(lg_r2, dec, -1.0, 0.0, ALU.mult, ALU.max))
                link(pool.tensor_scalar(lg_ax, dec, 0.0, None, ALU.max))
                pool.tensor_tensor(lg_ax, lg_ax, lg_r2, ALU.add).then_inc(ax_ready, 1)

            def log_decays():
                pool.wait_ge(e_ready, 1)
                link(pool.tensor_scalar(lg_s, lg_e, 2.0, None, ALU.add))
                link(pool.tensor_tensor(lg_s, lg_s, one_neg, ALU.pow))
                link(pool.tensor_tensor(lg_s, lg_s, lg_e, ALU.mult))
                link(pool.tensor_tensor(lg_z, lg_s, lg_s, ALU.mult))
                link(pool.tensor_scalar(lg_p, lg_z, 1.0 / 17, 1.0 / 15, ALU.mult, ALU.add))
                for n in (13, 11, 9, 7, 5, 3, 1):
                    link(pool.tensor_tensor(lg_p, lg_p, lg_z, ALU.mult))
                    link(pool.tensor_scalar(lg_p, lg_p, 1.0 / n, None, ALU.add))
                link(pool.tensor_tensor(lg_p, lg_p, lg_s, ALU.mult))
                link(pool.tensor_scalar(lg_p, lg_p, 2.0, None, ALU.mult))
                link(pool.tensor_tensor(lg_p, lg_p, lg_r2, ALU.add))
                pool.tensor_scalar(lg, lg_p, -1.0, None, ALU.mult).then_inc(lg_ready, 1)

            def parts(t, p, ph):
                pool.wait_ge(ss_ready[t], 2 * (p + 1))
                link(pool.tensor_scalar(ms[t], ss[t][:, 0:1], ss[t][:, 1:2], EPS, ALU.add, ALU.add))
                pool.tensor_tensor(rr[t], ms[t], half_neg[:, 0:1], ALU.pow).then_inc(r_ready[t], 1)
                if t == 1 and p == 0:
                    load_tables()
                    tables()
                if t == 1 and p == B_INDEX + 1:
                    log_decays()

            def tail(t, k, ph):
                if k < POST_NORMS:
                    pool.wait_ge(pss_ready[t], 2 * (k + 1))
                    link(pool.tensor_scalar(pms[t], pss[t][:, 0:1], pss[t][:, 1:2], EPS, ALU.add, ALU.add))
                    pool.tensor_tensor(prr[t], pms[t], half_neg[:, 0:1], ALU.pow).then_inc(pr_ready[t], 1)
                    if t == 1:
                        pool.wait_ge(h_ready[0], 2 * (k + 1))
                        pool.wait_ge(h_ready[1], 2 * (k + 1))
                        pool.dma_start(post[:], posts_in[k + 1].partition_broadcast(P)).then_inc(post_loaded, 16)

            def LAT(t, ph):
                pool.wait_ge(lat_ss[t], 2)
                link(pool.tensor_scalar(lms[t][:, 0:1], lss[t][:, 0:1], 1.0 / Q_RANK, EPS, ALU.mult, ALU.add))
                link(pool.tensor_scalar(lms[t][:, 1:2], lss[t][:, 1:2], 1.0 / KV_RANK, EPS, ALU.mult, ALU.add))
                pool.tensor_tensor(lrr[t], lms[t], half_neg[:, 0:2], ALU.pow).then_inc(lr_ready[t], 1)

            def U(t, ph):
                if t == 1:
                    pool.wait_ge(latT_psum[1], 1)
                    pool.wait_ge(mqk_ready[1], 2)

            def RROPE(t, part, ph):
                pool.wait_ge(x_out[t], 2 + part)
                z = rqk[t][:, 512 * part:512 * part + 512].rearrange("p (a f) -> p a f", f=HD)
                co, si = (x[:, t, :].unsqueeze(1).broadcast_to([P, 8, RHALF]) for x in (cos2, sin2))
                x1, x2 = z[:, :, 0:RHALF], z[:, :, RHALF:HD]
                if t or part:
                    pool.wait_ge(rrope_done[t if part else 0], 1 if part else 2)
                pool.tensor_tensor(ttmp[0][:], x1, co, ALU.mult).then_inc(rot_part, 1)
                pool.tensor_tensor(ttmp[1][:], x2, si, ALU.mult).then_inc(rot_part, 1)
                pool.tensor_tensor(ttmp[2][:], x1, si, ALU.mult).then_inc(rot_part, 1)
                pool.tensor_tensor(ttmp[3][:], x2, co, ALU.mult).then_inc(rot_part, 1)
                pool.wait_ge(rot_part, 4 * (2 * t + part + 1))
                pool.tensor_tensor(x1, ttmp[0][:], ttmp[1][:], ALU.subtract)
                pool.tensor_tensor(x2, ttmp[2][:], ttmp[3][:], ALU.add).then_inc(rrope_done[t], 1)

            def decay(hd, ph):
                pool.wait_ge(dm_exp, 3 * (hd + 1))
                pool.tensor_tensor(dm[hd][:, P:2 * P], dm[hd][:, P:2 * P], dtmp[hd % 2][:], ALU.mult).then_inc(dm_ready, 1)

            def GNvar(part, ph):
                g = gn[part]
                pool.wait_ge(gn_var, part + 1)
                link(pool.tensor_scalar(g[:, 2, :], g[:, 1, :], 1.0 / HD, EPS, ALU.mult, ALU.add))
                pool.tensor_tensor(g[:, 3, :], g[:, 2, :], half_neg, ALU.pow).then_inc(gn_r, 1)

            def last(t, ph):
                parts(t, LAST, ph)

            steps = {f.__name__: f for f in (start, parts, last, tail, LAT, U, RROPE, decay, GNvar)}
            in_loop = ("G", "D", "T", "Y", "R")

            def step(name, *args, ph=None):
                if name in steps:
                    steps[name](*args, ph)
            walk(NoLoop(), lambda name, *a, ph=None: None if name in in_loop else step(name, *a, ph=ph))

        @block.scalar
        def _(sc):
            def split_high(c, static, shift):
                sc.wait_ge(w_loaded[static % RAW], 16 * (static // RAW + 1) + shift * (16 * RING // RAW))
                if static >= RING:
                    sc.wait_ge(w_freed, c - RING + 1)
                sc.activation(w_high[:, slot(static):slot(static) + CHUNK],
                              raw[:, static % RAW * CHUNK:(static % RAW + 1) * CHUNK], ACT.Copy).then_inc(w_high_done, 1)

            def refill(first, n, shift, ph):
                for c in range(first + RING, first + RING + n):
                    if c < N_CHUNKS:
                        split_high(c + shift * RING, c, shift)

            def start(ph):
                sc.preload_act_table(ACT.Silu)

            def exp_table(ph):
                sc.preload_act_table(ACT.Exp)

            def fill(first, n, ph):
                for c in range(first, first + n):
                    split_high(c, c, 0)

            def square(t, p, half):
                if p == 0:
                    sc.wait_ge(x_loaded[t], 16)
                else:
                    sc.wait_ge(h_ready[t], 2 * (p - 1) + half + 1)
                cols = slice(512 * half, 512 * half + 512)
                sc.activation(junk[t][:, cols], h[t][:, cols], ACT.Square, scale=D ** -0.5,
                              accum_out=ss[t][:, half:half + 1]).then_inc(ss_ready[t], 1)

            def high_parts(t, high, n):
                for half in range(2):
                    sc.wait_ge(hg_ready[t], n + half + 1)
                    sc.activation(high[t][:, 4 * half:4 * half + 4, :].rearrange("p k r -> p (k r)"),
                                  hg[t][:, 512 * half:512 * half + 512], ACT.Copy).then_inc(xh_ready[t], 1)

            def turn(t, p, ph):
                if p > 0:
                    square(t, p, 0)

            def parts(t, p, ph):
                high_parts(t, xTh, xT_base(p))
                for half in range(0 if p == 0 else 1, 2):
                    square(t, p, half)

            def second(t, ph):
                high_parts(t, x2h, xT_base(B_INDEX) + 2)

            def last(t, ph):
                for half in range(2):
                    square(t, LAST, half)

            def tail(t, k, ph):
                if k < POST_NORMS:
                    for half in range(2):
                        branch_done(sc, t, k, half)
                        cols = slice(512 * half, 512 * half + 512)
                        sc.activation(junk[t][:, cols], pD[t][:, cols], ACT.Square, scale=D ** -0.5,
                                      accum_out=pss[t][:, half:half + 1]).then_inc(pss_ready[t], 1)

            def G(t, b, shift, ph):
                n = ph.first_block + b + 1 + shift * (RING // (ph.cg + ph.kd))
                if t == 1:
                    sc.wait_ge(w_freed, freed_by(ph, b, False) + shift * RING)
                else:
                    sc.wait_ge(g_done0, n)
                if b == 0:
                    sc.wait_ge(r_ready[t], ph.index + 1)
                sc.activation(gate[t][:], pG[t][:, 0:256], ACT.Copy if ph.mixer else ACT.Silu,
                              scale=rr[t]).then_inc(gate_ready[t], 1)

            def T(t, b, shift, ph):
                n = ph.first_block + b + 1 + shift * (RING // (ph.cg + ph.kd))
                sc.wait_ge(actT_psum[t], n)
                if ph.mixer:
                    if b < 3 and t == 0:
                        sc.wait_ge(halo_zero, b + 1)
                    if t == 0 and b >= 3:
                        sc.wait_ge(conv_done[1], 4 * (b - 2))
                    sc.activation(cv[b % 3][:, 2 + P * t:2 + P * (t + 1)], pT[t][:, P:2 * P], ACT.Copy).then_inc(cuT_ready[t], 1)
                else:
                    sc.activation(aTh[t][:].rearrange("p k r -> p (k r)"), pT[t][:, 0:256], ACT.Copy).then_inc(ah_ready[t], 1)
                if ph is FFN1 and t == 0 and b == 0:
                    sc.wait_ge(trig_ready, 1)
                    sc.activation(sinT, ang, ACT.Sin).then_inc(sincos_ready, 1)
                    sc.activation(cosT, cang, ACT.Sin).then_inc(sincos_ready, 1)

            def Y(t, b, shift, ph):
                sc.wait_ge(conv_done[t], 4 * (b + 1))
                sc.activation(aTh[t][:, 0, :], yT[t][:], ACT.Copy).then_inc(ah_ready[t], 1)

            def proj(j, t, c, ph):
                if c == 3:
                    proj_done(sc, j, t)
                    if j == 0:
                        sc.wait_ge(r_ready[t], B_INDEX + 1)
                    src = pG[t][:] if j == 2 else pD[t][:, 512 * j:512 * j + 512]
                    sc.activation(qkv[t][:, 512 * j:512 * j + 512], src, ACT.Copy, scale=rr[t]).then_inc(qkv_ready[t], 1)

            def QKT(t, part, ph):
                sc.wait_ge(qkT_psum[t], 2 * part + 1)
                if part == 0:
                    sc.activation(kT[:, :, P * t:P * (t + 1)], pD[t][:, 0:256].rearrange("p (a r) -> p a r", a=2),
                                  ACT.Copy).then_inc(kqT_act[t], 1)
                else:
                    sc.activation(qT[t][:, 4:8, :].rearrange("p a r -> p (a r)"), pG[t][:], ACT.Copy).then_inc(kqT_act[t], 1)

            def E(v, ph):
                t, m, half = v // 8, v % 8 // 2, v % 2
                keys = slice(P * (1 - t), SEQ)
                sc.wait_ge(sm_ready, v + 1)
                if v >= 2:
                    sc.wait_ge(pT_psum, v - 1)
                for x in range(2):
                    col = 2 * (2 * m + x) + half
                    sc.activation(pr[v % 2][:, x, keys], sm[v % 2][:, x, keys], ACT.Exp, bias=negm[t][:, col:col + 1],
                                  accum_out=lsum[t][:, col:col + 1]).then_inc(p_ready, 1)

            def AO(quarter, ph):
                t, half = quarter // 2, quarter % 2
                sc.wait_ge(es_arg[t], half + 1)
                cols = slice(8 * half, 8 * half + 8)
                sc.activation(esink[t][:, cols], esink[t][:, cols], ACT.Exp).then_inc(es_ready[t], 1)
                if t == 0 and half == 0:
                    sc.wait_ge(ax_ready, 1)
                    sc.activation(lg_e, lg_ax, ACT.Exp, scale=-1.0).then_inc(e_ready, 1)

            def AT(t, half, ph):
                sc.wait_ge(aoT_psum[t], half + 1)
                sc.activation(xTh[t][:, 4 * half:4 * half + 4, :].rearrange("p k r -> p (k r)"),
                              ao_bank(t, half), ACT.Copy).then_inc(aoh_ready[t], 1)

            def X(i, t, c, ph):
                if c == 3 and i < 4:
                    x_product(sc, i, t)
                    if i == 0:
                        sc.wait_ge(r_ready[t], C_INDEX + 1)
                    dst = [lat[t][:], rqk[t][:, 0:512], rqk[t][:, 512:1024], rv[t][:]][i]
                    sc.activation(dst, pD[t][:, 0:LATENT if i == 0 else 512], ACT.Copy, scale=rr[t]).then_inc(x_out[t], 1)

            def LAT(t, ph):
                sc.wait_ge(x_out[t], 1)
                sc.activation(junk[t][:, 0:Q_RANK], lat[t][:, 0:Q_RANK], ACT.Square, accum_out=lss[t][:, 0:1]).then_inc(lat_ss[t], 1)
                sc.activation(junk[t][:, Q_RANK:Q_RANK + KV_RANK], lat[t][:, Q_RANK:Q_RANK + KV_RANK], ACT.Square,
                              accum_out=lss[t][:, 1:2]).then_inc(lat_ss[t], 1)
                sc.wait_ge(latf_ready[t], 1)
                if t == 1:
                    sc.wait_ge(u_done0, 1)
                sc.activation(latTh[:], latf[:], ACT.Copy).then_inc(lath_ready[t], 1)

            def U(t, ph):
                if t == 1:
                    sc.wait_ge(w_freed, C_U + 3)
                    sc.wait_ge(mT_psum[0], 2)
                else:
                    sc.wait_ge(u_done0, 1)
                sc.wait_ge(lr_ready[t], 1)
                for half in range(2):
                    sc.activation(mq[:, 4 * half:4 * half + 4, :], (pG, pT)[half][0][:, 0:384].rearrange("p (a f) -> p a f", a=4),
                                  ACT.Copy, scale=lrr[t][:, 0:1]).then_inc(u_out[t], 1)
                sc.activation(mk[:, :, 0:NOPE], pG[1][:].rearrange("p (a f) -> p a f", a=8), ACT.Copy,
                              scale=lrr[t][:, 1:2]).then_inc(u_out[t], 1)
                sc.activation(mv[t][:], pT[1][:], ACT.Copy, scale=lrr[t][:, 1:2]).then_inc(u_out[t], 1)

            def MT(t, ph):
                sc.wait_ge(mT_psum[t], 1)
                for half in range(2):
                    sc.activation(mqT[:, 4 * half:4 * half + 4, P * t:P * (t + 1)],
                                  (pG, pT)[half][0][0:QK, :].rearrange("p (a r) -> p a r", a=4), ACT.Copy).then_inc(mqT_ready[t], 1)

            def ME(v, ph):
                t, j = v // 4, v % 4
                sc.wait_ge(mmax_ready, v + 1)
                if v >= 2:
                    sc.wait_ge(mpT_psum, v - 1)
                for x in range(2):
                    hd = 2 * j + x
                    sc.activation(mp[v % 2][:, x, :], pG[v % 2][:, SEQ * x:SEQ * (x + 1)], ACT.Exp, bias=negm[t][:, hd:hd + 1],
                                  scale=MLA_SCALE, accum_out=lsum[t][:, hd:hd + 1]).then_inc(mp_ready, 1)

            def RT(t, ph):
                sc.wait_ge(rT_psum[t], 1)
                sc.activation(rqT[:, :, P * t:P * (t + 1)], pG[0][:].rearrange("p (a r) -> p a r", a=4),
                              ACT.Copy).then_inc(rqT_ready[t], 1)

            def decay(hd, ph):
                f, b = lg[:, hd:hd + 1], lg[:, 8 + hd:9 + hd]
                if hd == 0:
                    sc.wait_ge(lg_ready, 1)
                    sc.wait_ge(rrope_done[1], 2)
                    sc.wait_ge(ms_psum, 8)
                if hd == 7:
                    sc.wait_ge(mpv_done, 8)
                if hd >= 2:
                    sc.wait_ge(dm_ready, hd - 1)
                sc.activation(dm[hd][:, P:3 * P], rel[:, 0:2 * P], ACT.Exp, scale=f).then_inc(dm_exp, 1)
                sc.activation(dtmp[hd % 2][:], rel[:, 2 * P:3 * P], ACT.Exp, scale=b).then_inc(dm_exp, 1)
                sc.activation(dm[hd][:, 0:P], rel[:, 3 * P:4 * P], ACT.Exp, scale=b).then_inc(dm_exp, 1)

            def gate_r(t, ph):
                x_product(sc, 4, t)
                sc.wait_ge(rT_psum[t], 2)
                sc.activation(rqk[t][:, 512:1024], pD[t][:, 0:512], ACT.Copy, scale=rr[t]).then_inc(rgate[t], 1)

            def silu(ph):
                for t in range(2):
                    sc.wait_ge(rgate[t], 1)
                sc.activation(rqk_both[:, :, 512:1024], rqk_both[:, :, 512:1024], ACT.Silu).then_inc(silu_ready, 1)

            def MAT(t, ph):
                sc.wait_ge(catT_psum[t], 1)
                sc.activation(xTh[t][:, 0:4, :].rearrange("p k r -> p (k r)"), pD[t][:, 512:1024], ACT.Copy).then_inc(cath_ready[t], 1)

            def RAT(t, ph):
                sc.wait_ge(catT_psum[t], 2)
                sc.activation(xTh[t][:, 4:8, :].rearrange("p k r -> p (k r)"), pG[t][:], ACT.Copy).then_inc(cath_ready[t], 1)

            steps = dict(start=start, exp_table=exp_table, fill=fill, R=refill, turn=turn, parts=parts, second=second, last=last,
                         tail=tail, G=G, T=T, Y=Y, proj=proj, QKT=QKT, E=E, AO=AO, AT=AT, X=X, LAT=LAT, U=U, MT=MT, ME=ME, RT=RT, decay=decay, gate=gate_r, silu=silu, MAT=MAT, RAT=RAT)
            walk(sc, lambda name, *a, ph=None: steps[name](*a, ph) if name in steps else None)

        @block.vector
        def _(ve):
            links = [0]

            def chain(ins):
                links[0] += 1
                return ins.then_inc(ve_chain, 1)

            def joined():
                ve.wait_ge(ve_chain, links[0])

            def split_low(c, static):
                ve.wait_ge(w_high_done, c + 1)
                ve.tensor_tensor(w_low[:, slot(static):slot(static) + CHUNK],
                                 raw[:, static % RAW * CHUNK:(static % RAW + 1) * CHUNK],
                                 w_high[:, slot(static):slot(static) + CHUNK].bitcast(F32), ALU.subtract).then_inc(w_split, 1)

            def refill(first, n, shift, ph):
                for c in range(first + RING, first + RING + n):
                    if c < N_CHUNKS:
                        split_low(c + shift * RING, c)

            def start(ph):
                ve.wait_ge(feats_loaded, 16)

            def sinks():
                ve.wait_ge(consts_loaded, 16)
                ve.wait_ge(table_loaded, 16)
                ve.tensor_scalar(nsink[:], table[:, T_SINK:T_SINK + 16], -1.0, None, ALU.mult).then_inc(nsink_ready, 1)

            def fill(first, n, ph):
                for c in range(first, first + n):
                    split_low(c, c)

            def gained(t, col, n):
                for half in range(2):
                    ve.wait_ge(hT_psum[t], n + half + 1)
                    g = feats[:, col + 4 * half:col + 4 * half + 4].unsqueeze(2).broadcast_to([P, 4, P])
                    ve.tensor_tensor(hg[t][:, 512 * half:512 * half + 512].rearrange("p (k r) -> p k r", k=4),
                                     (pG, pT)[half][t][:].rearrange("p (k r) -> p k r", k=4), g,
                                     ALU.mult).then_inc(hg_ready[t], 1)

            def low_parts(t, high, low, n):
                for half in range(2):
                    ve.wait_ge(xh_ready[t], n + half + 1)
                    ve.tensor_tensor(low[t][:, 4 * half:4 * half + 4, :].rearrange("p k r -> p (k r)"),
                                     hg[t][:, 512 * half:512 * half + 512],
                                     high[t][:, 4 * half:4 * half + 4, :].rearrange("p k r -> p (k r)").bitcast(F32),
                                     ALU.subtract).then_inc(xT_ready[t], 1)

            def turn(t, p, ph):
                if p == 1 and t == 0:
                    sinks()
                gained(t, GAIN[p], 2 * p)

            def parts(t, p, ph):
                low_parts(t, xTh, xTl, xT_base(p))

            def second(t, ph):
                ve.wait_ge(xT_ready[t], xT_base(B_INDEX) + 2)
                gained(t, GAIN["q"], 2 * B_INDEX)
                low_parts(t, x2h, x2l, xT_base(B_INDEX) + 2)

            def last(t, ph):
                ve.wait_ge(r_ready[t], LAST + 1)
                ve.wait_ge(post_loaded, 16 * (POST_NORMS + 1))
                for half in range(2):
                    cols = slice(512 * half, 512 * half + 512)
                    ve.scalar_tensor_tensor(hg[t][:, cols], h[t][:, cols], rr[t], post[:, cols], ALU.mult, ALU.mult).then_inc(out_ready[t], 1)

            def tail(t, k, ph):
                if k < POST_NORMS:
                    ve.wait_ge(post_loaded, 16 * (k + 1))
                    for half in range(2):
                        cols = slice(512 * half, 512 * half + 512)
                        ve.wait_ge(pss_ready[t], 2 * k + half + 1)
                        chain(ve.tensor_tensor(hg[t][:, cols], pD[t][:, cols], post[:, cols], ALU.mult))

            def join(t, k, ph):
                if k < POST_NORMS:
                    joined()
                    ve.wait_ge(pr_ready[t], k + 1)
                for half in range(2):
                    cols = slice(512 * half, 512 * half + 512)
                    if k >= POST_NORMS:
                        branch_done(ve, t, k, half)
                    branch, factor = (hg, prr[t]) if k < POST_NORMS else (pD, 1.0 if k == C_INDEX else 0.5)
                    ve.scalar_tensor_tensor(h[t][:, cols], branch[t][:, cols], factor, h[t][:, cols],
                                            ALU.mult, ALU.add).then_inc(h_ready[t], 1)

            def G(t, b, shift, ph):
                n = ph.first_block + b + 1 + shift * (RING // (ph.cg + ph.kd))
                ve.wait_ge(gate_ready[t], n)
                if ph.mixer:
                    ve.scalar_tensor_tensor(act[t][:, 0:P], pG[t][:, 256:384], rr[t], gate[t][:, P:2 * P],
                                            ALU.mult, ALU.mult).then_inc(act_ready[t], 1)
                else:
                    ve.scalar_tensor_tensor(act[t][:], pG[t][:, 256:512], rr[t], gate[t][:],
                                            ALU.mult, ALU.mult).then_inc(act_ready[t], 1)

            def T(t, b, shift, ph):
                n = ph.first_block + b + 1 + shift * (RING // (ph.cg + ph.kd))
                if ph.mixer:
                    ve.wait_ge(cuT_ready[t], b + 1)
                    taps = [feats[:, CONV + 3 * b + w:CONV + 3 * b + w + 1] for w in range(3)]
                    src = [cv[b % 3][:, P * t + w:P * t + w + P] for w in range(3)]
                    done = 4 * b
                    ve.tensor_scalar(yT[t][:], src[0], taps[0], None, ALU.mult).then_inc(conv_done[t], 1)
                    for w in (1, 2):
                        ve.wait_ge(conv_done[t], done + w)
                        ve.scalar_tensor_tensor(yT[t][:], src[w], taps[w], yT[t][:], ALU.mult, ALU.add).then_inc(conv_done[t], 1)
                    ve.wait_ge(conv_done[t], done + 3)
                    ve.tensor_tensor(yT[t][:], pT[t][:, 0:P], yT[t][:], ALU.mult).then_inc(conv_done[t], 1)
                else:
                    ve.wait_ge(ah_ready[t], n)
                    ve.tensor_tensor(aTl[t][:].rearrange("p k r -> p (k r)"), pT[t][:, 0:256],
                                     aTh[t][:].rearrange("p k r -> p (k r)").bitcast(F32), ALU.subtract).then_inc(aT_ready[t], 1)

            def Y(t, b, shift, ph):
                ve.wait_ge(ah_ready[t], ph.first_block + b + 1)
                ve.tensor_tensor(aTl[t][:, 0, :], yT[t][:], aTh[t][:, 0, :].bitcast(F32), ALU.subtract).then_inc(aT_ready[t], 1)

            def rope(t, part, ph):
                ve.wait_ge(qkv_ready[t], 2 + part)
                if part or t:
                    ve.wait_ge(rope_done, 2 * (2 * t + part))
                n = 8 if part else 12
                qk = qkv[t][:, (1024 if part else 256):(1536 if part else 1024)].rearrange("p (a f) -> p a f", f=HD)
                a, b = qk[:, :, 0:ROT_HALF], qk[:, :, ROT_HALF:2 * ROT_HALF]
                co, si = (rope1[:, t, i, :].unsqueeze(1).broadcast_to([P, n, ROT_HALF]) for i in range(2))
                tmp = [x[:, 0:n, :] for x in rtmp]
                for i, (u, w) in enumerate(((a, co), (b, si), (b, co), (a, si))):
                    chain(ve.tensor_tensor(tmp[i], u, w, ALU.mult))
                joined()
                ve.tensor_tensor(a, tmp[0], tmp[1], ALU.subtract).then_inc(rope_done, 1)
                ve.tensor_tensor(b, tmp[2], tmp[3], ALU.add).then_inc(rope_done, 1)

            def QKT(t, part, ph):
                if part == 0:
                    ve.wait_ge(qkT_psum[t], 2)
                    ve.tensor_copy(qT[t][:, 0:4, :].rearrange("p a r -> p (a r)"), pD[t][:, 512:1024]).then_inc(kqT_dve[t], 1)

            def S(v, ph):
                t, m, half = v // 8, v % 8 // 2, v % 2
                keys = slice(P * (1 - t), SEQ)
                nk = P * (1 + t)
                bank = (pT, pG)[half][0]
                ve.wait_ge(s_done, v + 1)
                if v >= 2:
                    ve.wait_ge(p_ready, 2 * (v - 1))
                for x in range(2):
                    col = 2 * (2 * m + x) + half
                    chain(ve.tensor_tensor_reduce(sm[v % 2][:, x, keys], bank[:, SEQ * x:SEQ * x + nk], mask[:, keys], HD ** -0.5,
                                                  NEG, ALU.add, ALU.max, mx[t][:, col:col + 1]))
                joined()
                if v == 0:
                    ve.wait_ge(nsink_ready, 1)
                cols = slice(4 * m + half, 4 * m + half + 3, 2)
                ve.scalar_tensor_tensor(negm[t][:, cols], mx[t][:, cols], -1.0, nsink[:, cols], ALU.mult, ALU.min).then_inc(sm_ready, 1)

            def PT(v, ph):
                t = v // 8
                ve.wait_ge(pT_psum, v + 1)
                if v >= 2:
                    ve.wait_ge(pv_done, v - 1)
                n = 2 * P * (1 + t)
                ve.tensor_copy(prT[v % 2][:, 0:n], turned_bank(v)[:, 0:n]).then_inc(pT_ready, 1)

            def AO(quarter, ph):
                t, half = quarter // 2, quarter % 2
                cols = slice(8 * half, 8 * half + 8)
                ve.tensor_tensor(esink[t][:, cols], negm[t][:, cols], table[:, T_SINK + 8 * half:T_SINK + 8 * half + 8],
                                 ALU.add).then_inc(es_arg[t], 1)
                ve.wait_ge(es_ready[t], half + 1)
                ve.wait_ge(p_ready, 16 * t + 8 * (half + 1))
                chain(ve.tensor_tensor(lsum[t][:, cols], lsum[t][:, cols], esink[t][:, cols], ALU.add))
                joined()
                chain(ve.reciprocal(lrec[t][:, cols], lsum[t][:, cols]))
                joined()
                ve.wait_ge(pv_done, 8 * t + 4 * half + 4)
                ve.tensor_tensor(qkv[t][:, 512 + 512 * half:1024 + 512 * half].rearrange("p (a f) -> p a f", f=HD),
                                 pD[t][:, 512:1024].rearrange("p (a f) -> p a f", f=HD),
                                 lrec[t][:, cols].unsqueeze(2).broadcast_to([P, 8, HD]), ALU.mult).then_inc(ao_ready[t], 1)

            def AT(t, half, ph):
                ve.wait_ge(aoh_ready[t], half + 1)
                ve.tensor_tensor(xTl[t][:, 4 * half:4 * half + 4, :].rearrange("p k r -> p (k r)"), ao_bank(t, half),
                                 xTh[t][:, 4 * half:4 * half + 4, :].rearrange("p k r -> p (k r)").bitcast(F32),
                                 ALU.subtract).then_inc(aoT_ready[t], 1)

            def LAT(t, ph):
                ve.wait_ge(latT_psum[t], 1)
                g = feats[:, GAIN_LAT:GAIN_LAT + 3].unsqueeze(2).broadcast_to([P, 3, P])
                ve.tensor_tensor(latf[:], pD[t][:, 512:896].rearrange("p (k r) -> p k r", k=3), g, ALU.mult).then_inc(latf_ready[t], 1)
                ve.wait_ge(lath_ready[t], 1)
                ve.tensor_tensor(latTl[:], latf[:], latTh[:].bitcast(F32), ALU.subtract).then_inc(latT_ready[t], 1)

            def rotate(x1, x2, co, si, tmp):
                chain(ve.tensor_tensor(tmp[0], x1, co, ALU.mult))
                chain(ve.tensor_tensor(tmp[1], x2, si, ALU.mult))
                chain(ve.tensor_tensor(tmp[2], x1, si, ALU.mult))
                chain(ve.tensor_tensor(tmp[3], x2, co, ALU.mult))
                joined()
                chain(ve.tensor_tensor(x1, tmp[0], tmp[1], ALU.subtract))
                return ve.tensor_tensor(x2, tmp[2], tmp[3], ALU.add)

            def U(t, ph):
                if t == 0:
                    ve.wait_ge(sincos_ready, 2)
                half = PE_DIM // 2
                co, si = (x[:, t, 0:32:2] for x in (cos2, sin2))
                kp = lat[t][:, Q_RANK + KV_RANK:LATENT]
                tmp = [mpT[0][:, i * 128:i * 128 + 128].rearrange("p (a f) -> p a f", a=8) for i in range(4)]
                chain(rotate(kp[:, 0:half], kp[:, half:PE_DIM], co, si, [x[:, 0, :] for x in tmp]))
                joined()
                ve.wait_ge(u_out[t], 4)
                ve.tensor_copy(mk[:, :, NOPE:QK], kp.unsqueeze(1).broadcast_to([P, MLA_HEADS, PE_DIM])).then_inc(mqk_ready[t], 1)
                wide = [x.unsqueeze(1).broadcast_to([P, 8, half]) for x in (co, si)]
                rotate(mq[:, :, NOPE:NOPE + half], mq[:, :, NOPE + half:QK], *wide, tmp).then_inc(mqk_ready[t], 1)

            def MT(t, ph):
                ve.wait_ge(mT_psum[t], 2)
                for half in range(2):
                    ve.tensor_copy(mkT[:, 4 * half:4 * half + 4, P * t:P * (t + 1)],
                                   (pG, pT)[half][1][0:QK, :].rearrange("p (a r) -> p a r", a=4)).then_inc(mkT_ready[t], 1)

            def MS(v, ph):
                t, j = v // 4, v % 4
                ve.wait_ge(ms_psum, v + 1)
                chain(ve.tensor_reduce(mx[t][:, 2 * j:2 * j + 2], pG[v % 2][:].rearrange("p (x k) -> p x k", x=2), AX.X, ALU.max,
                                       negate=True))
                joined()
                ve.tensor_scalar(negm[t][:, 2 * j:2 * j + 2], mx[t][:, 2 * j:2 * j + 2], MLA_SCALE, None, ALU.mult).then_inc(mmax_ready, 1)

            def MPT(v, ph):
                ve.wait_ge(mpT_psum, v + 1)
                if v >= 2:
                    ve.wait_ge(mpv_done, v - 1)
                ve.tensor_copy(mpT[v % 2][:], pT[v % 2][:]).then_inc(mpT_ready, 1)

            def MN(t, ph):
                ve.wait_ge(mp_ready, 8 * (t + 1))
                chain(ve.reciprocal(lrec[t][:, 0:8], lsum[t][:, 0:8]))
                joined()
                ve.wait_ge(mpv_done, 4 * (t + 1))
                ve.tensor_tensor(mo[t][:].rearrange("p (a f) -> p a f", f=HD), pD[t][:, 512:1024].rearrange("p (a f) -> p a f", f=HD),
                                 lrec[t][:, 0:8].unsqueeze(2).broadcast_to([P, 8, HD]), ALU.mult).then_inc(mo_ready[t], 1)

            def RT(t, ph):
                ve.wait_ge(rT_psum[t], 2)
                ve.tensor_copy(rkT[:, :, P * t:P * (t + 1)], pG[1][:].rearrange("p (a r) -> p a r", a=4)).then_inc(rkT_ready[t], 1)

            def RM(hd, ph):
                ve.wait_ge(rs_psum, hd + 1)
                ve.wait_ge(dm_ready, hd + 1)
                if hd >= 2:
                    ve.wait_ge(rpv_done, hd - 1)
                for jt in range(2):
                    ve.scalar_tensor_tensor(sd[hd % 2][:, jt, :], pG[hd % 2][:, SEQ * jt:SEQ * (jt + 1)], HD ** -0.5,
                                            dm[hd][:, P * (1 - jt):P * (3 - jt)], ALU.mult, ALU.mult).then_inc(sd_ready, 1)

            def heads(x):
                return x.rearrange("p t (a f) -> p t a f", f=HD)

            def gn_parts(part):
                return (heads(rqk_both[:, :, 256 * part:256 * part + 256]), heads(rqk_both[:, :, 512 + 256 * part:768 + 256 * part]),
                        heads(mpT[0][:].rearrange("p (t n) -> p t n", t=2)))

            def over_heads(part, i):
                return gn[part][:, i, :].rearrange("p (t a) -> p t a", t=2).unsqueeze(3).broadcast_to([P, 2, 4, HD])

            def GNmean(part, ph):
                ro, _, _ = gn_parts(part)
                ve.wait_ge(rpv_done, 4 * part + 4)
                chain(ve.tensor_reduce(gn[part][:, 0, :], pT[part][:].rearrange("p (g f) -> p g f", f=HD), AX.X, ALU.add))
                joined()
                chain(ve.tensor_scalar(gn[part][:, 0, :], gn[part][:, 0, :], 1.0 / HD, None, ALU.mult))
                joined()
                if part == 0:
                    for t in range(2):
                        ve.wait_ge(rT_psum[t], 2)
                chain(ve.tensor_tensor(ro, heads(pT[part][:].rearrange("p (t n) -> p t n", t=2)), over_heads(part, 0), ALU.subtract))

            def GNvar(part, ph):
                ro, _, sq = gn_parts(part)
                joined()
                if part == 1:
                    ve.wait_ge(gn_var, 1)
                chain(ve.tensor_tensor(sq, ro, ro, ALU.mult))
                joined()
                ve.tensor_reduce(gn[part][:, 1, :], mpT[0][:].rearrange("p (g f) -> p g f", f=HD), AX.X, ALU.add).then_inc(gn_var, 1)

            def GNout(part, ph):
                ro, gated, _ = gn_parts(part)
                ve.wait_ge(silu_ready, 1)
                chain(ve.tensor_tensor(gated, gated, ro, ALU.mult))
                joined()
                ve.wait_ge(gn_r, part + 1)
                ve.tensor_tensor(ro, gated, over_heads(part, 3), ALU.mult).then_inc(ro_ready, 1)

            def MAT(t, ph):
                ve.wait_ge(cath_ready[t], 1)
                ve.tensor_tensor(xTl[t][:, 0:4, :].rearrange("p k r -> p (k r)"), pD[t][:, 512:1024],
                                 xTh[t][:, 0:4, :].rearrange("p k r -> p (k r)").bitcast(F32), ALU.subtract).then_inc(catT_ready[t], 1)

            def RAT(t, ph):
                ve.wait_ge(cath_ready[t], 2)
                ve.tensor_tensor(xTl[t][:, 4:8, :].rearrange("p k r -> p (k r)"), pG[t][:],
                                 xTh[t][:, 4:8, :].rearrange("p k r -> p (k r)").bitcast(F32), ALU.subtract).then_inc(catT_ready[t], 1)

            steps = dict(start=start, fill=fill, R=refill, turn=turn, parts=parts, second=second, last=last, tail=tail, join=join, G=G, T=T, Y=Y,
                         rope=rope, QKT=QKT, S=S, PT=PT,
                         AO=AO, AT=AT, LAT=LAT, U=U, MT=MT, MS=MS, MPT=MPT, MN=MN, RT=RT, RM=RM, GNmean=GNmean, GNvar=GNvar, GNout=GNout,
                         MAT=MAT, RAT=RAT)
            walk(ve, lambda name, *a, ph=None: steps[name](*a, ph) if name in steps else None)

        @block.tensor
        def _(pe):
            def three_passes(dst, ah, al, where, n, start, stop):
                hi, lo = w_high[:, where:where + n], w_low[:, where:where + n]
                pe.matmul(dst, ah, hi, start=start, stop=False)
                pe.matmul(dst, ah, lo, start=False, stop=False)
                return pe.matmul(dst, al, hi, start=False, stop=stop)

            def turned(dst, src):
                return pe.transpose(dst, src, ident)

            def start(ph):
                pe.wait_ge(ident_loaded, 16)

            def turn(t, p, ph):
                if p == 0:
                    pe.wait_ge(x_loaded[t], 16)
                for kt in range(KT):
                    if p > 0 and kt % 4 == 0:
                        pe.wait_ge(h_ready[t], 2 * (p - 1) + kt // 4 + 1)
                    mm = turned((pG, pT)[kt // 4][t][:, kt % 4 * P:(kt % 4 + 1) * P], h[t][:, kt * P:(kt + 1) * P])
                    if kt % 4 == 3:
                        mm.then_inc(hT_psum[t], 1)

            def G(t, b, shift, ph):
                c0 = ph.g_chunk(b)
                have = 0
                for kt in range(KT):
                    if b == 0 and kt % 4 == 0:
                        pe.wait_ge(xT_ready[t], xT_base(ph.index) + kt // 4 + 1)
                    need = ((kt + 1) * ph.cols - 1) // CHUNK + 1
                    if need > have and t == 0:
                        pe.wait_ge(w_split, c0 + need + shift * RING)
                    mm = three_passes(pG[t][:, 0:ph.cols], xTh[t][:, kt, :], xTl[t][:, kt, :], slot(c0 + kt * ph.cols // CHUNK) + kt * ph.cols % CHUNK, ph.cols,
                                      kt == 0, kt == KT - 1)
                    have = need
                    if t == 1 and (kt + 1) * ph.cols // CHUNK > kt * ph.cols // CHUNK:
                        mm.then_inc(w_freed, 1)
                    if t == 0 and kt == KT - 1:
                        mm.then_inc(g_done0, 1)

            def T(t, b, shift, ph):
                n = ph.first_block + b + 1 + shift * (RING // (ph.cg + ph.kd))
                pe.wait_ge(act_ready[t], n)
                if ph.mixer:
                    turned(pT[t][:, 0:P], gate[t][:, 0:P])
                    turned(pT[t][:, P:2 * P], act[t][:, 0:P]).then_inc(actT_psum[t], 1)
                else:
                    turned(pT[t][:, 0:P], act[t][:, 0:P])
                    turned(pT[t][:, P:2 * P], act[t][:, P:2 * P]).then_inc(actT_psum[t], 1)

            def Dn(t, b, shift, ph):
                n = ph.first_block + b + 1 + shift * (RING // (ph.cg + ph.kd))
                pe.wait_ge(aT_ready[t], n)
                last = b == ph.nb - 1
                order = [(k, half) for k in range(ph.kd) for half in range(2)]
                if last:
                    order.sort(key=lambda x: x[1])
                for i, (k, half) in enumerate(order):
                    c = ph.d_chunk(b) + k
                    if t == 0 and (half == 0 or not last):
                        pe.wait_ge(w_split, c + 1 + shift * RING)
                    mm = three_passes(pD[t][:, 512 * half:512 * half + 512], aTh[t][:, k, :], aTl[t][:, k, :],
                                      slot(c) + 512 * half, 512, b == 0 and k == 0, last and k == ph.kd - 1)
                    if t == 1 and half == 1:
                        mm.then_inc(w_freed, 1)
                    elif last and k == ph.kd - 1:
                        mm.then_inc(d_done0 if half else d_half[t], 1)

            def proj(j, t, c, ph):
                dst = pG[t][:] if j == 2 else pD[t][:, 512 * j:512 * j + 512]
                high, low = (x2h, x2l) if j else (xTh, xTl)
                if c % 2 == 0:
                    pe.wait_ge(xT_ready[t], xT_base(B_INDEX) + (2 if j else 0) + c // 2 + 1)
                if j == 2 and c == 0:
                    pe.wait_ge(xT_ready[t], xT_base(B_INDEX) + 4)
                w = B_FIRST + 4 * j + c
                if t == 0:
                    pe.wait_ge(w_split, w + 1)
                for i in range(2):
                    kt = 2 * c + i
                    mm = three_passes(dst, high[t][:, kt, :], low[t][:, kt, :], slot(w) + 512 * i, 512, kt == 0, kt == KT - 1)
                if t == 1:
                    mm.then_inc(w_freed, 1)
                elif c == 3:
                    mm.then_inc(q_done0, 1)

            def QKT(t, part, ph):
                pe.wait_ge(rope_done, 2 * (2 * t + part + 1))
                if part == 0:
                    for i in range(2):
                        mm = turned(pD[t][:, P * i:P * (i + 1)], qkv[t][:, 256 + P * i:256 + P * (i + 1)])
                    mm.then_inc(qkT_psum[t], 1)
                for i in range(4):
                    first = 512 + 512 * part + P * i
                    mm = turned((pG[t][:] if part else pD[t][:, 512:1024])[:, i * P:(i + 1) * P], qkv[t][:, first:first + P])
                mm.then_inc(qkT_psum[t], 1)

            def S(v, ph):
                t, m, half = v // 8, v % 8 // 2, v % 2
                if v % 8 == 0:
                    pe.wait_ge(kqT_act[t], 1)
                    pe.wait_ge(kqT_dve[t], 1)
                if v == 1 or v % 8 == 4:
                    pe.wait_ge(kqT_act[t], 2)
                if v >= 2:
                    pe.wait_ge(sm_ready, v - 1)
                part = slice(HD * half, HD * half + HD)
                for x in range(2):
                    i = 2 * m + x
                    nk = P * (1 + t)
                    mm = pe.matmul((pT, pG)[half][0][:, SEQ * x:SEQ * x + nk], qT[t][part, i, :], kT[part, i // 4, 0:nk],
                                   start=True, stop=True)
                mm.then_inc(s_done, 1)

            def PT(v, ph):
                t = v // 8
                pe.wait_ge(p_ready, 2 * (v + 1))
                if v >= 2:
                    pe.wait_ge(pT_ready, v - 1)
                n = 0
                for x in range(2):
                    for kt in range(1 - t, 2):
                        mm = turned(turned_bank(v)[:, P * n:P * (n + 1)], pr[v % 2][:, x, P * kt:P * (kt + 1)])
                        n += 1
                mm.then_inc(pT_psum, 1)

            def PV(v, ph):
                t, u, m, half = v // 8, v % 8, v % 8 // 2, v % 2
                pe.wait_ge(pT_ready, v + 1)
                if u == 4:
                    pe.wait_ge(ao_ready[t], 1)
                n = 0
                for x in range(2):
                    i = 2 * m + x
                    kv = 2 * (i // 4) + half
                    dst = pD[t][:, 512 + i % 4 * P + HD * half:512 + i % 4 * P + HD * half + HD]
                    for kt in range(1 + t):
                        mm = pe.matmul(dst, prT[v % 2][:, P * n:P * (n + 1)], qkv[kt][:, HD * kv:HD * kv + HD],
                                       start=kt == 0, stop=kt == t)
                        n += 1
                mm.then_inc(pv_done, 1)

            def AT(t, half, ph):
                pe.wait_ge(ao_ready[t], half + 1)
                if half == 0 and t == 0:
                    pe.wait_ge(pT_ready, 8)
                for k in range(4):
                    first = 512 + 512 * half + P * k
                    mm = turned(ao_bank(t, half)[:, k * P:(k + 1) * P], qkv[t][:, first:first + P])
                mm.then_inc(aoT_psum[t], 1)

            def out_product(t, kt, w):
                for half in range(2):
                    mm = three_passes(pD[t][:, 512 * half:512 * half + 512], xTh[t][:, kt, :], xTl[t][:, kt, :],
                                      slot(w) + 512 * half, 512, kt == 0, kt == KT - 1)
                    if kt == KT - 1 and half == 0:
                        mm.then_inc(d_half[t], 1)
                if t == 1:
                    mm.then_inc(w_freed, 1)
                elif kt == KT - 1:
                    mm.then_inc(d_done0, 1)

            def O(t, kt, ph):
                if kt == 0 and t == 0:
                    pe.wait_ge(aoT_ready[t], 2)
                elif kt % 4 == 0:
                    pe.wait_ge(aoT_ready[t], kt // 4 + 1)
                if t == 0:
                    pe.wait_ge(w_split, B_WO + kt + 1)
                out_product(t, kt, B_WO + kt)

            def X(i, t, c, ph):
                n = LATENT if i == 0 else 512
                if i == 0 and c % 2 == 0:
                    pe.wait_ge(xT_ready[t], xT_base(C_INDEX) + c // 2 + 1)
                if c == 0 and i > 0:
                    pe.wait_ge(x_out[t], i)
                w = C_X[i] + c
                if t == 0:
                    pe.wait_ge(w_split, w + 1)
                for k in range(2):
                    kt = 2 * c + k
                    mm = three_passes(pD[t][:, 0:n], xTh[t][:, kt, :], xTl[t][:, kt, :], slot(w) + 512 * k, n, kt == 0, kt == KT - 1)
                if t == 1:
                    mm.then_inc(w_freed, 1)
                elif c == 3:
                    mm.then_inc(x_done0, 1)

            def LAT_(t, ph):
                pe.wait_ge(x_out[t], 1)
                for k in range(3):
                    mm = turned(pD[t][:, 512 + P * k:512 + P * (k + 1)], lat[t][:, P * k:P * (k + 1)])
                mm.then_inc(latT_psum[t], 1)

            def U(t, ph):
                pe.wait_ge(latT_ready[t], 1)
                if t == 1:
                    pe.wait_ge(mqT_ready[0], 2)
                    pe.wait_ge(mkT_ready[0], 2)
                else:
                    pe.wait_ge(xT_ready[1], xT_base(C_INDEX) + 2)
                for k in range(3):
                    w = C_U + k
                    if t == 0:
                        pe.wait_ge(w_split, w + 1)
                    for half in range(2):
                        if k < 2:
                            mm = three_passes((pG, pT)[half][0][:, 0:384], latTh[:, k, :], latTl[:, k, :], slot(w) + 384 * half, 384,
                                              k == 0, k == 1)
                        else:
                            mm = three_passes((pG, pT)[half][1][:], latTh[:, k, :], latTl[:, k, :], slot(w) + 512 * half, 512, True, True)
                    if t == 1:
                        mm.then_inc(w_freed, 1)
                if t == 0:
                    mm.then_inc(u_done0, 1)

            def MT(t, ph):
                pe.wait_ge(mqk_ready[t], 2)
                for i, src in enumerate((mq, mk)):
                    for hd in range(MLA_HEADS):
                        mm = turned((pG, pT)[hd // 4][i][0:QK, hd % 4 * P:(hd % 4 + 1) * P], src[:, hd, :])
                    mm.then_inc(mT_psum[t], 1)

            def MS(v, ph):
                t, j = v // 4, v % 4
                if v == 0:
                    for r in range(2):
                        pe.wait_ge(mqT_ready[r], 2)
                        pe.wait_ge(mkT_ready[r], 2)
                if v >= 2:
                    pe.wait_ge(mp_ready, 2 * (v - 1))
                for x in range(2):
                    hd = 2 * j + x
                    mm = pe.matmul(pG[v % 2][:, SEQ * x:SEQ * (x + 1)], mqT[:, hd, P * t:P * (t + 1)], mkT[:, hd, :],
                                   start=True, stop=True)
                mm.then_inc(ms_psum, 1)

            def MPT(v, ph):
                pe.wait_ge(mp_ready, 2 * (v + 1))
                if v >= 2:
                    pe.wait_ge(mpT_ready, v - 1)
                for x in range(2):
                    for kt in range(2):
                        mm = turned(pT[v % 2][:, (2 * x + kt) * P:(2 * x + kt + 1) * P], mp[v % 2][:, x, P * kt:P * (kt + 1)])
                mm.then_inc(mpT_psum, 1)

            def MPV(v, ph):
                t, j = v // 4, v % 4
                pe.wait_ge(mpT_ready, v + 1)
                for x in range(2):
                    hd = 2 * j + x
                    for kt in range(2):
                        mm = pe.matmul(pD[t][:, 512 + HD * hd:512 + HD * (hd + 1)], mpT[v % 2][:, (2 * x + kt) * P:(2 * x + kt + 1) * P],
                                       mv[kt][:, HD * hd:HD * (hd + 1)], start=kt == 0, stop=kt == 1)
                mm.then_inc(mpv_done, 1)

            def RT(t, ph):
                pe.wait_ge(rrope_done[t], 2)
                if t == 0:
                    pe.wait_ge(mp_ready, 16)
                else:
                    pe.wait_ge(rqT_ready[0], 1)
                    pe.wait_ge(rkT_ready[0], 1)
                for i in range(2):
                    for k in range(4):
                        mm = turned(pG[i][:, P * k:P * (k + 1)], rqk[t][:, 512 * i + P * k:512 * i + P * (k + 1)])
                    mm.then_inc(rT_psum[t], 1)

            def RS(hd, ph):
                if hd == 0:
                    pe.wait_ge(rqT_ready[1], 1)
                    pe.wait_ge(rkT_ready[1], 1)
                if hd >= 2:
                    pe.wait_ge(sd_ready, 2 * (hd - 1))
                part = slice(HD * (hd % 2), HD * (hd % 2) + HD)
                for jt in range(2):
                    mm = pe.matmul(pG[hd % 2][:, SEQ * jt:SEQ * (jt + 1)], rkT[part, hd // 2, P * jt:P * (jt + 1)],
                                   rqT[part, hd // 2, :], start=True, stop=True)
                mm.then_inc(rs_psum, 1)

            def RPV(hd, ph):
                pe.wait_ge(sd_ready, 2 * (hd + 1))
                if hd == 0:
                    pe.wait_ge(mpT_ready, 8)
                    pe.wait_ge(x_out[0], 4)
                    pe.wait_ge(x_out[1], 4)
                for t in range(2):
                    dst = pT[hd // 4][:, 256 * t + HD * (hd % 4):256 * t + HD * (hd % 4 + 1)]
                    for jt in range(2):
                        mm = pe.matmul(dst, sd[hd % 2][:, jt, P * t:P * (t + 1)],
                                       rv[jt][:, HD * hd:HD * (hd + 1)], start=jt == 0, stop=jt == 1)
                mm.then_inc(rpv_done, 1)

            def MAT(t, ph):
                pe.wait_ge(mo_ready[t], 1)
                for k in range(4):
                    mm = turned(pD[t][:, 512 + P * k:512 + P * (k + 1)], mo[t][:, P * k:P * (k + 1)])
                mm.then_inc(catT_psum[t], 1)

            def RAT(t, ph):
                pe.wait_ge(ro_ready, 2)
                for k in range(4):
                    mm = turned(pG[t][:, P * k:P * (k + 1)], rqk[t][:, P * k:P * (k + 1)])
                mm.then_inc(catT_psum[t], 1)

            def Oc(t, kt, ph):
                if kt == 0:
                    pe.wait_ge(rgate[t], 1)
                if kt % 4 == 0:
                    pe.wait_ge(catT_ready[t], kt // 4 + 1)
                if t == 0:
                    pe.wait_ge(w_split, C_WO + kt + 1)
                out_product(t, kt, C_WO + kt)

            steps = dict(start=start, turn=turn, G=G, D=Dn, T=T, proj=proj, QKT=QKT, S=S, PT=PT, PV=PV, AT=AT, O=O, X=X, LAT=LAT_,
                         U=U, MT=MT, MS=MS, MPT=MPT, MPV=MPV, RT=RT, RS=RS, RPV=RPV, MAT=MAT, RAT=RAT, Oc=Oc)
            walk(pe, lambda name, *a, ph=None: steps[name](*a, ph) if name in steps else None)


class NoLoop:

    def Fori(self, first, last):
        return ExitStack()



def weight_chunks(w):
    parts = []

    def sliced(cols, pad=0):
        if pad:
            cols = np.concatenate([cols, np.zeros((cols.shape[0], pad), cols.dtype)], axis=1)
        wide = cols.reshape(KT, P, -1).transpose(1, 0, 2).reshape(P, -1)
        return list(wide.reshape(P, -1, CHUNK).transpose(1, 0, 2))

    def blocks(ph, inputs, output):
        found = {}
        wide = ph.cols // len(inputs)
        for b in range(ph.nb):
            cols = np.concatenate([m[:, wide * b:wide * (b + 1)] for m in inputs], axis=1)
            for i, c in enumerate(sliced(cols)):
                found[ph.g_chunk(b) + i] = c
            for k in range(ph.kd):
                row = P * (ph.kd * b + k)
                found[ph.d_chunk(b) + k] = output[row:row + P]
        parts.extend(found[c] for c in sorted(found))

    a_in = w["a_w_in"][0]
    blocks(MIX, [a_in[:, D * i:D * (i + 1)] for i in range(3)], w["a_w_out"][0])

    def ffn(ph, layer):
        both = w["ffn_w_gate_up"][layer]
        f = both.shape[1] // 2
        blocks(ph, [both[:, :f], both[:, f:]], w["ffn_w_down"][layer])

    ffn(FFN1, 0)
    kv = w["w_kv"]
    parts.extend(sliced(np.concatenate([kv[:, 256:], kv[:, :256]], axis=1)))
    order = [head_at(i, p) for i in range(PAIRS) for p in range(2)]
    q = w["b_w_q"][0].reshape(D, HEADS, HD)[:, order, :].reshape(D, D)
    for j in range(2):
        parts.extend(sliced(q[:, 512 * j:512 * j + 512]))
    parts.extend(w["b_w_o"][0].reshape(HEADS, HD, D)[order].reshape(KT, P, D))
    ffn(FFN2, 1)
    blocks(FFN3, [w["ffn1_w_gate_2"][0], w["ffn1_w_up_2"][0]], w["ffn1_w_down_2"][0])
    w_in = w["w_in_2"][0]
    parts.extend(sliced(w_in[:, 0:LATENT], 512 - LATENT))
    uq, ukv = w["w_uq_2"][0], w["w_ukv_2"][0].reshape(KV_RANK, MLA_HEADS, 2, HD)
    pad = np.zeros((P, CHUNK - uq.shape[1]), uq.dtype)
    for i in range(4):
        if i == 2:
            parts.extend(np.concatenate([uq[P * k:P * (k + 1)], pad], axis=1) for k in range(2))
            parts.append(ukv.transpose(0, 2, 1, 3).reshape(P, CHUNK))
        parts.extend(sliced(w_in[:, LATENT + 512 * i:LATENT + 512 * (i + 1)]))
    parts.extend(w["w_o_2"][0].reshape(KT, P, D))
    blocks(FFN4, [w["ffn2_w_gate_2"][0], w["ffn2_w_up_2"][0]], w["ffn2_w_down_2"][0])
    return np.ascontiguousarray(np.stack(parts))


def shape_constants():
    f32 = np.float32
    c = np.zeros((P, CONSTS), f32)
    c[:, C_ID:C_ID + P] = np.eye(P)
    inv = (f32(500000.0) ** (-np.arange(0, 16, 2, dtype=f32) / f32(16))).astype(f32)
    angle = (np.arange(SEQ, dtype=f32)[:, None] * inv[None, :]).astype(f32)
    tab = np.stack([np.cos(angle), np.sin(angle)], axis=1).astype(f32)
    c[:, C_ROPE:C_ROPE + 32] = tab.reshape(2, P, 16).transpose(1, 0, 2).reshape(P, 32)
    i, j = np.arange(P)[:, None], np.arange(P)[None, :]
    c[:, C_MASK:C_MASK + P] = np.where(j > i, 0.0, NEG)
    c[:, C_MASK + P:C_MASK + 2 * P] = np.where(j <= i, 0.0, NEG)
    c[:, C_INV:C_INV + 32] = (f32(10000.0) ** (-np.arange(32, dtype=f32) / f32(32)))[None, :]
    dist = j - i
    c[:, C_REL:C_REL + 4 * P] = np.concatenate(
        [np.maximum(dist, 0), dist + P, np.maximum(-dist, 0), P - dist], axis=1)
    return c


def kernel(**inputs):
    import concourse.bacc as bacc
    from concourse.bass_utils import run_bass_kernel_spmd

    w = {k: np.asarray(v) for k, v in inputs.items()}

    def by_feature(g):
        return np.asarray(g).reshape(-1, P).T

    feats = np.ascontiguousarray(np.concatenate(
        [by_feature(g) for g in (w["a_pre_norm"][0], w["ffn_pre_norm"][0], w["kv_norm"], w["b_pre_norm"][0], w["ffn_pre_norm"][1],
                                 w["ffn1_norm_2"][0], w["mix_norm_2"][0], w["ffn2_norm_2"][0], w["q_norm_2"][0], w["kv_norm_2"][0])]
        + [w["a_conv_w"][0].reshape(3, KT, P).transpose(2, 1, 0).reshape(P, 24)], axis=1))
    order = [head_at(i, p) for i in range(PAIRS) for p in range(2)]
    row = np.concatenate([w["b_sinks"][0][order], w["ret_decay_fwd_2"][0], w["ret_decay_bwd_2"][0]])
    arrays = {
        "x": np.ascontiguousarray(w["x"][0]),
        "stream": weight_chunks(w),
        "feats": feats,
        "consts": shape_constants(),
        "table": np.ascontiguousarray(np.broadcast_to(row, (P, TAB))),
        "positions": np.ascontiguousarray(w["positions_2"].reshape(2, P).T),
        "posts": np.ascontiguousarray(np.stack([w["a_post_norm"][0], w["ffn_post_norm"][0], w["b_post_norm"][0],
                                                w["ffn_post_norm"][1], w["final_norm_2"]])),
    }
    nc = bacc.Bacc("TRN2", target_bir_lowering=False, num_devices=1)
    args = [nc.dram_tensor(f"in_{k}", a.shape, mybir.dt.from_np(a.dtype), kind="ExternalInput").ap() for k, a in arrays.items()]
    out = nc.dram_tensor("out", (SEQ, D), F32, kind="ExternalOutput").ap()
    build(nc, *args, out)
    result = run_bass_kernel_spmd(nc, [{f"in_{k}": a for k, a in arrays.items()}], core_ids=[0])
    return result.results[0]["out"].reshape(1, SEQ, D)
```
